# Optimizing a Trainium2 kernel written in Bass

```python
import math
import jax, jax.numpy as jnp
from jax import lax
import numpy as np

D_MODEL = 1024
BATCH = 1
SEQ = 256
DEPTH = 2

HEAD_DIM = 64
ROT_DIM = HEAD_DIM // 4
ROPE_THETA = 500000.0
EPS = 1e-6
NEG = -1e30
FORCE_SCORE = 1e9
Q_BLOCK = 128

DSA_HEADS = 8
DSA_WIDTH = DSA_HEADS * HEAD_DIM
DSA_KV_RANK = 128
IDX_HEADS = 4
IDX_DIM = 64
DSA_TOPK_MAX = 256

POOL_GROUPS = 4
POOL_WINDOWS = (2, 4, 8, 16)
POOL_WIDTH = 512
POOL_GDIM = POOL_WIDTH // POOL_GROUPS

NSA_HEADS = 8
NSA_KV_HEADS = 2
NSA_REP = NSA_HEADS // NSA_KV_HEADS
NSA_WIDTH = NSA_HEADS * HEAD_DIM
NSA_KV_COLS = 2 * NSA_KV_HEADS * HEAD_DIM
CMP_LEN = 32
CMP_STRIDE = 16
CMP_HIDDEN = 128
SEL_BLOCK = 64
SEL_N = 8
WINDOW = 256

D_FF = 2816

IN_SPLITS = (
    DSA_WIDTH,
    DSA_KV_RANK,
    IDX_HEADS * IDX_DIM,
    IDX_DIM,
    IDX_HEADS,
    POOL_WIDTH,
    NSA_WIDTH,
    NSA_KV_COLS,
    NSA_KV_COLS,
    NSA_KV_COLS,
    NSA_HEADS * 3,
    3 * D_MODEL,
)
N_IN = sum(IN_SPLITS)

kernel_name = "hybrid_dsa_pool_nsa_macaron"

def rms_norm(x, g):
    x32 = x.astype(jnp.float32)
    y = x32 * lax.rsqrt(jnp.mean(x32 * x32, axis=-1, keepdims=True) + EPS)
    return (y * g.astype(jnp.float32)).astype(x.dtype)

def swiglu(x, w_gate, w_up, w_down):
    return (jax.nn.silu(x @ w_gate) * (x @ w_up)) @ w_down

def rope_tables(positions):
    inv_freq = ROPE_THETA ** (-jnp.arange(0, ROT_DIM, 2, dtype=jnp.float32) / ROT_DIM)
    ang = positions.astype(jnp.float32)[..., None] * inv_freq
    return jnp.cos(ang), jnp.sin(ang)

def partial_rope(x, cos, sin):
    half = ROT_DIM // 2
    shape = cos.shape[:2] + (1,) * (x.ndim - 3) + (half,)
    c = cos.reshape(shape)
    s = sin.reshape(shape)
    x1 = x[..., :half].astype(jnp.float32)
    x2 = x[..., half:ROT_DIM].astype(jnp.float32)
    r1 = (x1 * c - x2 * s).astype(x.dtype)
    r2 = (x2 * c + x1 * s).astype(x.dtype)
    return jnp.concatenate([r1, r2, x[..., ROT_DIM:]], axis=-1)

def masked_softmax(s, mask):
    return jax.nn.softmax(jnp.where(mask, s.astype(jnp.float32), NEG), axis=-1)

def dsa_mixer(q, c_kv, iq, ik, iw, kv_norm, w_ukv, cos, sin):
    B, S = q.shape[:2]
    q = partial_rope(q.reshape(B, S, DSA_HEADS, HEAD_DIM), cos, sin) * (HEAD_DIM ** -0.5)
    kv = rms_norm(c_kv, kv_norm) @ w_ukv
    k = partial_rope(kv[..., :HEAD_DIM], cos, sin)
    v = kv[..., HEAD_DIM:]
    iq = partial_rope(iq.reshape(B, S, IDX_HEADS, IDX_DIM), cos, sin) * (IDX_DIM ** -0.5)
    ik = partial_rope(ik, cos, sin)
    iw = (iw * (IDX_HEADS ** -0.5)).astype(jnp.float32)
    top_k = min(DSA_TOPK_MAX, S // 4)
    key_pos = jnp.arange(S)
    gather = jax.vmap(lambda table, idx: table[idx])

    def block(q0):
        t = q0 + jnp.arange(Q_BLOCK)
        qb = lax.dynamic_slice_in_dim(q, q0, Q_BLOCK, axis=1)
        iqb = lax.dynamic_slice_in_dim(iq, q0, Q_BLOCK, axis=1)
        iwb = lax.dynamic_slice_in_dim(iw, q0, Q_BLOCK, axis=1)
        logits = jnp.einsum('bqhd,bsd->bqhs', iqb, ik).astype(jnp.float32)
        score = jnp.einsum('bqhs,bqh->bqs', jax.nn.relu(logits), iwb)
        score = jnp.where(key_pos[None, None, :] <= t[None, :, None], score, NEG)
        _, sel = lax.top_k(score, top_k)
        kg = gather(k, sel)
        vg = gather(v, sel)
        s = jnp.einsum('bqhd,bqkd->bhqk', qb, kg)
        p = masked_softmax(s, (sel <= t[None, :, None])[:, None])
        return jnp.einsum('bhqk,bqkd->bqhd', p.astype(vg.dtype), vg)

    out = lax.map(block, jnp.arange(S // Q_BLOCK) * Q_BLOCK)
    return out.transpose(1, 0, 2, 3, 4).reshape(B, S, DSA_WIDTH)

def pool_mixer(u, pool_w, pool_scale):
    B, S, _ = u.shape
    u32 = u.reshape(B, S, POOL_GROUPS, POOL_GDIM).astype(jnp.float32)
    csum = jnp.pad(jnp.cumsum(u32, axis=1), ((0, 0), (1, 0), (0, 0), (0, 0)))
    t = jnp.arange(S)
    pooled = []
    for g, w in enumerate(POOL_WINDOWS):
        lo = jnp.maximum(t + 1 - w, 0)
        cnt = (t + 1 - lo).astype(jnp.float32)
        win_sum = csum[:, 1:, g] - csum[:, lo, g]
        pooled.append(win_sum / cnt[None, :, None] - u32[:, :, g])
    pooled = jnp.stack(pooled, axis=2).astype(u.dtype)
    y = jnp.einsum('bsgc,gcd->bsgd', pooled, pool_w)
    return y.reshape(B, S, POOL_WIDTH) * pool_scale

def nsa_mixer(q, kv_cmp, kv_sel, kv_win, gates, cmp_pos, cmp_w1, cmp_w2, cos, sin):
    B, S = q.shape[:2]
    G, R = NSA_KV_HEADS, NSA_REP
    q = partial_rope(q.reshape(B, S, G, R, HEAD_DIM), cos, sin) * (HEAD_DIM ** -0.5)

    def split_kv(kv):
        kv = kv.reshape(B, S, 2, G, HEAD_DIM)
        return partial_rope(kv[:, :, 0], cos, sin), kv[:, :, 1]

    kc_tok, vc_tok = split_kv(kv_cmp)
    ks, vs = split_kv(kv_sel)
    kw, vw = split_kv(kv_win)

    n_cmp = (S - CMP_LEN) // CMP_STRIDE + 1
    cmp_start = jnp.arange(n_cmp) * CMP_STRIDE
    cmp_end = cmp_start + CMP_LEN - 1
    tok_idx = cmp_start[:, None] + jnp.arange(CMP_LEN)[None, :]

    def compress(x, pos, w1, w2):
        blocks = x[:, tok_idx] + pos[None, None, :, None, :]
        flat = blocks.transpose(0, 1, 3, 2, 4).reshape(B, n_cmp, G, CMP_LEN * HEAD_DIM)
        return jax.nn.gelu(flat @ w1) @ w2

    kc = compress(kc_tok, cmp_pos[0], cmp_w1[0], cmp_w2[0])
    vc = compress(vc_tok, cmp_pos[1], cmp_w1[1], cmp_w2[1])

    n_blk = S // SEL_BLOCK
    blk = jnp.arange(n_blk)
    sel_start = blk * SEL_BLOCK
    overlap = jnp.clip(jnp.minimum(cmp_end[:, None], sel_start[None, :] + SEL_BLOCK - 1)
                       - jnp.maximum(cmp_start[:, None], sel_start[None, :]) + 1, 0)
    cmp_to_sel = overlap.astype(jnp.float32) / CMP_LEN
    n_sel = min(SEL_N, n_blk)

    ks_g = ks.transpose(0, 2, 1, 3)
    vs_g = vs.transpose(0, 2, 1, 3)
    kw_pad = jnp.pad(kw, ((0, 0), (WINDOW, 0), (0, 0), (0, 0)))
    vw_pad = jnp.pad(vw, ((0, 0), (WINDOW, 0), (0, 0), (0, 0)))
    gate = jax.nn.sigmoid(gates.reshape(B, S, G, R, 3).astype(jnp.float32)).astype(q.dtype)
    gather = jax.vmap(jax.vmap(lambda table, idx: table[idx]))
    blk_off = jnp.arange(SEL_BLOCK)
    win_off = jnp.arange(WINDOW + Q_BLOCK) - WINDOW

    def block(q0):
        t = q0 + jnp.arange(Q_BLOCK)
        qb = lax.dynamic_slice_in_dim(q, q0, Q_BLOCK, axis=1)
        gb = lax.dynamic_slice_in_dim(gate, q0, Q_BLOCK, axis=1)
        s_c = jnp.einsum('bqgrd,bngd->bgrqn', qb, kc)
        m_c = cmp_end[None, :] <= t[:, None]
        p_c = masked_softmax(s_c, m_c) * jnp.any(m_c, axis=-1)[:, None]
        o_c = jnp.einsum('bgrqn,bngd->bqgrd', p_c.astype(vc.dtype), vc)
        imp = jnp.einsum('bgrqn,nj->bgqj', p_c, cmp_to_sel)
        forced = (blk[None, :] == 0) | (blk[None, :] == (t // SEL_BLOCK)[:, None])
        admissible = sel_start[None, :] <= t[:, None]
        imp = jnp.where(forced, FORCE_SCORE, jnp.where(admissible, imp, NEG))
        _, sel = lax.top_k(imp, n_sel)
        tok = (sel[..., None] * SEL_BLOCK + blk_off).reshape(B, G, Q_BLOCK, n_sel * SEL_BLOCK)
        k_s = gather(ks_g, tok)
        v_s = gather(vs_g, tok)
        s_s = jnp.einsum('bqgrd,bgqtd->bgrqt', qb, k_s)
        p_s = masked_softmax(s_s, (tok <= t[None, None, :, None])[:, :, None])
        o_s = jnp.einsum('bgrqt,bgqtd->bqgrd', p_s.astype(v_s.dtype), v_s)
        k_w = lax.dynamic_slice_in_dim(kw_pad, q0, WINDOW + Q_BLOCK, axis=1)
        v_w = lax.dynamic_slice_in_dim(vw_pad, q0, WINDOW + Q_BLOCK, axis=1)
        kpos = q0 + win_off
        diff = t[:, None] - kpos[None, :]
        m_w = (kpos[None, :] >= 0) & (diff >= 0) & (diff < WINDOW)
        s_w = jnp.einsum('bqgrd,bkgd->bgrqk', qb, k_w)
        p_w = masked_softmax(s_w, m_w)
        o_w = jnp.einsum('bgrqk,bkgd->bqgrd', p_w.astype(v_w.dtype), v_w)
        o = gb[..., 0:1] * o_c + gb[..., 1:2] * o_s + gb[..., 2:3] * o_w
        return o.reshape(B, Q_BLOCK, NSA_WIDTH)

    out = lax.map(block, jnp.arange(S // Q_BLOCK) * Q_BLOCK)
    return out.transpose(1, 0, 2, 3).reshape(B, S, NSA_WIDTH)

def setup_inputs(seed: int = 0) -> dict:
    key = jax.random.key(seed)
    ks = jax.random.split(key, 32)

    def nrm(k, shape, scale):
        return jax.random.normal(k, shape, jnp.float32) * scale

    def gain(k, shape):
        return 1.0 + 0.05 * jax.random.normal(k, shape, jnp.float32)

    L, D, F = DEPTH, D_MODEL, D_FF
    start = jax.random.randint(ks[1], (BATCH, 1), 0, 1024)
    positions = (start + jnp.arange(SEQ, dtype=jnp.int32)[None, :]).astype(jnp.int32)
    return {
        "x": nrm(ks[0], (BATCH, SEQ, D), 1.0),
        "positions": positions,
        "ffn1_norm": gain(ks[2], (L, D)),
        "ffn1_gate": nrm(ks[3], (L, D, F), D ** -0.5),
        "ffn1_up": nrm(ks[4], (L, D, F), D ** -0.5),
        "ffn1_down": nrm(ks[5], (L, F, D), F ** -0.5),
        "mix_norm": gain(ks[6], (L, D)),
        "w_in": nrm(ks[7], (L, D, N_IN), D ** -0.5),
        "dsa_kv_norm": gain(ks[8], (L, DSA_KV_RANK)),
        "dsa_w_ukv": nrm(ks[9], (L, DSA_KV_RANK, 2 * HEAD_DIM), DSA_KV_RANK ** -0.5),
        "pool_w": nrm(ks[10], (L, POOL_GROUPS, POOL_GDIM, POOL_GDIM), POOL_GDIM ** -0.5),
        "pool_scale": gain(ks[11], (L, POOL_WIDTH)),
        "nsa_cmp_pos": nrm(ks[12], (L, 2, CMP_LEN, HEAD_DIM), 0.02),
        "nsa_cmp_w1": nrm(ks[13], (L, 2, CMP_LEN * HEAD_DIM, CMP_HIDDEN), (CMP_LEN * HEAD_DIM) ** -0.5),
        "nsa_cmp_w2": nrm(ks[14], (L, 2, CMP_HIDDEN, HEAD_DIM), CMP_HIDDEN ** -0.5),
        "proj_a": nrm(ks[15], (L, DSA_WIDTH, D), DSA_WIDTH ** -0.5),
        "proj_b": nrm(ks[16], (L, POOL_WIDTH, D), POOL_WIDTH ** -0.5),
        "proj_c": nrm(ks[17], (L, NSA_WIDTH, D), NSA_WIDTH ** -0.5),
        "w_out": nrm(ks[18], (L, D, D), D ** -0.5),
        "ffn2_norm": gain(ks[19], (L, D)),
        "ffn2_gate": nrm(ks[20], (L, D, F), D ** -0.5),
        "ffn2_up": nrm(ks[21], (L, D, F), D ** -0.5),
        "ffn2_down": nrm(ks[22], (L, F, D), F ** -0.5),
        "final_norm": gain(ks[23], (D,)),
    }

def reference(x, positions, ffn1_norm, ffn1_gate, ffn1_up, ffn1_down, mix_norm, w_in,
              dsa_kv_norm, dsa_w_ukv, pool_w, pool_scale, nsa_cmp_pos, nsa_cmp_w1, nsa_cmp_w2,
              proj_a, proj_b, proj_c, w_out, ffn2_norm, ffn2_gate, ffn2_up, ffn2_down, final_norm):
    cos, sin = rope_tables(positions)
    offsets = [int(o) for o in np.cumsum(IN_SPLITS)[:-1]]
    for l in range(DEPTH):
        x = x + 0.5 * swiglu(rms_norm(x, ffn1_norm[l]), ffn1_gate[l], ffn1_up[l], ffn1_down[l])
        h = rms_norm(x, mix_norm[l])
        (a_q, a_ckv, a_iq, a_ik, a_iw, b_u, c_q, c_kv_cmp, c_kv_sel, c_kv_win, c_gate,
         merge_gate) = jnp.split(h @ w_in[l], offsets, axis=-1)
        y_a = dsa_mixer(a_q, a_ckv, a_iq, a_ik, a_iw, dsa_kv_norm[l], dsa_w_ukv[l], cos, sin)
        y_b = pool_mixer(b_u, pool_w[l], pool_scale[l])
        y_c = nsa_mixer(c_q, c_kv_cmp, c_kv_sel, c_kv_win, c_gate,
                        nsa_cmp_pos[l], nsa_cmp_w1[l], nsa_cmp_w2[l], cos, sin)
        g_a, g_b, g_c = jnp.split(jax.nn.sigmoid(merge_gate), 3, axis=-1)
        merged = g_a * (y_a @ proj_a[l]) + g_b * (y_b @ proj_b[l]) + g_c * (y_c @ proj_c[l])
        x = x + merged @ w_out[l]
        x = x + 0.5 * swiglu(rms_norm(x, ffn2_norm[l]), ffn2_gate[l], ffn2_up[l], ffn2_down[l])
    return rms_norm(x, final_norm)


_drawn_inputs = setup_inputs


def setup_inputs(seed=0):
    import zlib

    import numpy as np

    out = dict(_drawn_inputs(seed))
    spreads = {}
    factors = {'dsa_kv_norm': 4.217, 'nsa_cmp_pos': 8.0}
    for name, (base, spread) in spreads.items():
        noise = np.random.default_rng([zlib.crc32(name.encode()), seed]).standard_normal(out[name].shape)
        drawn = base * np.exp(spread * noise) if base else spread * noise
        out[name] = __import__('jax').numpy.asarray(drawn.astype(out[name].dtype))
    for name, factor in factors.items():
        out[name] = (out[name] * factor).astype(out[name].dtype)
    return out
```

```python
from contextlib import ExitStack

import numpy as np

import concourse.bass as bass
from concourse import mybir

F32 = mybir.dt.float32
F32R = mybir.dt.float32r
I32 = mybir.dt.int32
ALU = mybir.AluOpType
ACT = mybir.ActivationFunctionType
AX = mybir.AxisListType

P = 128
L, S, D, F = 2, 256, 1024, 2816
TOKS = S // P
KT = D // P
HD, HALF_ROT = 64, 8
EPS = 1e-6
NEG = -1e30
TAKEN = -3e38
THETA = 500000.0
TOPK = min(256, S // 4)
N_CMP = (S - 32) // 16 + 1
WINDOWS = (2, 4, 8, 16)

UNIT = 2048
RING = 3
CREDIT = RING
FCH = 256
FI = F // FCH
FFN_UNITS = 3 * FI
MIX_UNITS = 33
LAYER_UNITS = 2 * FFN_UNITS + MIX_UNITS
assert FFN_UNITS % RING == 0 and MIX_UNITS % RING == 0
PAD_UNITS = RING

C_CKV, C_IK, C_IW, C_GATE = 0, 128, 192, 196
C_S = 220
C_IQ, C_KVC, C_KVS, C_KVW, C_QN, C_QD, C_U = 220, 476, 732, 988, 1244, 1756, 2268
ZC = 2780
Z_CHUNKS = 6
CHUNKS = 12

W_G1, W_GM, W_G2, W_KVG, W_PSC, W_POS = 0, 8, 16, 24, 25, 29
W_UKV, W_POOL, W_W2 = 61, 189, 701
W_SMALL = 829
W1C = 2 * 16 * P

K_ID, K_CB, K_CMPB, K_VALID, K_BAND, K_FREQ = 0, 128, 384, 416, 418, 418 + 4 * 384
KC = K_FREQ + HALF_ROT

BATCHES = (
    [("sel", qt, g) for qt in range(2) for g in range(2)]
    + [("win", qt, g) for qt in range(2) for g in range(2)]
    + [("cmp", qt, 0) for qt in range(2)]
    + [("dsa", qt, g) for qt in range(2) for g in range(2)]
)
NB = len(BATCHES)
LEAD = 2


def keys_of(b):
    kind, qt, _ = BATCHES[b]
    return N_CMP if kind == "cmp" else P * (qt + 1)


def heads_of(b):
    return 8 if BATCHES[b][0] == "cmp" else 4


def turns_of(b):
    kind, qt, _ = BATCHES[b]
    if kind == "cmp":
        return [[(h, 0) for h in range(4)], [(h, 0) for h in range(4, 8)]]
    blocks = [(h, kb) for h in range(4) for kb in range(qt + 1)]
    return [blocks[i : i + 4] for i in range(0, len(blocks), 4)]


def turn_names(b):
    return [f"p{b}_{j}" for j in range(len(turns_of(b)))]


def turn_order():
    names = ["ckv", "kv", "ik", "iq", "kd", "kvc", "ksw", "qn0", "qn1", "hid", "qd0", "qd1", "cmpo"]
    names += turn_names(0)
    extra = {0: ["band0"], 1: ["band1"], 2: ["yb0"], 3: ["yb1"]}
    for k in range(12):
        names += turn_names(k + 1) + extra.get(k, [])
    names += ["yc0", "yc1"] + turn_names(13) + ["ya0", "ya1", "mg0", "mg1", "mg2", "mg3"]
    return names


TURNS = turn_order()
TURN_AT = {n: i for i, n in enumerate(TURNS)}
PER_BANK = [len(TURNS[0::2]), len(TURNS[1::2])]


def trunk(nc, x_in, pos_in, stream, small_in, w1_in, const_in, final_in, out):
    ctx = ExitStack()
    with ctx:
        def sb(name, shape, dt=F32):
            return ctx.enter_context(nc.sbuf_tensor(name, shape, dt))

        def sem(name):
            return ctx.enter_context(nc.semaphore(name))

        raw = [sb(f"raw{i}", [P, UNIT]) for i in range(RING)]
        whi = [sb(f"whi{i}", [P, UNIT], F32R) for i in range(RING)]
        wlo = [sb(f"wlo{i}", [P, UNIT], F32R) for i in range(RING)]
        x = sb("x", [P, TOKS, D])
        xhi = sb("xhi", [P, KT, S], F32R)
        xlo = sb("xlo", [P, KT, S], F32R)
        z = sb("z", [P, TOKS, ZC])
        gates = sb("gates", [P, TOKS, 3 * D])
        w1 = gates[:, :, :].rearrange("p t c -> p (t c)")[:, 0:W1C].rearrange("p (y k h) -> p y k h", y=2, k=16)
        ybhi = sb("ybhi", [P, 4, S], F32R)
        yblo = sb("yblo", [P, 4, S], F32R)
        small = sb("small", [P, W_SMALL])
        const = sb("const", [P, KC])
        ident = const[:, K_ID : K_ID + P]
        shared_q = sb("shared_q", [P, 2048])
        qnT = shared_q[:, 0:1024].rearrange("p (a t) -> p a t", a=4)
        qdT = shared_q[:, 1024:2048].rearrange("p (a t) -> p a t", a=4)
        h = shared_q[:, 0:512].rearrange("p (t c) -> p t c", t=TOKS)
        tg = shared_q[:, 512:1024].rearrange("p (t c) -> p t c", t=TOKS)
        hThi, hTlo = ybhi[:, 0:2, :], yblo[:, 0:2, :]
        ikd = sb("ikd", [P, TOKS, 2, HD])
        kd = sb("kd", [P, TOKS, 2, HD])
        iqT = sb("iqT", [P, 2, S])
        oacc = iqT[:, :, :].rearrange("p a t -> p (a t)")
        ikT = sb("ikT", [P, S])
        kdT = sb("kdT", [P, S])
        kswT = sb("kswT", [P, 2, S])
        zkv = sb("zkv", [P, TOKS, P])
        ckvT = sb("ckvT", [P, S])
        kvcT = sb("kvcT", [P, 4, S])
        pooledT = kvcT
        sm = sb("sm", [P, 1024])
        probs = sb("probs", [P, 1024])
        pT = sb("pT", [P, 8, P])
        y = sb("y", [P, TOKS, 2, 512])
        work = sb("work", [P, TOKS, S])
        top8 = sb("top8", [P, TOKS, 8])
        trig = sb("trig", [P, 2, TOKS, 16])
        cos16, sin16 = trig[:, 0], trig[:, 1]
        rot = sb("rot", [P, 2, TOKS, 8, 16])
        stat = sb("stat", [P, 64])
        ss, ms, msh, rs, t0, t1, rs_half, rs_sq = (stat[:, 2 * i : 2 * i + 2] for i in range(8))
        sskv, kms, kmsh, rkv, kt0, kt1 = (stat[:, 16 + 2 * i : 18 + 2 * i] for i in range(6))
        unread = stat[:, 28:29]
        negmax = stat[:, 32:40]
        rowmax = stat[:, 40:48]
        sums = [stat[:, 48 + 8 * i : 56 + 8 * i] for i in range(2)]
        sig = sb("sig", [P, TOKS, 24])
        fac = sb("fac", [P, 8])
        gel = oacc[:, 0:300].rearrange("p (s y n) -> p s y n", s=5, y=2)
        gbias = oacc[:, 300:302]
        kcT = sb("kcT", [P, 16])
        vc = ikd[:, 0, :, :]
        posi = sb("posi", [P, TOKS], I32)
        ang = sm[:, 0 : 5 * 16].rearrange("p (s t f) -> p s t f", s=5, t=TOKS)

        def bank(name):
            return ctx.enter_context(nc.psum_tensor(name, [P, 512], F32))

        G = [bank("G0"), bank("G1")]
        T = [bank("T0"), bank("T1")]
        SC = [bank("SC0"), bank("SC1")]
        O = [bank("O0"), bank("O1")]
        ACC = [[SC[0], SC[1]], [O[0], O[1]]]

        raw_in = [sem(f"raw_in{i}") for i in range(RING)]
        hi_done = sem("hi_done")
        lo_done = sem("lo_done")
        unit_used = sem("unit_used")
        x_in_sem = sem("x_in_sem")
        const_in_sem = sem("const_in_sem")
        pos_in_sem = sem("pos_in_sem")
        small_in_sem = sem("small_in_sem")
        w1_in_sem = sem("w1_in_sem")
        final_in_sem = sem("final_in_sem")
        x_up = sem("x_up")
        xt_filled = sem("xt_filled")
        xhi_done = sem("xhi_done")
        xlo_done = sem("xlo_done")
        squares_done = sem("squares_done")
        rstd_done = sem("rstd_done")
        gu_filled = sem("gu_filled")
        tanh_done = sem("tanh_done")
        h_done = sem("h_done")
        ht_filled = sem("ht_filled")
        ht_hi_done = sem("ht_hi_done")
        ht_lo_done = sem("ht_lo_done")
        acc_done = sem("acc_done")
        g_filled = sem("g_filled")
        gz_drained = sem("gz_drained")
        gp_drained = sem("gp_drained")
        t_filled = sem("t_filled")
        t_drained = [sem("t_drained0"), sem("t_drained1")]
        t_hi_done = sem("t_hi_done")
        s_filled = sem("s_filled")
        s_drained = sem("s_drained")
        index_summed = sem("index_summed")
        o_filled = sem("o_filled")
        o_drained = sem("o_drained")
        negmax_done = sem("negmax_done")
        exp_done = sem("exp_done")
        roped = sem("roped")
        kv_squares = sem("kv_squares")
        gate_tanh = sem("gate_tanh")
        shifted = sem("shifted")
        gelu_inner = sem("gelu_inner")
        gelu_tanh = sem("gelu_tanh")
        gelu_done = sem("gelu_done")
        y_done = sem("y_done")
        merged_done = sem("merged_done")
        trig_arg = sem("trig_arg")
        trig_done = sem("trig_done")
        tables_ready = sem("tables_ready")
        out_ready = sem("out_ready")
        out_sent = sem("out_sent")
        dve_step = sem("dve_step")
        pool_step = sem("pool_step")

        block = ctx.enter_context(nc.Block())

        class Steps:

            def __init__(self, eng, s):
                self.eng, self.s, self.n = eng, s, 0

            def restart(self):
                self.eng.sem_clear(self.s)
                self.n = 0

            def then(self, ins):
                ins.then_inc(self.s, 1)
                self.n += 1
                self.eng.wait_ge(self.s, self.n)

        def filled(l, name):
            return l * len(TURNS) + TURN_AT[name] + 1

        def wait_drained(eng, l, *names, opening=None):
            last = [0, 0]
            for i in map(TURN_AT.get, names):
                last[i % 2] = max(last[i % 2], i // 2 + 1)
            if opening is not None:
                i = TURN_AT[opening]
                last[i % 2] = max(last[i % 2], i // 2)
            for b in range(2):
                if last[b]:
                    eng.wait_ge(t_drained[b], l * PER_BANK[b] + last[b])

        def turn_bank(name):
            return T[TURN_AT[name] % 2]

        def mark_drained(ins, name):
            ins.then_inc(t_drained[TURN_AT[name] % 2], 1)

        def ffn_base(l, occ):
            return l * LAYER_UNITS + occ * (FFN_UNITS + MIX_UNITS)

        def mix_base(l):
            return l * LAYER_UNITS + FFN_UNITS

        def unit_value(l, n):
            return l * LAYER_UNITS + n + 1 + CREDIT

        def wait_g(eng, l, f):
            if f % 2 == 0:
                eng.wait_ge(g_filled, l * 20 + f // 2 + 1)
            else:
                n = f - 1 if f < 24 else 23 + (f - 25) // 2 if f < 36 else 30 + (f - 37)
                eng.wait_ge(unit_used, unit_value(l, FFN_UNITS + n))

        BY_TOK = [(0, 0), (0, 1), (1, 0), (1, 1)]
        BY_HALF = [(0, 0), (1, 0), (0, 1), (1, 1)]

        def lift_of(l, which):
            return l * 3 + which

        LIFT_ORDER = [BY_TOK, BY_TOK, BY_HALF]
        LIFT_GAIN = [W_G1, W_GM, W_G2]
        MERGED_ORDER = BY_HALF

        @block.sync
        def _(sp):
            sp.dma_start(x[:, :, :], x_in.rearrange("(t p) d -> p t d", p=P)).then_inc(x_in_sem, 16)
            sp.dma_start(const[:, :], const_in).then_inc(const_in_sem, 16)
            n_groups = (L * LAYER_UNITS + PAD_UNITS) // RING
            with sp.Fori(0, n_groups) as r:
                for j in range(RING):
                    sp.wait_ge(hi_done, r * RING + (j + 1))
                    sp.wait_ge(lo_done, r * RING + (j + 1))
                    sp.dma_start(
                        raw[j][:, :], stream[bass.ds(r * RING + j, 1), :, :].rearrange("u p n -> p (u n)")
                    ).then_inc(raw_in[j], 16)
            sp.wait_ge(x_up, 4 * (3 * L + 1))
            sp.dma_start(z[:, 0, 0:D], final_in.partition_broadcast(P)).then_inc(final_in_sem, 16)
            out_v = out.rearrange("(t p) d -> p t d", p=P)
            for tok in range(TOKS):
                sp.wait_ge(out_ready, tok + 1)
                sp.dma_start(out_v[:, tok, :], x[:, tok, :]).then_inc(out_sent, 16)
            sp.wait_ge(out_sent, 16 * TOKS)

        @block.gpsimd
        def _(pool):
            pool.dma_start(posi[:, :], pos_in).then_inc(pos_in_sem, 16)
            steps = Steps(pool, pool_step)

            def rope(cols, heads, last):
                v = cols.rearrange("p t (h d) -> p t h d", d=HD)
                c = cos16[:, :, :].unsqueeze(2).to_broadcast([P, TOKS, heads, 16])
                s = sin16[:, :, :].unsqueeze(2).to_broadcast([P, TOKS, heads, 16])
                a, b = rot[:, 0, :, 0:heads, :], rot[:, 1, :, 0:heads, :]
                pool.tensor_tensor(a, v[:, :, :, 0:16], c, ALU.mult)
                pool.tensor_tensor(b[:, :, :, 0:8], v[:, :, :, 8:16], s[:, :, :, 0:8], ALU.mult)
                steps.then(pool.tensor_tensor(b[:, :, :, 8:16], v[:, :, :, 0:8], s[:, :, :, 8:16], ALU.mult))
                o = pool.tensor_tensor(v[:, :, :, 0:16], a, b, ALU.add)
                if last:
                    o.then_inc(roped, 1)
                else:
                    steps.then(o)

            pool.wait_ge(tables_ready, 1)
            with pool.Fori(0, L) as l:
                steps.restart()
                pool.wait_ge(gz_drained, l * 24 + 2)
                rope(z[:, :, C_IK : C_IK + HD], 1, False)
                src = z[:, :, C_IK : C_IK + HD].unsqueeze(2).to_broadcast([P, TOKS, 2, HD])
                pool.tensor_copy(ikd[:, :, :, :], src).then_inc(roped, 1)
                pool.wait_ge(gz_drained, l * 24 + 4)
                rope(z[:, :, C_IQ : C_IQ + 256], 4, True)
                pool.wait_ge(roped, l * 8 + 2)
                rope(z[:, :, C_KVC : C_KVC + 128], 2, True)
                wait_drained(pool, l, "kv")
                pool.wait_ge(roped, l * 8 + 3)
                rope(zkv[:, :, 0:HD], 1, False)
                src = zkv[:, :, 0:HD].unsqueeze(2).to_broadcast([P, TOKS, 2, HD])
                pool.tensor_copy(kd[:, :, :, :], src).then_inc(roped, 1)
                pool.wait_ge(gz_drained, l * 24 + 6)
                rope(z[:, :, C_KVS : C_KVS + 128], 2, True)
                pool.wait_ge(roped, l * 8 + 5)
                rope(z[:, :, C_KVW : C_KVW + 128], 2, True)
                pool.wait_ge(gz_drained, l * 24 + 8)
                pool.wait_ge(roped, l * 8 + 6)
                rope(z[:, :, C_QN : C_QN + 512], 8, True)
                pool.wait_ge(gz_drained, l * 24 + 10)
                pool.wait_ge(roped, l * 8 + 7)
                rope(z[:, :, C_QD : C_QD + 512], 8, True)
                pool.wait_ge(roped, l * 8 + 8)

        @block.scalar
        def _(act):
            def split(l, at, u):
                n = at + u
                s = n % RING
                act.wait_ge(raw_in[s], (l * (LAYER_UNITS // RING) + n // RING + 1) * 16)
                act.wait_ge(unit_used, l * LAYER_UNITS + (n + 1))
                act.activation(whi[s][:, :], raw[s][:, :], ACT.Copy).then_inc(hi_done, 1)

            def split_in_loop(l, i, at, u):
                n = at + u
                s = n % RING
                act.wait_ge(raw_in[s], (l * (LAYER_UNITS // RING) + i + n // RING + 1) * 16)
                act.wait_ge(unit_used, l * LAYER_UNITS + i * RING + (n + 1))
                act.activation(whi[s][:, :], raw[s][:, :], ACT.Copy).then_inc(hi_done, 1)

            def lift(l, which):
                v = lift_of(l, which)
                if which == 0:
                    act.wait_ge(small_in_sem, (l + 1) * 16)
                for j, (tok, half) in enumerate(LIFT_ORDER[which]):
                    act.wait_ge(xt_filled, v * 4 + j + 1)
                    for k in range(4):
                        g = LIFT_GAIN[which] + half * 4 + k
                        act.activation(
                            xhi[:, half * 4 + k, tok * P : (tok + 1) * P], T[j % 2][:, k * P : (k + 1) * P],
                            ACT.Copy, scale=small[:, g : g + 1],
                        ).then_inc(xhi_done, 1)
                squares(v)

            def squares(v):
                for tok in range(TOKS):
                    if tok:
                        act.wait_ge(squares_done, v * 2 + 1)
                    act.activation(
                        probs[:, :], x[:, tok, :], ACT.Square, accum_out=ss[:, tok : tok + 1]
                    ).then_inc(squares_done, 1)

            def ffn(l, occ):
                o = l * 2 + occ
                at = occ * (FFN_UNITS + MIX_UNITS)
                lift(l, 2 * occ)

                def swish(g, tok, last_unit):
                    if tok:
                        act.wait_ge(unit_used, last_unit + 1 + CREDIT)
                    else:
                        act.wait_ge(gu_filled, g + 1)
                    act.activation(tg[:, tok, :], G[tok][:, 0:FCH], ACT.Tanh, scale=rs_half[:, tok : tok + 1]).then_inc(
                        tanh_done, 1
                    )

                def turn_h(n):
                    act.wait_ge(ht_filled, n)
                    act.activation(hThi[:, :, :].rearrange("p k t -> p (k t)"), T[0][:, :], ACT.Copy).then_inc(
                        ht_hi_done, 1
                    )

                act.wait_ge(rstd_done, lift_of(l, 2 * occ) + 1)
                if occ == 0:
                    act.wait_ge(merged_done, l * 4 + 1)
                    act.dma_start(
                        gates[:, :, :].rearrange("p t c -> p (t c)")[:, 0:W1C],
                        w1_in[bass.ds(l, 1), :, :].rearrange("l p n -> p (l n)"),
                    ).then_inc(w1_in_sem, 16)
                else:
                    act.dma_start(
                        small[:, :], small_in[bass.ds(l + 1, 1), :, :].rearrange("l p n -> p (l n)")
                    ).then_inc(small_in_sem, 16)
                swish(o * FI, 0, None)
                split(l, at, 3)
                swish(o * FI, 1, l * LAYER_UNITS + (at + 1))
                split(l, at, 4)
                with act.Fori(1, FI) as i:
                    g = o * FI + i
                    swish(g, 0, None)
                    turn_h(g)
                    split_in_loop(l, i, at, 2)
                    swish(g, 1, l * LAYER_UNITS + i * RING + at)
                    split_in_loop(l, i, at, 3)
                    split_in_loop(l, i, at, 4)
                turn_h(o * FI + FI)
                split(l, at, 3 * FI + 2)

            def mixer(l):
                at = FFN_UNITS
                lift(l, 1)
                act.wait_ge(rstd_done, lift_of(l, 1) + 1)

                def drain_z(c, tok):
                    wait_g(act, l, 2 * c + tok)
                    lo, hi = (0, C_S) if c == 0 else (C_S + (c - 1) * 512, C_S + c * 512)
                    act.activation(
                        z[:, tok, lo:hi], G[tok][:, 0 : hi - lo], ACT.Copy, scale=rs[:, tok : tok + 1]
                    ).then_inc(gz_drained, 1)

                def drain_gate(c, tok):
                    wait_g(act, l, 2 * c + tok)
                    o = (c - Z_CHUNKS) * 512
                    act.activation(
                        gates[:, tok, o : o + 512], G[tok][:, :], ACT.Tanh, scale=rs_half[:, tok : tok + 1]
                    ).then_inc(gz_drained, 1)

                def drain(name, dst, src, **kw):
                    act.wait_ge(t_filled, filled(l, name))
                    mark_drained(act.activation(dst, src, kw.pop("func", ACT.Copy), **kw), name)

                def relu(qt):
                    n = P * (qt + 1)
                    act.wait_ge(s_filled, l * (NB + 2) + qt + 1)
                    if qt:
                        act.wait_ge(index_summed, l * 2 + 1)
                    rl = sm[:, 0 : 4 * n].rearrange("p (a b n) -> p a b n", a=2, b=2)
                    for half in range(2):
                        ins = act.activation(
                            rl[:, :, half, :], SC[half][:, 0 : 2 * n].rearrange("p (a n) -> p a n", a=2),
                            ACT.Relu, scale=1.0 / 16,
                        )
                    ins.then_inc(s_drained, 1)

                def exps(b):
                    n, nh = keys_of(b), heads_of(b)
                    w = 16 if n == N_CMP else n
                    act.wait_ge(negmax_done, l * NB + b + 1)
                    if b:
                        act.wait_ge(t_filled, filled(l, turn_names(b - 1)[-1]))
                    for hh in range(nh):
                        ins = act.activation(
                            probs[:, hh * w : hh * w + n], sm[:, hh * w : hh * w + n], ACT.Exp,
                            scale=0.125, bias=negmax[:, hh : hh + 1], accum_out=sums[b % 2][:, hh : hh + 1],
                        )
                    ins.then_inc(exp_done, 1)

                def drain_probs(b):
                    if b:
                        act.wait_ge(o_filled, l * NB + b)
                    rows = N_CMP if BATCHES[b][0] == "cmp" else P
                    for j, name in enumerate(turn_names(b)):
                        n = len(turns_of(b)[j])
                        drain(
                            name, pT[0:rows, 4 * j : 4 * j + n, :].rearrange("p b q -> p (b q)"),
                            turn_bank(name)[0:rows, 0 : n * P],
                        )

                def split_y(name, dst, ks):
                    tok = int(name[-1]) if name[:2] in ("yc", "ya") else MERGED_ORDER[int(name[-1])][0]
                    act.wait_ge(t_filled, filled(l, name))
                    act.activation(
                        dst[:, ks : ks + 4, tok * P : (tok + 1) * P],
                        turn_bank(name)[:, :].rearrange("p (k t) -> p k t", k=4), ACT.Copy,
                    ).then_inc(t_hi_done, 1)

                drain_z(0, 0)
                drain_z(0, 1)
                act.wait_ge(gz_drained, l * 24 + 2)
                for tok in range(TOKS):
                    if tok:
                        act.wait_ge(kv_squares, l * 2 + 1)
                    act.activation(
                        probs[:, 0:P], z[:, tok, C_CKV : C_CKV + P], ACT.Square, accum_out=sskv[:, tok : tok + 1]
                    ).then_inc(kv_squares, 1)
                act.activation(sig[:, :, :], z[:, :, C_GATE : C_GATE + 24], ACT.Tanh, scale=0.5).then_inc(gate_tanh, 1)
                split(l, at, 3)
                drain_z(1, 0)
                drain("ckv", ckvT[:, :], turn_bank("ckv")[:, 0:S], scale=small[:, W_KVG : W_KVG + 1])
                drain_z(1, 1)
                split(l, at, 4)
                split(l, at, 5)
                drain_z(2, 0)
                drain("ik", ikT[:, :], turn_bank("ik")[:, 0:S])
                drain("iq", iqT[:, :, :].rearrange("p a t -> p (a t)"), turn_bank("iq")[:, :])
                split(l, at, 6)
                drain_z(2, 1)
                drain("kd", kdT[:, :], turn_bank("kd")[:, 0:S])
                relu(0)
                split(l, at, 7)
                drain_z(3, 0)
                kvc = turn_bank("kvc")[:, :].rearrange("p (y t) -> p y t", y=2)
                act.wait_ge(t_filled, filled(l, "kvc"))
                act.activation(kvcT[0:HD, 0:4:2, :], kvc[0:HD], ACT.Copy)
                drain("kvc", kvcT[0:HD, 1:4:2, :], kvc[HD:P])
                wait_drained(act, l, "kvc")
                act.dma_start(kvcT[HD:P, :, 0 : S - 1], kvcT[0:HD, :, 1:S]).then_inc(shifted, 16)
                relu(1)
                split(l, at, 8)
                drain_z(3, 1)
                drain("ksw", kswT[:, :, :].rearrange("p a t -> p (a t)"), turn_bank("ksw")[:, :])
                split(l, at, 9)
                drain_z(4, 0)
                for j in range(2):
                    drain(
                        f"qn{j}", qnT[:, 2 * j : 2 * j + 2, :].rearrange("p a t -> p (a t)"),
                        turn_bank(f"qn{j}")[:, :],
                    )
                split(l, at, 10)
                drain_z(4, 1)
                act.wait_ge(gelu_inner, l + 1)
                act.activation(gel[:, 3, :, :], gel[:, 2, :, :], ACT.Tanh, scale=0.7978845608028654).then_inc(
                    gelu_tanh, 1
                )
                split(l, at, 11)
                drain_z(5, 0)
                for j in range(2):
                    drain(
                        f"qd{j}", qdT[:, 2 * j : 2 * j + 2, :].rearrange("p a t -> p (a t)"),
                        turn_bank(f"qd{j}")[:, :],
                    )
                exps(0)
                split(l, at, 12)
                drain_z(5, 1)
                act.wait_ge(t_filled, filled(l, "cmpo"))
                act.activation(kcT[:, 0:N_CMP], turn_bank("cmpo")[:, 0:N_CMP], ACT.Copy, scale=0.5)
                drain(
                    "cmpo", vc[0:N_CMP, :, :].rearrange("p g d -> p (g d)"), turn_bank("cmpo")[0:N_CMP, 64:192],
                    scale=0.5,
                )
                drain_probs(0)
                exps(1)
                split(l, at, 13)
                for k in range(12):
                    c, tok = Z_CHUNKS + k // 2, k % 2
                    if tok:
                        split(l, at, 2 * c + 2)
                    drain_gate(c, tok)
                    drain_probs(k + 1)
                    if k + LEAD < NB:
                        exps(k + LEAD)
                    if k < 2:
                        drain(
                            f"band{k}", pooledT[:, 2 * k : 2 * k + 2, :].rearrange("p g t -> p (g t)"),
                            turn_bank(f"band{k}")[:, :],
                        )
                    elif k < 4:
                        name = f"yb{k - 2}"
                        act.wait_ge(t_filled, filled(l, name))
                        for g in range(2):
                            gg = 2 * (k - 2) + g
                            ins = act.activation(
                                ybhi[:, gg, :], turn_bank(name)[:, g * S : (g + 1) * S], ACT.Copy,
                                scale=small[:, W_PSC + gg : W_PSC + gg + 1],
                            )
                        ins.then_inc(t_hi_done, 1)
                    if tok:
                        split(l, at, 2 * c + 3)
                for j in range(2):
                    split_y(f"yc{j}", xhi, 0)
                split(l, at, 26)
                drain_probs(13)
                split(l, at, 27)
                split(l, at, 28)
                split(l, at, 29)
                for j in range(2):
                    split_y(f"ya{j}", xhi, 4)
                split(l, at, 30)
                split(l, at, 31)
                for j, (tok, half) in enumerate(MERGED_ORDER):
                    split_y(f"mg{j}", xhi, 4 * half)
                for u in range(32, 36):
                    split(l, at, u)

            act.dma_start(small[:, :], small_in[0, :, :]).then_inc(small_in_sem, 16)
            act.nop().then_inc(hi_done, CREDIT)
            act.wait_ge(trig_arg, 1)
            act.activation(ang[:, 3, :, :], ang[:, 0, :, :], ACT.Sin)
            act.activation(ang[:, 4, :, :], ang[:, 1, :, :], ACT.Sin).then_inc(trig_done, 1)
            for u in range(RING):
                act.wait_ge(raw_in[u], 16)
                act.wait_ge(unit_used, u + 1)
                act.activation(whi[u][:, :], raw[u][:, :], ACT.Copy).then_inc(hi_done, 1)
            with act.Fori(0, L) as l:
                ffn(l, 0)
                mixer(l)
                ffn(l, 1)
            act.wait_ge(x_up, 4 * (3 * L + 1))
            squares(3 * L)
            act.wait_ge(small_in_sem, (L + 1) * 16)

        @block.vector
        def _(dve):
            steps = Steps(dve, dve_step)

            def subtract_hi(s):
                dve.tensor_tensor(
                    wlo[s][:, :], raw[s][:, :], whi[s][:, :].bitcast(F32), ALU.subtract
                ).then_inc(lo_done, 1)

            def split(l, at, u):
                n = at + u
                dve.wait_ge(hi_done, l * LAYER_UNITS + n + 1 + CREDIT)
                subtract_hi(n % RING)

            def split_in_loop(l, i, at, u):
                n = at + u
                dve.wait_ge(hi_done, l * LAYER_UNITS + i * RING + n + 1 + CREDIT)
                subtract_hi(n % RING)

            def rsqrt(sumsq, m, mh, r, a, b, n):
                then = steps.then
                then(dve.tensor_scalar(m, sumsq, 1.0 / n, EPS, ALU.mult, ALU.add))
                dve.tensor_scalar(r.bitcast(I32), m.bitcast(I32), -0.5, float(0x5F3759DF), ALU.mult, ALU.add)
                then(dve.tensor_scalar(mh, m, -0.5, None, ALU.mult))
                for _ in range(4):
                    then(dve.tensor_tensor(a, r, r, ALU.mult))
                    then(dve.tensor_tensor(b, a, mh, ALU.mult))
                    then(dve.scalar_tensor_tensor(r, b, 1.5, r, ALU.add, ALU.mult))

            def lift(l, which):
                v = lift_of(l, which)
                if which == 0:
                    dve.wait_ge(small_in_sem, (l + 1) * 16)
                for j, (tok, half) in enumerate(LIFT_ORDER[which]):
                    dve.wait_ge(xhi_done, v * 16 + j * 4 + 4)
                    for k in range(4):
                        g = LIFT_GAIN[which] + half * 4 + k
                        kt, sl = half * 4 + k, slice(tok * P, (tok + 1) * P)
                        dve.scalar_tensor_tensor(
                            xlo[:, kt, sl], T[j % 2][:, k * P : (k + 1) * P], small[:, g : g + 1],
                            xhi[:, kt, sl].bitcast(F32), ALU.mult, ALU.subtract,
                        ).then_inc(xlo_done, 1)
                root_mean_square(v * 2 + 2)
                dve.tensor_scalar(rs_half, rs, 0.5, None, ALU.mult)
                dve.tensor_tensor(rs_sq, rs, rs, ALU.mult).then_inc(rstd_done, 1)

            def root_mean_square(count):
                dve.wait_ge(squares_done, count)
                rsqrt(ss, ms, msh, rs, t0, t1, D)

            def ffn(l, occ):
                o = l * 2 + occ
                at = occ * (FFN_UNITS + MIX_UNITS)
                lift(l, 2 * occ)

                def swiglu(g, tok, chain):
                    dve.wait_ge(tanh_done, g * 2 + tok + 1)
                    chain(dve.scalar_tensor_tensor(h[:, tok, :], tg[:, tok, :], 1.0, G[tok][:, 0:FCH], ALU.add, ALU.mult))
                    dve.scalar_tensor_tensor(
                        h[:, tok, :], h[:, tok, :], rs_sq[:, tok : tok + 1], G[tok][:, FCH : 2 * FCH], ALU.mult, ALU.mult
                    ).then_inc(h_done, 1)

                def turn_h(n):
                    dve.wait_ge(ht_hi_done, n)
                    dve.tensor_tensor(
                        hTlo[:, :, :].rearrange("p k t -> p (k t)"), T[0][:, :],
                        hThi[:, :, :].rearrange("p k t -> p (k t)").bitcast(F32), ALU.subtract,
                    ).then_inc(ht_lo_done, 1)

                steps.restart()
                dve.wait_ge(rstd_done, lift_of(l, 2 * occ) + 1)
                swiglu(o * FI, 0, steps.then)
                split(l, at, 3)
                swiglu(o * FI, 1, steps.then)
                split(l, at, 4)
                with dve.Fori(1, FI) as i:
                    steps.restart()
                    g = o * FI + i
                    dve.wait_ge(ht_filled, g)
                    swiglu(g, 0, steps.then)
                    turn_h(g)
                    split_in_loop(l, i, at, 2)
                    swiglu(g, 1, steps.then)
                    split_in_loop(l, i, at, 3)
                    split_in_loop(l, i, at, 4)
                turn_h(o * FI + FI)
                for tok in range(TOKS):
                    if tok:
                        dve.wait_ge(unit_used, unit_value(l, at + FFN_UNITS - 1))
                    else:
                        dve.wait_ge(acc_done, o + 1)
                    for half in range(2):
                        sl = slice(half * 512, half * 512 + 512)
                        dve.scalar_tensor_tensor(
                            x[:, tok, sl], ACC[tok][half][:, :], 0.25, x[:, tok, sl], ALU.mult, ALU.add
                        ).then_inc(x_up, 1)
                split(l, at, 3 * FI + 2)
                steps.restart()

            def mixer(l):
                at = FFN_UNITS
                then = steps.then
                lift(l, 1)

                def index_scores(qt):
                    n = P * (qt + 1)
                    dve.wait_ge(s_drained, l * (NB + 2) + qt + 1)
                    w = work[:, qt, 0:n]
                    for hh in range(4):
                        r = sm[:, hh * n : (hh + 1) * n]
                        iw = z[:, qt, C_IW + hh : C_IW + hh + 1]
                        if hh == 0:
                            then(dve.tensor_scalar(w, r, iw, None, ALU.mult))
                        else:
                            ins = dve.scalar_tensor_tensor(w, r, iw, w, ALU.mult, ALU.add)
                            if hh == 3:
                                ins.then_inc(index_summed, 1)
                                dve.wait_ge(index_summed, l * 2 + qt + 1)
                            else:
                                then(ins)
                    then(dve.tensor_tensor(w, w, const[:, K_CB + S - n : K_CB + S], ALU.add))

                def topk_round():
                    for qt in range(2):
                        ins = dve.max(top8[:, qt, :], work[:, qt, 0 : P * (qt + 1)])
                    then(ins)
                    for qt in range(2):
                        w = work[:, qt, 0 : P * (qt + 1)]
                        ins = dve.match_replace(w, top8[:, qt, :], w, TAKEN)
                    then(ins)

                def selection_bias():
                    for qt in range(2):
                        w = work[:, qt, 0 : P * (qt + 1)]
                        ins = dve.tensor_scalar(w, w, 0.5 * TAKEN, NEG, ALU.is_ge, ALU.mult)
                    then(ins)
                    for qt in range(2):
                        n = P * (qt + 1)
                        w = work[:, qt, 0:n]
                        ins = dve.tensor_tensor(w, w, const[:, K_CB + S - n : K_CB + S], ALU.min)
                    then(ins)

                def mask_and_max(b):
                    kind, qt, _ = BATCHES[b]
                    n, nh = keys_of(b), heads_of(b)
                    w = 16 if kind == "cmp" else n
                    if kind == "cmp":
                        bias = const[:, K_CMPB + 16 * qt : K_CMPB + 16 * qt + n]
                    elif kind == "dsa":
                        bias = work[:, qt, 0:n]
                    else:
                        bias = const[:, K_CB + S - n : K_CB + S]
                    dve.wait_ge(s_filled, l * (NB + 2) + b + 3)
                    if b:
                        dve.wait_ge(exp_done, l * NB + b)
                    dve.memset(unread, 0.0)
                    for hh in range(nh):
                        ins = dve.tensor_tensor_reduce(
                            sm[:, hh * w : hh * w + n], SC[hh % 2][:, (hh // 2) * n : (hh // 2 + 1) * n], bias,
                            1.0, -3.4e38, ALU.add, ALU.max, rowmax[:, hh : hh + 1],
                        )
                    ins.then_inc(s_drained, 1)
                    dve.wait_ge(s_drained, l * (NB + 2) + b + 3)
                    dve.tensor_scalar(negmax[:, 0:nh], rowmax[:, 0:nh], -0.125, None, ALU.mult).then_inc(negmax_done, 1)

                def drain_o(b):
                    kind, qt, g = BATCHES[b]
                    nh = heads_of(b)
                    f = fac[:, 0:nh]
                    dve.wait_ge(exp_done, l * NB + b + 1)
                    then(dve.reciprocal(f, sums[b % 2][:, 0:nh]))
                    if kind != "dsa":
                        j = ("cmp", "sel", "win").index(kind)
                        gate = sig[:, qt, 8 * j + 4 * g : 8 * j + 4 * g + nh]
                        if kind == "cmp":
                            then(dve.scalar_tensor_tensor(
                                f, f, const[:, K_VALID + qt : K_VALID + qt + 1], gate, ALU.mult, ALU.mult))
                        else:
                            then(dve.tensor_tensor(f, f, gate, ALU.mult))
                    dve.wait_ge(o_filled, l * NB + b + 1)
                    src = O[b % 2][:, 0 : nh * HD].rearrange("p (h d) -> p h d", d=HD)
                    fb = f.unsqueeze(2).to_broadcast([P, nh, HD])
                    branch = 0 if kind == "dsa" else 1
                    dst = y[:, qt, branch, 256 * g : 256 * g + nh * HD].rearrange("p (h d) -> p h d", d=HD)
                    if kind in ("dsa", "sel"):
                        dve.tensor_tensor(dst, src, fb, ALU.mult).then_inc(o_drained, 1)
                    else:
                        tmp = oacc[:, 0 : nh * HD].rearrange("p (h d) -> p h d", d=HD)
                        dve.tensor_tensor(tmp, src, fb, ALU.mult).then_inc(o_drained, 1)
                        dve.wait_ge(o_drained, l * NB + b + 1)
                        ins = dve.tensor_tensor(dst, dst, tmp, ALU.add)
                        if kind == "cmp":
                            ins.then_inc(y_done, 1)
                        else:
                            then(ins)

                def split_y(name, n_hi, dst_hi, dst_lo, ks):
                    tok = int(name[-1]) if name[:2] in ("yc", "ya") else MERGED_ORDER[int(name[-1])][0]
                    dve.wait_ge(t_hi_done, l * 10 + n_hi)
                    sl = slice(tok * P, (tok + 1) * P)
                    mark_drained(dve.tensor_tensor(
                        dst_lo[:, ks : ks + 4, sl], turn_bank(name)[:, :].rearrange("p (k t) -> p k t", k=4),
                        dst_hi[:, ks : ks + 4, sl].bitcast(F32), ALU.subtract), name)

                def gated(b_, branch, half, tok):
                    f = 24 + 4 * b_ + 2 * half + tok
                    wait_g(dve, l, f)
                    if b_ == 0 and half == 0:
                        dve.wait_ge(gz_drained, l * 24 + 24)
                    own = gates[:, tok, branch * D + half * 512 : branch * D + half * 512 + 512]
                    total = gates[:, tok, D + half * 512 : D + half * 512 + 512]
                    dve.scalar_tensor_tensor(own, own, 1.0, G[tok][:, :], ALU.add, ALU.mult).then_inc(gp_drained, 1)
                    dve.wait_ge(gp_drained, l * 12 + f - 24 + 1)
                    if b_:
                        ins = dve.tensor_tensor(total, total, own, ALU.add)
                        if b_ == 2:
                            ins.then_inc(merged_done, 1)
                        else:
                            then(ins)

                split(l, at, 3)
                dve.wait_ge(gate_tanh, l + 1)
                then(dve.tensor_scalar(sig[:, :, :], sig[:, :, :], 0.5, 0.5, ALU.mult, ALU.add))
                dve.wait_ge(kv_squares, l * 2 + 2)
                rsqrt(sskv, kms, kmsh, rkv, kt0, kt1, P)
                split(l, at, 4)
                dve.wait_ge(t_filled, filled(l, "kv"))
                for tok in range(TOKS):
                    ins = dve.tensor_scalar(
                        zkv[:, tok, :], turn_bank("kv")[:, tok * P : (tok + 1) * P], rkv[:, tok : tok + 1], None, ALU.mult
                    )
                mark_drained(ins, "kv")
                split(l, at, 5)
                split(l, at, 6)
                index_scores(0)
                split(l, at, 7)
                index_scores(1)
                split(l, at, 8)
                split(l, at, 9)
                split(l, at, 10)
                dve.wait_ge(t_filled, filled(l, "hid"))
                hid = turn_bank("hid")
                then(dve.tensor_copy(gbias[:, :], hid[:, 64:66]))
                for y_ in range(2):
                    ins = dve.tensor_scalar(
                        gel[:, 0, y_, :], hid[:, 32 * y_ : 32 * y_ + 30], gbias[:, y_ : y_ + 1], None, ALU.add)
                mark_drained(ins, "hid")
                i = TURN_AT["hid"]
                dve.wait_ge(t_drained[i % 2], l * PER_BANK[i % 2] + i // 2 + 1)
                then(dve.tensor_tensor(gel[:, 1, :, :], gel[:, 0, :, :], gel[:, 0, :, :], ALU.mult))
                then(dve.tensor_scalar(gel[:, 1, :, :], gel[:, 1, :, :], 0.044715, 1.0, ALU.mult, ALU.add))
                dve.tensor_tensor(gel[:, 2, :, :], gel[:, 1, :, :], gel[:, 0, :, :], ALU.mult).then_inc(gelu_inner, 1)
                split(l, at, 11)
                dve.wait_ge(gelu_tanh, l + 1)
                dve.scalar_tensor_tensor(
                    gel[:, 4, :, :], gel[:, 3, :, :], 1.0, gel[:, 0, :, :], ALU.add, ALU.mult).then_inc(gelu_done, 1)
                mask_and_max(0)
                split(l, at, 12)
                mask_and_max(1)
                split(l, at, 13)
                for k in range(12):
                    c, tok = Z_CHUNKS + k // 2, k % 2
                    if tok:
                        split(l, at, 2 * c + 2)
                    drain_o(k)
                    if k == 8:
                        selection_bias()
                    if k + LEAD < NB:
                        mask_and_max(k + LEAD)
                    if k < 8:
                        topk_round()
                    if 2 <= k < 4:
                        name = f"yb{k - 2}"
                        dve.wait_ge(t_hi_done, l * 10 + k - 1)
                        for g in range(2):
                            gg = 2 * (k - 2) + g
                            ins = dve.scalar_tensor_tensor(
                                yblo[:, gg, :], turn_bank(name)[:, g * S : (g + 1) * S],
                                small[:, W_PSC + gg : W_PSC + gg + 1], ybhi[:, gg, :].bitcast(F32),
                                ALU.mult, ALU.subtract)
                        mark_drained(ins, name)
                    if tok:
                        split(l, at, 2 * c + 3)
                for j in range(2):
                    split_y(f"yc{j}", 3 + j, xhi, xlo, 0)
                gated(0, 1, 0, 0)
                gated(0, 1, 0, 1)
                split(l, at, 26)
                drain_o(12)
                gated(0, 1, 1, 0)
                gated(0, 1, 1, 1)
                split(l, at, 27)
                drain_o(13)
                for half in range(2):
                    for tok in range(TOKS):
                        gated(1, 2, half, tok)
                    split(l, at, 28 + half)
                for j in range(2):
                    split_y(f"ya{j}", 5 + j, xhi, xlo, 4)
                for half in range(2):
                    for tok in range(TOKS):
                        gated(2, 0, half, tok)
                    split(l, at, 30 + half)
                for j, (tok, half) in enumerate(MERGED_ORDER):
                    split_y(f"mg{j}", 7 + j, xhi, xlo, 4 * half)
                for half in range(2):
                    split(l, at, 32 + 2 * half)
                    for tok in range(TOKS):
                        f = 36 + 2 * half + tok
                        sl = slice(half * 512, half * 512 + 512)
                        wait_g(dve, l, f)
                        dve.scalar_tensor_tensor(
                            x[:, tok, sl], G[tok][:, :], 0.5, x[:, tok, sl], ALU.mult, ALU.add
                        ).then_inc(x_up, 1)
                    split(l, at, 33 + 2 * half)

            dve.nop().then_inc(lo_done, CREDIT)
            dve.nop().then_inc(merged_done, 1)
            dve.wait_ge(pos_in_sem, 16)
            dve.wait_ge(const_in_sem, 16)
            then = steps.then
            a0, a1, a2 = ang[:, 0, :, :], ang[:, 1, :, :], ang[:, 2, :, :]
            a3, a4 = ang[:, 3, :, :], ang[:, 4, :, :]
            then(dve.tensor_copy(t0, posi[:, :]))
            freq = const[:, K_FREQ : K_FREQ + HALF_ROT].unsqueeze(1).to_broadcast([P, TOKS, HALF_ROT])
            then(dve.tensor_tensor(a0, t0.unsqueeze(2).to_broadcast([P, TOKS, HALF_ROT]), freq, ALU.mult))
            magic = 1.5 * 2.0**23
            turns = a1
            then(dve.tensor_scalar(turns, a0, float(np.float32(1 / (2 * np.pi))), magic, ALU.mult, ALU.add))
            then(dve.tensor_scalar(turns, turns, -magic, None, ALU.add))
            then(dve.tensor_scalar(a2, turns, 1.0 / 4096, magic, ALU.mult, ALU.add))
            then(dve.tensor_scalar(a2, a2, -magic, 4096.0, ALU.add, ALU.mult))
            then(dve.tensor_tensor(a3, turns, a2, ALU.subtract))
            rest = 2 * np.pi
            for bits in (9, 21, 33, 45):
                part = np.floor(rest * 2.0**bits) / 2.0**bits
                rest -= part
                for src in (a2, a3):
                    then(dve.scalar_tensor_tensor(a0, src, -float(part), a0, ALU.mult, ALU.add))
            then(dve.tensor_scalar(a0, a0, 3.1415925, -3.1415925, ALU.min, ALU.max))
            then(dve.tensor_scalar(a1, a0, -1.0, None, ALU.mult))
            then(dve.tensor_tensor(a1, a0, a1, ALU.max))
            dve.tensor_scalar(a1, a1, -1.0, float(np.pi / 2), ALU.mult, ALU.add).then_inc(trig_arg, 1)
            dve.wait_ge(trig_done, 1)
            dve.tensor_copy(cos16[:, :, 0:8], a4)
            dve.tensor_copy(cos16[:, :, 8:16], a4)
            dve.tensor_scalar(sin16[:, :, 0:8], a3, -1.0, None, ALU.mult)
            then(dve.tensor_copy(sin16[:, :, 8:16], a3))
            dve.nop().then_inc(tables_ready, 1)
            for u in range(RING):
                dve.wait_ge(hi_done, u + 1 + CREDIT)
                subtract_hi(u)
            dve.wait_ge(x_in_sem, 16)
            dve.nop().then_inc(x_up, 4)
            with dve.Fori(0, L) as l:
                steps.restart()
                ffn(l, 0)
                mixer(l)
                ffn(l, 1)
            root_mean_square(6 * L + 2)
            dve.wait_ge(final_in_sem, 16)
            for tok in range(TOKS):
                dve.scalar_tensor_tensor(
                    x[:, tok, :], x[:, tok, :], rs[:, tok : tok + 1], z[:, 0, 0:D], ALU.mult, ALU.mult
                ).then_inc(out_ready, 1)

        @block.tensor
        def _(pe):
            def mm3(o, ahi, alo, bhi, blo, first, last):
                pe.matmul(o, ahi, bhi, start=first, stop=False)
                pe.matmul(o, ahi, blo, start=False, stop=False)
                return pe.matmul(o, alo, bhi, start=False, stop=last)

            def wait_unit(l, n):
                pe.wait_ge(lo_done, l * LAYER_UNITS + n + 1 + CREDIT)

            def lift(l, which):
                v = lift_of(l, which)
                for j, (tok, half) in enumerate(LIFT_ORDER[which]):
                    pe.wait_ge(x_up, v * 4 + j + 1)
                    if j >= 2:
                        pe.wait_ge(xlo_done, v * 16 + 4 * (j - 1))
                    for k in range(4):
                        c = half * 512 + k * P
                        ins = pe.transpose(T[j % 2][:, k * P : (k + 1) * P], x[:, tok, c : c + P], ident)
                    ins.then_inc(xt_filled, 1)

            def wait_lifted(l, which, tok, half):
                j = LIFT_ORDER[which].index((tok, half))
                pe.wait_ge(xlo_done, lift_of(l, which) * 16 + 4 * (j + 1))

            def gemm_half(o, tok, hi, lo, k0, s, n, first, last, kts=4):
                for k in range(kts):
                    sl = slice(tok * P, (tok + 1) * P)
                    ins = mm3(
                        o[:, 0:n], hi[:, k0 + k, sl], lo[:, k0 + k, sl], whi[s][:, k * n : (k + 1) * n],
                        wlo[s][:, k * n : (k + 1) * n], first and k == 0, last and k == kts - 1,
                    )
                return ins

            def ffn(l, occ):
                o = l * 2 + occ
                at = occ * (FFN_UNITS + MIX_UNITS)
                which = 2 * occ
                lift(l, which)

                def gate_up(i, tok, peeled=False):
                    first_unit = at if peeled else i * RING + (at - 1)
                    slot = at if peeled else at - 1
                    if not peeled:
                        pe.wait_ge(h_done, (o * FI + i) * 2 + tok - 1)
                    for a in range(2):
                        if tok == 0:
                            pe.wait_ge(lo_done, l * LAYER_UNITS + first_unit + a + 1 + CREDIT)
                        if peeled:
                            wait_lifted(l, which, tok, a)
                        ins = gemm_half(G[tok], tok, xhi, xlo, 4 * a, (slot + a) % RING, 512, a == 0, a == 1)
                        if tok and a == 0:
                            ins.then_inc(unit_used, 1)
                    ins.then_inc(unit_used if tok else gu_filled, 1)

                def turn_h(n):
                    pe.wait_ge(h_done, n * 2)
                    for k in range(2):
                        for tok in range(TOKS):
                            ins = pe.transpose(
                                T[0][:, k * S + tok * P : k * S + (tok + 1) * P], h[:, tok, k * P : (k + 1) * P], ident)
                    ins.then_inc(ht_filled, 1)

                def down(n, unit, s, first, last):
                    pe.wait_ge(ht_lo_done, n)
                    pe.wait_ge(lo_done, unit + 1 + CREDIT)
                    for tok in range(TOKS):
                        sl = slice(tok * P, (tok + 1) * P)
                        for half in range(2):
                            for k in range(2):
                                c = k * D + half * 512
                                ins = mm3(
                                    ACC[tok][half][:, :], hThi[:, k, sl], hTlo[:, k, sl], whi[s][:, c : c + 512],
                                    wlo[s][:, c : c + 512], first and k == 0, last and k == 1,
                                )
                        if tok:
                            ins.then_inc(unit_used, 1)
                        elif last:
                            ins.then_inc(acc_done, 1)

                gate_up(0, 0, peeled=True)
                gate_up(0, 1, peeled=True)
                gate_up(1, 0)
                turn_h(o * FI + 1)
                gate_up(1, 1)
                down(o * FI + 1, l * LAYER_UNITS + (at + 4), (at + 4) % RING, True, False)
                with pe.Fori(2, FI) as i:
                    gate_up(i, 0)
                    turn_h(o * FI + i)
                    gate_up(i, 1)
                    down(o * FI + i, l * LAYER_UNITS + i * RING + (at + 1), (at + 1) % RING, False, False)
                turn_h(o * FI + FI)
                down(o * FI + FI, l * LAYER_UNITS + at + 32, (at + 32) % RING, False, True)

            def mixer(l):
                at = FFN_UNITS
                lift(l, 1)

                def chunk(c, tok):
                    f = 2 * c + tok
                    if f >= 2:
                        pe.wait_ge(gz_drained, l * 24 + f - 1)
                    n = C_S if c == 0 else 512
                    for a in range(2):
                        if c == 0:
                            u, off = 0, a * 4
                        else:
                            u, off = 2 * c - 1 + a, 0
                            if tok == 0:
                                wait_unit(l, at + u)
                        if c == 0:
                            wait_unit(l, at)
                            wait_lifted(l, 1, tok, a)
                        s = (at + u) % RING
                        sl = slice(tok * P, (tok + 1) * P)
                        for k in range(4):
                            w = slice((off + k) * n, (off + k + 1) * n)
                            ins = mm3(
                                G[tok][:, 0:n], xhi[:, 4 * a + k, sl], xlo[:, 4 * a + k, sl], whi[s][:, w], wlo[s][:, w],
                                a == 0 and k == 0, a == 1 and k == 3)
                        if tok and c and a == 0:
                            ins.then_inc(unit_used, 1)
                    ins.then_inc(unit_used if tok else g_filled, 1)

                def unit_gemm(f, u, hi, lo, k0, tok, first, last):
                    s = (at + u) % RING
                    if tok == 0:
                        wait_unit(l, at + u)
                    return gemm_half(G[tok], tok, hi, lo, k0, s, 512, first, last)

                def open_turn(name, *needs):
                    wait_drained(pe, l, *needs, opening=name)
                    return turn_bank(name)

                def turn(name, tiles, rows=P):
                    t = open_turn(name)
                    for n, src in enumerate(tiles):
                        ins = pe.transpose(t[0:rows, n * P : (n + 1) * P], src, ident)
                    ins.then_inc(t_filled, 1)

                def scores(si, qT, kT_, pairs, qt, n):
                    if si:
                        pe.wait_ge(s_drained, l * (NB + 2) + si)
                    for j, pr in enumerate(pairs):
                        for half in range(2):
                            rows = slice(half * HD, (half + 1) * HD)
                            ins = pe.matmul(
                                SC[half][:, j * n : (j + 1) * n], qT[rows, pr, qt * P : (qt + 1) * P], kT_[rows, 0:n],
                                start=True, stop=True)
                    ins.then_inc(s_filled, 1)

                def batch_scores(b):
                    kind, qt, g = BATCHES[b]
                    if b == 0:
                        wait_drained(pe, l, "qn0", "qn1", "ksw")
                    if kind == "cmp" and qt == 0:
                        wait_drained(pe, l, "cmpo")
                    if kind == "dsa" and qt == 0 and g == 0:
                        wait_drained(pe, l, "qd0", "qd1", "kd")
                    qT = qdT if kind == "dsa" else qnT
                    keys = {"sel": kswT[:, 0, :], "win": kswT[:, 1, :], "cmp": kcT, "dsa": kdT}[kind]
                    pairs = range(4) if kind == "cmp" else range(2 * g, 2 * g + 2)
                    scores(b + 2, qT, keys, pairs, qt, keys_of(b))

                def batch_turn(b):
                    n = keys_of(b)
                    w = 16 if n == N_CMP else n
                    bw = min(n, P)
                    pe.wait_ge(exp_done, l * NB + b + 1)
                    for j, name in enumerate(turn_names(b)):
                        turn(
                            name, [probs[:, hh * w + kb * P : hh * w + kb * P + bw] for hh, kb in turns_of(b)[j]],
                            rows=bw)

                def batch_values(b):
                    kind, qt, g = BATCHES[b]
                    if b >= 2:
                        pe.wait_ge(o_drained, l * NB + b - 1)
                    wait_drained(pe, l, *turn_names(b))
                    for j, name in enumerate(turn_names(b)):
                        for n, (hh, kb) in enumerate(turns_of(b)[j]):
                            grp = hh % 2
                            if kind == "cmp":
                                lhs, rhs, last = pT[0:N_CMP, 4 * j + n, :], vc[0:N_CMP, grp, :], True
                            else:
                                v = {
                                    "sel": z[:, kb, C_KVS + 128 + HD * grp : C_KVS + 128 + HD * (grp + 1)],
                                    "win": z[:, kb, C_KVW + 128 + HD * grp : C_KVW + 128 + HD * (grp + 1)],
                                    "dsa": zkv[:, kb, HD:P],
                                }[kind]
                                lhs, rhs, last = pT[:, 4 * j + n, :], v, kb == qt
                            ins = pe.matmul(O[b % 2][:, hh * HD : (hh + 1) * HD], lhs, rhs, start=kb == 0, stop=last)
                    ins.then_inc(o_filled, 1)

                def wait_roped(n):
                    pe.wait_ge(roped, l * 8 + n)

                def pairs_of(col, n):
                    return [z[:, tok, col + P * pr : col + P * (pr + 1)] for pr in n for tok in range(TOKS)]

                chunk(0, 0)
                chunk(0, 1)
                chunk(1, 0)
                pe.wait_ge(gz_drained, l * 24 + 2)
                turn("ckv", [z[:, tok, C_CKV : C_CKV + P] for tok in range(TOKS)])
                chunk(1, 1)
                t = open_turn("kv", "ckv")
                for tok in range(TOKS):
                    ins = pe.matmul(
                        t[:, tok * P : (tok + 1) * P], ckvT[:, tok * P : (tok + 1) * P], small[:, W_UKV : W_UKV + P],
                        start=True, stop=True)
                ins.then_inc(t_filled, 1)
                chunk(2, 0)
                wait_roped(2)
                turn("ik", [ikd[:, tok, :, :].rearrange("p a d -> p (a d)") for tok in range(TOKS)])
                turn("iq", pairs_of(C_IQ, range(2)))
                chunk(2, 1)
                wait_roped(4)
                turn("kd", [kd[:, tok, :, :].rearrange("p a d -> p (a d)") for tok in range(TOKS)])
                wait_drained(pe, l, "ik", "iq")
                scores(0, iqT, ikT, range(2), 0, P)
                chunk(3, 0)
                wait_roped(3)
                turn("kvc", pairs_of(C_KVC, range(2)))
                scores(1, iqT, ikT, range(2), 1, S)
                chunk(3, 1)
                wait_roped(6)
                turn("ksw", pairs_of(C_KVS, [0]) + pairs_of(C_KVW, [0]))
                chunk(4, 0)
                wait_roped(7)
                turn("qn0", pairs_of(C_QN, [0, 1]))
                turn("qn1", pairs_of(C_QN, [2, 3]))
                chunk(4, 1)
                t = open_turn("hid")
                pe.wait_ge(shifted, l * 16 + 16)
                pe.wait_ge(w1_in_sem, l * 16 + 16)
                for y_ in range(2):
                    for k in range(16):
                        pe.matmul(
                            t[:, 64 + y_ : 65 + y_], w1[:, y_, k, :], small[:, W_POS + 16 * y_ + k : W_POS + 16 * y_ + k + 1],
                            start=k == 0, stop=k == 15)
                    for k in range(16):
                        ins = pe.matmul(
                            t[:, 32 * y_ : 32 * y_ + 30].rearrange("p (g n) -> p g n", g=2), w1[:, y_, k, :],
                            kvcT[:, 2 * y_ : 2 * y_ + 2, 2 * k : 2 * k + 16 * (N_CMP - 1) + 1 : 16],
                            start=k == 0, stop=k == 15)
                ins.then_inc(t_filled, 1)
                chunk(5, 0)
                wait_roped(8)
                turn("qd0", pairs_of(C_QD, [0, 1]))
                turn("qd1", pairs_of(C_QD, [2, 3]))
                batch_scores(0)
                chunk(5, 1)
                t = open_turn("cmpo")
                pe.wait_ge(gelu_done, l + 1)
                for g in range(2):
                    pe.matmul(
                        t[g * HD : (g + 1) * HD, 0:N_CMP], small[:, W_W2 : W_W2 + HD],
                        gel[:, 4, 0, g * N_CMP : (g + 1) * N_CMP], start=True, stop=True)
                for g in range(2):
                    ins = pe.matmul(
                        t[0:N_CMP, 64 + g * HD : 64 + (g + 1) * HD], gel[:, 4, 1, g * N_CMP : (g + 1) * N_CMP],
                        small[:, W_W2 + HD : W_W2 + 2 * HD], start=True, stop=True)
                ins.then_inc(t_filled, 1)
                batch_turn(0)
                batch_scores(1)
                for k in range(12):
                    c, tok = Z_CHUNKS + k // 2, k % 2
                    chunk(c, tok)
                    batch_values(k)
                    batch_turn(k + 1)
                    if k + LEAD < NB:
                        batch_scores(k + LEAD)
                    if k < 2:
                        pe.wait_ge(gz_drained, l * 24 + 12)
                        t = open_turn(f"band{k}")
                        for g in range(2):
                            gg = 2 * k + g
                            u = [z[:, tk, C_U + gg * P : C_U + (gg + 1) * P] for tk in range(TOKS)]
                            band = const[:, K_BAND + gg * 384 : K_BAND + (gg + 1) * 384]
                            pe.matmul(t[:, g * S : (g + 1) * S], u[0], band[:, 0:S], start=g == 0, stop=False,
                                      skip_group_check=True)
                            ins = pe.matmul(t[:, g * S + P : (g + 1) * S], u[1], band[:, S : S + P], start=False,
                                            stop=True, skip_group_check=True)
                        ins.then_inc(t_filled, 1)
                    elif k < 4:
                        t = open_turn(f"yb{k - 2}", f"band{k - 2}")
                        for g in range(2):
                            gg = 2 * (k - 2) + g
                            ins = pe.matmul(
                                t[:, g * S : (g + 1) * S], small[:, W_POOL + gg * P : W_POOL + (gg + 1) * P],
                                pooledT[:, gg, :], start=True, stop=True)
                        ins.then_inc(t_filled, 1)

                def y_tiles(branch, tok):
                    return [y[:, tok, branch, k * P : (k + 1) * P] for k in range(4)]

                def project(b_, half, hi, lo, k0):
                    for tok in range(TOKS):
                        f = 24 + 4 * b_ + 2 * half + tok
                        if f < 26:
                            pe.wait_ge(gz_drained, l * 24 + f - 1)
                        else:
                            pe.wait_ge(gp_drained, l * 12 + f - 25)
                        ins = unit_gemm(f, 23 + 2 * b_ + half, hi, lo, k0, tok, True, True)
                        ins.then_inc(unit_used if tok else g_filled, 1)

                pe.wait_ge(y_done, l * 2 + 2)
                turn("yc0", y_tiles(1, 0))
                turn("yc1", y_tiles(1, 1))
                wait_drained(pe, l, "yb0", "yb1")
                project(0, 0, ybhi, yblo, 0)
                batch_values(12)
                batch_turn(13)
                project(0, 1, ybhi, yblo, 0)
                batch_values(13)
                wait_drained(pe, l, "yc0", "yc1")
                project(1, 0, xhi, xlo, 0)
                project(1, 1, xhi, xlo, 0)
                pe.wait_ge(o_drained, l * NB + NB)
                turn("ya0", y_tiles(0, 0))
                turn("ya1", y_tiles(0, 1))
                wait_drained(pe, l, "ya0", "ya1")
                project(2, 0, xhi, xlo, 4)
                project(2, 1, xhi, xlo, 4)
                for j, (tok, half) in enumerate(MERGED_ORDER):
                    pe.wait_ge(merged_done, l * 4 + j + 2)
                    turn(f"mg{j}", [gates[:, tok, D + half * 512 + k * P : D + half * 512 + (k + 1) * P] for k in range(4)])
                for n in range(2):
                    for tok in range(TOKS):
                        f = 36 + 2 * n + tok
                        if n == 0:
                            pe.wait_ge(gp_drained, l * 12 + f - 25)
                        else:
                            pe.wait_ge(x_up, lift_of(l, 2) * 4 + f - 37)
                        for a in range(2):
                            u = 29 + 2 * n + a
                            wait_drained(pe, l, f"mg{MERGED_ORDER.index((tok, a))}")
                            ins = unit_gemm(f, u, xhi, xlo, 4 * a, tok, a == 0, a == 1)
                            if tok and a == 0:
                                ins.then_inc(unit_used, 1)
                        ins.then_inc(unit_used if tok else g_filled, 1)

            pe.nop().then_inc(unit_used, CREDIT)
            pe.wait_ge(const_in_sem, 16)
            with pe.Fori(0, L) as l:
                ffn(l, 0)
                mixer(l)
                ffn(l, 1)


IN_SPLITS = (512, 128, 256, 64, 4, 512, 512, 256, 256, 256, 24, 3072)
PAIRED = [0, 4, 1, 5, 2, 6, 3, 7]


def _tiles(w):
    k, n = w.shape
    return w.reshape(k // P, P, n).transpose(1, 0, 2).reshape(P, -1)


def _ffn_units(gate, up, down):
    units = []

    def gu(i):
        c = slice(i * FCH, (i + 1) * FCH)
        w = np.concatenate([gate[:, c], up[:, c]], axis=1)
        units.extend([_tiles(w[:512]), _tiles(w[512:])])

    def dn(i):
        units.append(_tiles(down[i * FCH : (i + 1) * FCH]))

    gu(0)
    for i in range(1, FI):
        gu(i)
        dn(i - 1)
    dn(FI - 1)
    return units


def _mix_units(w_in, pa, pb, pc, w_out):
    offs = np.cumsum((0,) + IN_SPLITS)
    q, ckv, iq, ik, iw, u, cq, kvc, kvs, kvw, gate, merge = (
        w_in[:, offs[i] : offs[i + 1]] for i in range(len(IN_SPLITS)))
    cq = cq.reshape(D, 8, HD)[:, PAIRED].reshape(D, 512)
    gate = gate.reshape(D, 8, 3)[:, PAIRED].transpose(0, 2, 1).reshape(D, 24)
    pc = pc.reshape(8, HD, D)[PAIRED].reshape(512, D)
    cols = np.concatenate([ckv, ik, iw, gate, iq, kvc, kvs, kvw, cq, q, u, merge], axis=1)
    first = np.zeros((P, UNIT), np.float32)
    first[:, : KT * C_S] = _tiles(cols[:, :C_S])
    units = [first]
    for c in range(CHUNKS - 1):
        w = cols[:, C_S + c * 512 : C_S + (c + 1) * 512]
        units += [_tiles(w[:512]), _tiles(w[512:])]
    for w in (pb, pc, pa):
        units += [_tiles(w[:, :512]), _tiles(w[:, 512:])]
    for n in range(2):
        w = w_out[:, n * 512 : (n + 1) * 512]
        units += [_tiles(w[:512]), _tiles(w[512:])]
    return units


def _constants():
    c = np.zeros((P, KC), np.float32)
    r = np.arange(P)
    c[:, K_ID : K_ID + P] = np.eye(P)
    c[:, K_CB + P : K_CB + 2 * P] = np.where(r[None, :] <= r[:, None], 0.0, NEG)
    ends = np.arange(N_CMP) * 16 + 31
    for qt in range(2):
        t = qt * P + r
        ok = ends[None, :] <= t[:, None]
        c[:, K_CMPB + 16 * qt : K_CMPB + 16 * qt + N_CMP] = np.where(ok, 0.0, NEG)
        c[:, K_VALID + qt] = ok.any(axis=1)
    for g, w in enumerate(WINDOWS):
        s, t = np.arange(S)[:, None], np.arange(S)[None, :]
        band = ((s <= t) & (s > t - w)) / np.minimum(t + 1, w) - (s == t)
        c[:, K_BAND + g * 384 : K_BAND + g * 384 + S] = band[:P]
        c[:, K_BAND + g * 384 + S : K_BAND + (g + 1) * 384] = band[P:, P:]
    exps = -np.arange(0, 2 * HALF_ROT, 2, dtype=np.float32) / np.float32(2 * HALF_ROT)
    c[:, K_FREQ : K_FREQ + HALF_ROT] = np.float64(THETA) ** exps.astype(np.float64)
    return c


def kernel(x, positions, ffn1_norm, ffn1_gate, ffn1_up, ffn1_down, mix_norm, w_in,
           dsa_kv_norm, dsa_w_ukv, pool_w, pool_scale, nsa_cmp_pos, nsa_cmp_w1, nsa_cmp_w2,
           proj_a, proj_b, proj_c, w_out, ffn2_norm, ffn2_gate, ffn2_up, ffn2_down, final_norm):
    import concourse.bacc as _bacc
    from concourse.bass_utils import run_bass_kernel_spmd as _run

    a = [np.asarray(v) for v in (
        x, positions, ffn1_norm, ffn1_gate, ffn1_up, ffn1_down, mix_norm, w_in, dsa_kv_norm, dsa_w_ukv, pool_w,
        pool_scale, nsa_cmp_pos, nsa_cmp_w1, nsa_cmp_w2, proj_a, proj_b, proj_c, w_out, ffn2_norm, ffn2_gate,
        ffn2_up, ffn2_down, final_norm)]
    (x, positions, ffn1_norm, ffn1_gate, ffn1_up, ffn1_down, mix_norm, w_in, dsa_kv_norm, dsa_w_ukv, pool_w,
     pool_scale, nsa_cmp_pos, nsa_cmp_w1, nsa_cmp_w2, proj_a, proj_b, proj_c, w_out, ffn2_norm, ffn2_gate,
     ffn2_up, ffn2_down, final_norm) = a
    units = []
    small = np.zeros((L + 1, P, W_SMALL), np.float32)
    w1 = np.zeros((L, P, W1C), np.float32)
    for l in range(L):
        units += _ffn_units(ffn1_gate[l], ffn1_up[l], ffn1_down[l])
        units += _mix_units(w_in[l], proj_a[l], proj_b[l], proj_c[l], w_out[l])
        units += _ffn_units(ffn2_gate[l], ffn2_up[l], ffn2_down[l])
        s = small[l]
        s[:, W_G1 : W_G1 + 8] = ffn1_norm[l].reshape(8, P).T
        s[:, W_GM : W_GM + 8] = mix_norm[l].reshape(8, P).T
        s[:, W_G2 : W_G2 + 8] = ffn2_norm[l].reshape(8, P).T
        s[:, W_KVG] = dsa_kv_norm[l]
        s[:, W_PSC : W_PSC + 4] = pool_scale[l].reshape(4, P).T
        s[:, W_POS : W_POS + 32] = nsa_cmp_pos[l].reshape(2, 16, P).transpose(2, 0, 1).reshape(P, 32)
        s[:, W_UKV : W_UKV + P] = dsa_w_ukv[l]
        s[:, W_POOL : W_POOL + 512] = pool_w[l].transpose(1, 0, 2).reshape(P, 512)
        s[:, W_W2 : W_W2 + P] = nsa_cmp_w2[l].transpose(1, 0, 2).reshape(P, P)
        w1[l] = nsa_cmp_w1[l].reshape(2, 16, P, P).transpose(2, 0, 1, 3).reshape(P, W1C)
    units += [np.zeros((P, UNIT), np.float32)] * PAD_UNITS
    arrays = {
        "x_in": x.reshape(S, D), "pos_in": positions.reshape(TOKS, P).T, "stream": np.stack(units), "small_in": small,
        "w1_in": w1, "const_in": _constants(), "final_in": final_norm,
    }
    nc = _bacc.Bacc("TRN2", target_bir_lowering=False, num_devices=1)
    args = []
    for name, v in arrays.items():
        arrays[name] = v = np.ascontiguousarray(v)
        args.append(nc.dram_tensor(name, v.shape, mybir.dt.from_np(v.dtype), kind="ExternalInput").ap())
    args.append(nc.dram_tensor("out", (S, D), F32, kind="ExternalOutput").ap())
    trunk(nc, *args)
    r = _run(nc, [arrays], core_ids=[0])
    return r.results[0]["out"].reshape(1, S, D)
```

```python
import math
from contextlib import ExitStack

import numpy as np

import concourse.bass as bass
from concourse import mybir

F32 = mybir.dt.float32
F32R = mybir.dt.float32r
I32 = mybir.dt.int32
ALU = mybir.AluOpType
ACT = mybir.ActivationFunctionType
AX = mybir.AxisListType

P = 128
L, S, D, F = 2, 256, 1024, 2816
TOKS = S // P
KT = D // P
HD, HALF_ROT = 64, 8
EPS = 1e-6
NEG = -1e30
TAKEN = -3e38
THETA = 500000.0
TOPK = min(256, S // 4)
N_CMP = (S - 32) // 16 + 1
WINDOWS = (2, 4, 8, 16)

UNIT = 2048
RING = 3
CREDIT = RING
PARTS = 2
PART = UNIT // PARTS
FCH = 256
FI = F // FCH
FFN_UNITS = 3 * FI
MIX_UNITS = 33
LAYER_UNITS = 2 * FFN_UNITS + MIX_UNITS
assert FFN_UNITS % RING == 0 and MIX_UNITS % RING == 0
PAD_UNITS = RING

C_CKV, C_IK, C_IW, C_GATE = 0, 128, 192, 196
C_S = 220
C_IQ, C_KVC, C_KVS, C_KVW, C_QN, C_QD, C_U = 220, 476, 732, 988, 1244, 1756, 2268
ZC = 2780
Z_CHUNKS = 6
CHUNKS = 12

W_G1, W_GM, W_G2, W_KVG, W_PSC, W_POS = 0, 8, 16, 24, 25, 29
W_UKV, W_POOL, W_W2 = 61, 189, 701
W_SMALL = 829
W1C = 2 * 16 * P

K_ID, K_FREQ = 0, 128
KC_FIRST = K_FREQ + HALF_ROT
K_CB, K_CMPB, K_VALID, K_BAND = (KC_FIRST + o for o in (0, 256, 288, 290))
KC = K_BAND + 4 * 384

BATCHES = (
    [("sel", qt, g) for qt in range(2) for g in range(2)]
    + [("win", qt, g) for qt in range(2) for g in range(2)]
    + [("cmp", qt, 0) for qt in range(2)]
    + [("dsa", qt, g) for qt in range(2) for g in range(2)]
)
NB = len(BATCHES)
LEAD = 2


def keys_of(b):
    kind, qt, _ = BATCHES[b]
    return N_CMP if kind == "cmp" else P * (qt + 1)


def heads_of(b):
    return 8 if BATCHES[b][0] == "cmp" else 4


def turns_of(b):
    kind, qt, _ = BATCHES[b]
    if kind == "cmp":
        return [[(h, 0) for h in range(4)], [(h, 0) for h in range(4, 8)]]
    blocks = [(h, kb) for h in range(4) for kb in range(qt + 1)]
    return [blocks[i : i + 4] for i in range(0, len(blocks), 4)]


def turn_names(b):
    return [f"p{b}_{j}" for j in range(len(turns_of(b)))]


def turn_order():
    names = ["ckv", "kv", "ik", "iq", "kd", "kvc", "ksw", "qn0", "qn1", "hid", "qd0", "qd1", "cmpo"]
    names += turn_names(0)
    extra = {0: ["band0"], 1: ["band1"], 2: ["yb0"], 3: ["yb1"]}
    for k in range(12):
        names += turn_names(k + 1) + extra.get(k, [])
    names += ["yc0", "yc1"] + turn_names(13) + ["ya0", "ya1", "mg0", "mg1", "mg2", "mg3"]
    return names


TURNS = turn_order()
TURN_AT = {n: i for i, n in enumerate(TURNS)}
PER_BANK = [len(TURNS[0::2]), len(TURNS[1::2])]


def trunk(nc, x_in, pos_in, stream, small_in, w1_in, const_in, final_in, out):
    ctx = ExitStack()
    with ctx:
        def sb(name, shape, dt=F32):
            return ctx.enter_context(nc.sbuf_tensor(name, shape, dt))

        def sem(name):
            return ctx.enter_context(nc.semaphore(name))

        raw = [sb(f"raw{i}", [P, UNIT]) for i in range(RING)]
        whi = [sb(f"whi{i}", [P, UNIT], F32R) for i in range(RING)]
        wlo = [sb(f"wlo{i}", [P, UNIT], F32R) for i in range(RING)]
        x = sb("x", [P, TOKS, D])
        xhi = sb("xhi", [P, KT, S], F32R)
        xlo = sb("xlo", [P, KT, S], F32R)
        z = sb("z", [P, TOKS, ZC])
        gates = sb("gates", [P, TOKS, 3 * D])
        w1 = gates[:, :, :].rearrange("p t c -> p (t c)")[:, 0:W1C].rearrange("p (y k h) -> p y k h", y=2, k=16)
        ybhi = sb("ybhi", [P, 4, S], F32R)
        yblo = sb("yblo", [P, 4, S], F32R)
        small = sb("small", [P, W_SMALL])
        const = sb("const", [P, KC])
        ident = const[:, K_ID : K_ID + P]
        shared_q = sb("shared_q", [P, 2048])
        qnT = shared_q[:, 0:1024].rearrange("p (a t) -> p a t", a=4)
        qdT = shared_q[:, 1024:2048].rearrange("p (a t) -> p a t", a=4)
        h = shared_q[:, 0:512].rearrange("p (t c) -> p t c", t=TOKS)
        tg = shared_q[:, 512:1024].rearrange("p (t c) -> p t c", t=TOKS)
        hThi = [ybhi[:, 0:2, :], ybhi[:, 2:4, :]]
        hTlo = [yblo[:, 0:2, :], yblo[:, 2:4, :]]
        ikd = sb("ikd", [P, TOKS, 2, HD])
        kd = sb("kd", [P, TOKS, 2, HD])
        iqT = sb("iqT", [P, 2, S])
        oacc = iqT[:, :, :].rearrange("p a t -> p (a t)")
        ikT = sb("ikT", [P, S])
        kdT = sb("kdT", [P, S])
        kswT = sb("kswT", [P, 2, S])
        zkv = sb("zkv", [P, TOKS, P])
        ckvT = sb("ckvT", [P, S])
        kvcT = sb("kvcT", [P, 4, S])
        pooledT = kvcT
        sm = sb("sm", [P, 1024])
        probs = sb("probs", [P, 1024])
        pT = sb("pT", [P, 8, P])
        y = sb("y", [P, TOKS, 2, 512])
        work = sb("work", [P, TOKS, S])
        top8 = sb("top8", [P, TOKS, 8])
        trig = sb("trig", [P, 2, TOKS, 16])
        cos16, sin16 = trig[:, 0], trig[:, 1]
        rot = sb("rot", [P, 2, TOKS, 8, 16])
        stat = sb("stat", [P, 64])
        ss, ms, msh, rs, t0, t1, rs_half, rs_sq = (stat[:, 2 * i : 2 * i + 2] for i in range(8))
        sskv, kms, kmsh, rkv, kt0, kt1 = (stat[:, 16 + 2 * i : 18 + 2 * i] for i in range(6))
        unread = stat[:, 28:29]
        posf = stat[:, 30:32]
        negmax = stat[:, 32:40]
        rowmax = stat[:, 40:48]
        sums = [stat[:, 48 + 8 * i : 56 + 8 * i] for i in range(2)]
        sig = sb("sig", [P, TOKS, 24])
        fac = sb("fac", [P, 8])
        gel = oacc[:, 0:300].rearrange("p (s y n) -> p s y n", s=5, y=2)
        gbias = oacc[:, 300:302]
        kcT = sb("kcT", [P, 16])
        vc = ikd[:, 0, :, :]
        posi = sb("posi", [P, TOKS], I32)
        ang = rot[:, 0, :, :, :].rearrange("p t h d -> p (t h d)")[:, 0 : 5 * 16].rearrange("p (s t f) -> p s t f", s=5, t=TOKS)

        def bank(name):
            return ctx.enter_context(nc.psum_tensor(name, [P, 512], F32))

        G = [bank("G0"), bank("G1")]
        T = [bank("T0"), bank("T1")]
        SC = [bank("SC0"), bank("SC1")]
        O = [bank("O0"), bank("O1")]
        ACC = [[SC[0], SC[1]], [O[0], O[1]]]

        raw_in = [sem(f"raw_in{i}") for i in range(RING)]
        hi_done = sem("hi_done")
        lo_done = sem("lo_done")
        unit_used = sem("unit_used")
        x_in_sem = [sem(f"x_in_sem{i}") for i in range(TOKS)]
        first_const_in_sem = sem("first_const_in_sem")
        const_in_sem = sem("const_in_sem")
        pos_in_sem = sem("pos_in_sem")
        small_in_sem = sem("small_in_sem")
        w1_in_sem = sem("w1_in_sem")
        final_in_sem = sem("final_in_sem")
        x_up = sem("x_up")
        xt_filled = sem("xt_filled")
        xhi_done = sem("xhi_done")
        xlo_done = sem("xlo_done")
        squares_done = sem("squares_done")
        rstd_done = sem("rstd_done")
        gu_filled = sem("gu_filled")
        tanh_done = sem("tanh_done")
        h_done = sem("h_done")
        ht_filled = sem("ht_filled")
        ht_hi_done = sem("ht_hi_done")
        ht_lo_done = sem("ht_lo_done")
        acc_done = sem("acc_done")
        g_filled = sem("g_filled")
        gz_drained = sem("gz_drained")
        gp_drained = sem("gp_drained")
        t_filled = sem("t_filled")
        t_drained = [sem("t_drained0"), sem("t_drained1")]
        t_hi_done = sem("t_hi_done")
        s_filled = sem("s_filled")
        s_drained = sem("s_drained")
        index_summed = sem("index_summed")
        o_filled = sem("o_filled")
        o_drained = sem("o_drained")
        negmax_done = sem("negmax_done")
        exp_done = sem("exp_done")
        roped = sem("roped")
        kv_squares = sem("kv_squares")
        gate_tanh = sem("gate_tanh")
        shifted = sem("shifted")
        gelu_inner = sem("gelu_inner")
        gelu_tanh = sem("gelu_tanh")
        gelu_done = sem("gelu_done")
        y_done = sem("y_done")
        merged_done = sem("merged_done")
        out_ready = sem("out_ready")
        out_sent = sem("out_sent")
        dve_step = sem("dve_step")
        pool_step = sem("pool_step")

        block = ctx.enter_context(nc.Block())

        class Steps:

            def __init__(self, eng, s):
                self.eng, self.s, self.n = eng, s, 0

            def restart(self):
                self.eng.sem_clear(self.s)
                self.n = 0

            def then(self, ins):
                ins.then_inc(self.s, 1)
                self.n += 1
                self.eng.wait_ge(self.s, self.n)

        def filled(l, name):
            return l * len(TURNS) + TURN_AT[name] + 1

        def wait_drained(eng, l, *names, opening=None):
            last = [0, 0]
            for i in map(TURN_AT.get, names):
                last[i % 2] = max(last[i % 2], i // 2 + 1)
            if opening is not None:
                i = TURN_AT[opening]
                last[i % 2] = max(last[i % 2], i // 2)
            for b in range(2):
                if last[b]:
                    eng.wait_ge(t_drained[b], l * PER_BANK[b] + last[b])

        def turn_bank(name):
            return T[TURN_AT[name] % 2]

        def mark_drained(ins, name):
            ins.then_inc(t_drained[TURN_AT[name] % 2], 1)

        def ffn_base(l, occ):
            return l * LAYER_UNITS + occ * (FFN_UNITS + MIX_UNITS)

        def mix_base(l):
            return l * LAYER_UNITS + FFN_UNITS

        def unit_value(l, n):
            return l * LAYER_UNITS + n + 1 + CREDIT

        def part_value(n, part, base=0):
            return base * PARTS + (n * PARTS + part + 1 + CREDIT * PARTS)

        def wait_g(eng, l, f):
            if f % 2 == 0:
                eng.wait_ge(g_filled, l * 20 + f // 2 + 1)
            else:
                n = f - 1 if f < 24 else 23 + (f - 25) // 2 if f < 36 else 30 + (f - 37)
                eng.wait_ge(unit_used, unit_value(l, FFN_UNITS + n))

        BY_HALF = [(0, 0), (1, 0), (0, 1), (1, 1)]


        def lift_of(l, which):
            return l * 3 + which

        LIFT_GAIN = [W_G1, W_GM, W_G2]
        LIFT_NEEDS = [[1, 2, 3, 4], [1, 2, 3, 4], [1, 3, 3, 4]]
        MERGED_ORDER = BY_HALF

        @block.sync
        def _(sp):
            def load_unit(j, n):
                sp.dma_start(raw[j][:, :], stream[n, :, :].rearrange("u p n -> p (u n)")).then_inc(raw_in[j], 16)

            x_v = x_in.rearrange("(t p) d -> p t d", p=P)
            sp.dma_start(x[:, 0, :], x_v[:, 0, :]).then_inc(x_in_sem[0], 16)
            sp.dma_start(const[:, 0:KC_FIRST], const_in[:, 0:KC_FIRST]).then_inc(first_const_in_sem, 16)
            load_unit(0, slice(0, 1))
            sp.dma_start(x[:, 1, :], x_v[:, 1, :]).then_inc(x_in_sem[1], 16)
            load_unit(1, slice(1, 2))
            load_unit(2, slice(2, 3))
            sp.dma_start(const[:, KC_FIRST:KC], const_in[:, KC_FIRST:KC]).then_inc(const_in_sem, 16)
            n_units = L * LAYER_UNITS + PAD_UNITS
            with sp.Fori(1, n_units // RING) as r:
                for j in range(RING):
                    sp.wait_ge(hi_done, r * RING * PARTS + (j + 1) * PARTS)
                    sp.wait_ge(lo_done, r * RING * PARTS + (j + 1) * PARTS)
                    load_unit(j, bass.ds(r * RING + j, 1))
            sp.wait_ge(raw_in[RING - 1], n_units // RING * 16)
            sp.wait_ge(x_up, 4 * (3 * L + 1))
            sp.dma_start(z[:, 0, 0:D], final_in.partition_broadcast(P)).then_inc(final_in_sem, 16)
            out_v = out.rearrange("(t p) d -> p t d", p=P)
            for tok in range(TOKS):
                sp.wait_ge(out_ready, tok + 1)
                sp.dma_start(out_v[:, tok, :], x[:, tok, :]).then_inc(out_sent, 16)
            sp.wait_ge(out_sent, 16 * TOKS)

        @block.gpsimd
        def _(pool):
            pool.dma_start(posi[:, :], pos_in).then_inc(pos_in_sem, 16)
            steps = Steps(pool, pool_step)

            def series_term(n):
                return (-1.0) ** (n // 2) / float(math.factorial(n))

            def rope(cols, heads, last):
                v = cols.rearrange("p t (h d) -> p t h d", d=HD)
                c = cos16[:, :, :].unsqueeze(2).to_broadcast([P, TOKS, heads, 16])
                s = sin16[:, :, :].unsqueeze(2).to_broadcast([P, TOKS, heads, 16])
                a, b = rot[:, 0, :, 0:heads, :], rot[:, 1, :, 0:heads, :]
                pool.tensor_tensor(a, v[:, :, :, 0:16], c, ALU.mult)
                pool.tensor_tensor(b[:, :, :, 0:8], v[:, :, :, 8:16], s[:, :, :, 0:8], ALU.mult)
                steps.then(pool.tensor_tensor(b[:, :, :, 8:16], v[:, :, :, 0:8], s[:, :, :, 8:16], ALU.mult))
                o = pool.tensor_tensor(v[:, :, :, 0:16], a, b, ALU.add)
                if last:
                    o.then_inc(roped, 1)
                else:
                    steps.then(o)

            pool.wait_ge(pos_in_sem, 16)
            pool.wait_ge(first_const_in_sem, 16)
            then = steps.then
            a0, a1, a2, a3, sq = (ang[:, i, :, :] for i in range(5))
            then(pool.tensor_copy(posf, posi[:, :]))
            freq = const[:, K_FREQ : K_FREQ + HALF_ROT].unsqueeze(1).to_broadcast([P, TOKS, HALF_ROT])
            then(pool.tensor_tensor(a0, posf.unsqueeze(2).to_broadcast([P, TOKS, HALF_ROT]), freq, ALU.mult))
            magic = 1.5 * 2.0**23
            turns = a1
            then(pool.tensor_scalar(turns, a0, float(np.float32(1 / (2 * np.pi))), magic, ALU.mult, ALU.add))
            then(pool.tensor_scalar(turns, turns, -magic, None, ALU.add))
            then(pool.tensor_scalar(a2, turns, 1.0 / 4096, magic, ALU.mult, ALU.add))
            then(pool.tensor_scalar(a2, a2, -magic, 4096.0, ALU.add, ALU.mult))
            then(pool.tensor_tensor(a3, turns, a2, ALU.subtract))
            rest = 2 * np.pi
            for bits in (9, 21, 33, 45):
                part = np.floor(rest * 2.0**bits) / 2.0**bits
                rest -= part
                for src in (a2, a3):
                    then(pool.tensor_scalar(sq, src, -float(part), None, ALU.mult))
                    then(pool.tensor_tensor(a0, a0, sq, ALU.add))
            then(pool.tensor_scalar(a0, a0, 0.5, None, ALU.mult))
            then(pool.tensor_tensor(sq, a0, a0, ALU.mult))
            for series, start in ((a1, 1), (a2, 0)):
                n = start + 14
                then(pool.tensor_scalar(series, sq, series_term(n), series_term(n - 2), ALU.mult, ALU.add))
                for k in range(n - 4, start - 1, -2):
                    then(pool.tensor_tensor(series, series, sq, ALU.mult))
                    then(pool.tensor_scalar(series, series, series_term(k), None, ALU.add))
            then(pool.tensor_tensor(a1, a1, a0, ALU.mult))
            then(pool.tensor_tensor(a2, a2, a1, ALU.mult))
            then(pool.tensor_tensor(a3, a1, a1, ALU.mult))
            for i in range(2):
                pool.tensor_scalar(cos16[:, :, 8 * i : 8 * i + 8], a3, -2.0, 1.0, ALU.mult, ALU.add)
            pool.tensor_scalar(sin16[:, :, 0:8], a2, -2.0, None, ALU.mult)
            then(pool.tensor_scalar(sin16[:, :, 8:16], a2, 2.0, None, ALU.mult))
            with pool.Fori(0, L) as l:
                steps.restart()
                pool.wait_ge(gz_drained, l * 24 + 2)
                rope(z[:, :, C_IK : C_IK + HD], 1, False)
                src = z[:, :, C_IK : C_IK + HD].unsqueeze(2).to_broadcast([P, TOKS, 2, HD])
                pool.tensor_copy(ikd[:, :, :, :], src).then_inc(roped, 1)
                pool.wait_ge(gz_drained, l * 24 + 4)
                rope(z[:, :, C_IQ : C_IQ + 256], 4, True)
                pool.wait_ge(roped, l * 8 + 2)
                rope(z[:, :, C_KVC : C_KVC + 128], 2, True)
                wait_drained(pool, l, "kv")
                pool.wait_ge(roped, l * 8 + 3)
                rope(zkv[:, :, 0:HD], 1, False)
                src = zkv[:, :, 0:HD].unsqueeze(2).to_broadcast([P, TOKS, 2, HD])
                pool.tensor_copy(kd[:, :, :, :], src).then_inc(roped, 1)
                pool.wait_ge(gz_drained, l * 24 + 6)
                rope(z[:, :, C_KVS : C_KVS + 128], 2, True)
                pool.wait_ge(roped, l * 8 + 5)
                rope(z[:, :, C_KVW : C_KVW + 128], 2, True)
                pool.wait_ge(gz_drained, l * 24 + 8)
                pool.wait_ge(roped, l * 8 + 6)
                rope(z[:, :, C_QN : C_QN + 512], 8, True)
                pool.wait_ge(gz_drained, l * 24 + 10)
                pool.wait_ge(roped, l * 8 + 7)
                rope(z[:, :, C_QD : C_QD + 512], 8, True)
                pool.wait_ge(roped, l * 8 + 8)

        @block.scalar
        def _(act):
            def round_unit(s):
                for c in range(0, UNIT, PART):
                    act.activation(whi[s][:, c : c + PART], raw[s][:, c : c + PART], ACT.Copy).then_inc(hi_done, 1)

            def split(l, at, u):
                n = at + u
                s = n % RING
                act.wait_ge(raw_in[s], (l * (LAYER_UNITS // RING) + n // RING + 1) * 16)
                act.wait_ge(unit_used, l * LAYER_UNITS + (n + 1))
                round_unit(s)

            def split_in_loop(l, i, at, u):
                n = at + u
                s = n % RING
                act.wait_ge(raw_in[s], (l * (LAYER_UNITS // RING) + i + n // RING + 1) * 16)
                act.wait_ge(unit_used, l * LAYER_UNITS + i * RING + (n + 1))
                round_unit(s)

            def lift(l, which, tok):
                v = lift_of(l, which)
                if which == 0 and tok == 0:
                    act.wait_ge(small_in_sem, (l + 1) * 16)
                if tok:
                    square(v, tok)
                for half in range(2):
                    act.wait_ge(xt_filled, v * 4 + 2 * tok + half + 1)
                    for k in range(4):
                        g = LIFT_GAIN[which] + half * 4 + k
                        act.activation(
                            xhi[:, half * 4 + k, tok * P : (tok + 1) * P], T[half][:, k * P : (k + 1) * P],
                            ACT.Copy, scale=small[:, g : g + 1],
                        ).then_inc(xhi_done, 1)
                if tok == 0:
                    square(v, tok)

            def square(v, tok):
                if tok:
                    act.wait_ge(x_up, (v + 1) * 4)
                    act.wait_ge(squares_done, v * 2 + 1)
                act.activation(
                    probs[:, :], x[:, tok, :], ACT.Square, accum_out=ss[:, tok : tok + 1]
                ).then_inc(squares_done, 1)

            def ffn(l, occ):
                o = l * 2 + occ
                at = occ * (FFN_UNITS + MIX_UNITS)
                if occ == 0:
                    lift(l, 0, 0)
                    lift(l, 0, 1)
                    split(l, at, 2)

                def swish(g, tok, last_unit):
                    if tok:
                        act.wait_ge(unit_used, last_unit + 1 + CREDIT)
                    else:
                        act.wait_ge(gu_filled, g + 1)
                    act.activation(tg[:, tok, :], G[tok][:, 0:FCH], ACT.Tanh, scale=rs_half[:, tok : tok + 1]).then_inc(
                        tanh_done, 1
                    )

                def turn_h(n, j=0):
                    act.wait_ge(ht_filled, n)
                    act.activation(hThi[j].rearrange("p k t -> p (k t)"), T[0][:, :], ACT.Copy).then_inc(ht_hi_done, 1)

                act.wait_ge(rstd_done, lift_of(l, 2 * occ) + 1)
                if occ == 0:
                    act.wait_ge(merged_done, l * 4 + 1)
                    act.dma_start(
                        gates[:, :, :].rearrange("p t c -> p (t c)")[:, 0:W1C],
                        w1_in[bass.ds(l, 1), :, :].rearrange("l p n -> p (l n)"),
                    ).then_inc(w1_in_sem, 16)
                else:
                    act.dma_start(
                        small[:, :], small_in[bass.ds(l + 1, 1), :, :].rearrange("l p n -> p (l n)")
                    ).then_inc(small_in_sem, 16)
                swish(o * FI, 0, None)
                split(l, at, 3)
                swish(o * FI, 1, l * LAYER_UNITS + (at + 1))
                split(l, at, 4)
                with act.Fori(1, FI - 1) as i:
                    g = o * FI + i
                    swish(g, 0, None)
                    turn_h(g)
                    split_in_loop(l, i, at, 2)
                    swish(g, 1, l * LAYER_UNITS + i * RING + at)
                    split_in_loop(l, i, at, 3)
                    split_in_loop(l, i, at, 4)
                last = FI - 1
                swish(o * FI + last, 0, None)
                turn_h(o * FI + last)
                split(l, at, 3 * last + 2)
                swish(o * FI + last, 1, l * LAYER_UNITS + last * RING + at)
                split(l, at, 3 * last + 3)
                turn_h(o * FI + FI, 1)
                split(l, at, 3 * last + 4)
                if occ == 0:
                    lift(l, 1, 0)
                    lift(l, 1, 1)
                    split(l, FFN_UNITS, 2)

            def mixer(l):
                at = FFN_UNITS
                act.wait_ge(rstd_done, lift_of(l, 1) + 1)

                def drain_z(c, tok):
                    wait_g(act, l, 2 * c + tok)
                    lo, hi = (0, C_S) if c == 0 else (C_S + (c - 1) * 512, C_S + c * 512)
                    act.activation(
                        z[:, tok, lo:hi], G[tok][:, 0 : hi - lo], ACT.Copy, scale=rs[:, tok : tok + 1]
                    ).then_inc(gz_drained, 1)

                def drain_gate(c, tok):
                    wait_g(act, l, 2 * c + tok)
                    o = (c - Z_CHUNKS) * 512
                    act.activation(
                        gates[:, tok, o : o + 512], G[tok][:, :], ACT.Tanh, scale=rs_half[:, tok : tok + 1]
                    ).then_inc(gz_drained, 1)

                def drain(name, dst, src, **kw):
                    act.wait_ge(t_filled, filled(l, name))
                    mark_drained(act.activation(dst, src, kw.pop("func", ACT.Copy), **kw), name)

                def relu(qt):
                    n = P * (qt + 1)
                    act.wait_ge(s_filled, l * (NB + 2) + qt + 1)
                    if qt:
                        act.wait_ge(index_summed, l * 2 + 1)
                    rl = sm[:, 0 : 4 * n].rearrange("p (a b n) -> p a b n", a=2, b=2)
                    for half in range(2):
                        ins = act.activation(
                            rl[:, :, half, :], SC[half][:, 0 : 2 * n].rearrange("p (a n) -> p a n", a=2),
                            ACT.Relu, scale=1.0 / 16,
                        )
                    ins.then_inc(s_drained, 1)

                def exps(b):
                    n, nh = keys_of(b), heads_of(b)
                    w = 16 if n == N_CMP else n
                    act.wait_ge(negmax_done, l * NB + b + 1)
                    if b:
                        act.wait_ge(t_filled, filled(l, turn_names(b - 1)[-1]))
                    for hh in range(nh):
                        ins = act.activation(
                            probs[:, hh * w : hh * w + n], sm[:, hh * w : hh * w + n], ACT.Exp,
                            scale=0.125, bias=negmax[:, hh : hh + 1], accum_out=sums[b % 2][:, hh : hh + 1],
                        )
                    ins.then_inc(exp_done, 1)

                def drain_probs(b):
                    if b:
                        act.wait_ge(o_filled, l * NB + b)
                    rows = N_CMP if BATCHES[b][0] == "cmp" else P
                    for j, name in enumerate(turn_names(b)):
                        n = len(turns_of(b)[j])
                        drain(
                            name, pT[0:rows, 4 * j : 4 * j + n, :].rearrange("p b q -> p (b q)"),
                            turn_bank(name)[0:rows, 0 : n * P],
                        )

                def split_y(name, dst, ks):
                    tok = int(name[-1]) if name[:2] in ("yc", "ya") else MERGED_ORDER[int(name[-1])][0]
                    act.wait_ge(t_filled, filled(l, name))
                    act.activation(
                        dst[:, ks : ks + 4, tok * P : (tok + 1) * P],
                        turn_bank(name)[:, :].rearrange("p (k t) -> p k t", k=4), ACT.Copy,
                    ).then_inc(t_hi_done, 1)

                drain_z(0, 0)
                drain_z(0, 1)
                act.wait_ge(gz_drained, l * 24 + 2)
                for tok in range(TOKS):
                    if tok:
                        act.wait_ge(kv_squares, l * 2 + 1)
                    act.activation(
                        probs[:, 0:P], z[:, tok, C_CKV : C_CKV + P], ACT.Square, accum_out=sskv[:, tok : tok + 1]
                    ).then_inc(kv_squares, 1)
                act.activation(sig[:, :, :], z[:, :, C_GATE : C_GATE + 24], ACT.Tanh, scale=0.5).then_inc(gate_tanh, 1)
                split(l, at, 3)
                drain_z(1, 0)
                drain("ckv", ckvT[:, :], turn_bank("ckv")[:, 0:S], scale=small[:, W_KVG : W_KVG + 1])
                drain_z(1, 1)
                split(l, at, 4)
                split(l, at, 5)
                drain_z(2, 0)
                drain("ik", ikT[:, :], turn_bank("ik")[:, 0:S])
                drain("iq", iqT[:, :, :].rearrange("p a t -> p (a t)"), turn_bank("iq")[:, :])
                split(l, at, 6)
                drain_z(2, 1)
                drain("kd", kdT[:, :], turn_bank("kd")[:, 0:S])
                relu(0)
                split(l, at, 7)
                drain_z(3, 0)
                kvc = turn_bank("kvc")[:, :].rearrange("p (y t) -> p y t", y=2)
                act.wait_ge(t_filled, filled(l, "kvc"))
                act.activation(kvcT[0:HD, 0:4:2, :], kvc[0:HD], ACT.Copy)
                drain("kvc", kvcT[0:HD, 1:4:2, :], kvc[HD:P])
                wait_drained(act, l, "kvc")
                act.dma_start(kvcT[HD:P, :, 0 : S - 1], kvcT[0:HD, :, 1:S]).then_inc(shifted, 16)
                relu(1)
                split(l, at, 8)
                drain_z(3, 1)
                drain("ksw", kswT[:, :, :].rearrange("p a t -> p (a t)"), turn_bank("ksw")[:, :])
                split(l, at, 9)
                drain_z(4, 0)
                for j in range(2):
                    drain(
                        f"qn{j}", qnT[:, 2 * j : 2 * j + 2, :].rearrange("p a t -> p (a t)"),
                        turn_bank(f"qn{j}")[:, :],
                    )
                split(l, at, 10)
                drain_z(4, 1)
                act.wait_ge(gelu_inner, l + 1)
                act.activation(gel[:, 3, :, :], gel[:, 2, :, :], ACT.Tanh, scale=0.7978845608028654).then_inc(
                    gelu_tanh, 1
                )
                split(l, at, 11)
                drain_z(5, 0)
                for j in range(2):
                    drain(
                        f"qd{j}", qdT[:, 2 * j : 2 * j + 2, :].rearrange("p a t -> p (a t)"),
                        turn_bank(f"qd{j}")[:, :],
                    )
                exps(0)
                split(l, at, 12)
                drain_z(5, 1)
                act.wait_ge(t_filled, filled(l, "cmpo"))
                act.activation(kcT[:, 0:N_CMP], turn_bank("cmpo")[:, 0:N_CMP], ACT.Copy, scale=0.5)
                drain(
                    "cmpo", vc[0:N_CMP, :, :].rearrange("p g d -> p (g d)"), turn_bank("cmpo")[0:N_CMP, 64:192],
                    scale=0.5,
                )
                drain_probs(0)
                exps(1)
                split(l, at, 13)
                for k in range(12):
                    c, tok = Z_CHUNKS + k // 2, k % 2
                    if tok:
                        split(l, at, 2 * c + 2)
                    drain_gate(c, tok)
                    drain_probs(k + 1)
                    if k + LEAD < NB:
                        exps(k + LEAD)
                    if k < 2:
                        drain(
                            f"band{k}", pooledT[:, 2 * k : 2 * k + 2, :].rearrange("p g t -> p (g t)"),
                            turn_bank(f"band{k}")[:, :],
                        )
                    elif k < 4:
                        name = f"yb{k - 2}"
                        act.wait_ge(t_filled, filled(l, name))
                        for g in range(2):
                            gg = 2 * (k - 2) + g
                            ins = act.activation(
                                ybhi[:, gg, :], turn_bank(name)[:, g * S : (g + 1) * S], ACT.Copy,
                                scale=small[:, W_PSC + gg : W_PSC + gg + 1],
                            )
                        ins.then_inc(t_hi_done, 1)
                    if tok:
                        split(l, at, 2 * c + 3)
                for j in range(2):
                    split_y(f"yc{j}", xhi, 0)
                split(l, at, 26)
                drain_probs(13)
                split(l, at, 27)
                split(l, at, 28)
                split(l, at, 29)
                for j in range(2):
                    split_y(f"ya{j}", xhi, 4)
                split(l, at, 30)
                split(l, at, 31)
                for j, (tok, half) in enumerate(MERGED_ORDER):
                    split_y(f"mg{j}", xhi, 4 * half)
                for u in range(32, 34):
                    split(l, at, u)
                lift(l, 2, 0)
                split(l, at, 34)
                lift(l, 2, 1)
                split(l, at, 35)

            act.dma_start(small[:, :], small_in[0, :, :]).then_inc(small_in_sem, 16)
            act.nop().then_inc(hi_done, CREDIT * PARTS)
            for u in range(2):
                act.wait_ge(raw_in[u], 16)
                act.wait_ge(unit_used, u + 1)
                round_unit(u)
            with act.Fori(0, L) as l:
                ffn(l, 0)
                mixer(l)
                ffn(l, 1)
            for tok in range(TOKS):
                act.wait_ge(x_up, 12 * L + 2 * tok + 2)
                square(3 * L, tok)
            act.wait_ge(small_in_sem, (L + 1) * 16)

        @block.vector
        def _(dve):
            steps = Steps(dve, dve_step)

            def split(l, at, u):
                n = at + u
                for part in range(PARTS):
                    dve.wait_ge(hi_done, part_value(n, part, l * LAYER_UNITS))
                    subtract_hi(n % RING, part)

            def split_in_loop(l, i, at, u):
                n = at + u
                for part in range(PARTS):
                    dve.wait_ge(hi_done, part_value(n, part, l * LAYER_UNITS + i * RING))
                    subtract_hi(n % RING, part)

            def subtract_hi(s, part):
                c = slice(part * PART, (part + 1) * PART)
                dve.tensor_tensor(
                    wlo[s][:, c], raw[s][:, c], whi[s][:, c].bitcast(F32), ALU.subtract
                ).then_inc(lo_done, 1)

            def rsqrt(sumsq, m, mh, r, a, b, n):
                then = steps.then
                then(dve.tensor_scalar(m, sumsq, 1.0 / n, EPS, ALU.mult, ALU.add))
                dve.tensor_scalar(r.bitcast(I32), m.bitcast(I32), -0.5, float(0x5F3759DF), ALU.mult, ALU.add)
                then(dve.tensor_scalar(mh, m, -0.5, None, ALU.mult))
                for _ in range(3):
                    then(dve.tensor_tensor(a, r, r, ALU.mult))
                    then(dve.tensor_tensor(b, a, mh, ALU.mult))
                    then(dve.scalar_tensor_tensor(r, b, 1.5, r, ALU.add, ALU.mult))

            def lift(l, which, tok):
                v = lift_of(l, which)
                if which == 0 and tok == 0:
                    dve.wait_ge(small_in_sem, (l + 1) * 16)
                for half in range(2):
                    dve.wait_ge(xhi_done, v * 16 + tok * 8 + half * 4 + 4)
                    for k in range(4):
                        kt, sl = half * 4 + k, slice(tok * P, (tok + 1) * P)
                        g = LIFT_GAIN[which] + kt
                        dve.scalar_tensor_tensor(
                            xlo[:, kt, sl], T[half][:, k * P : (k + 1) * P], small[:, g : g + 1],
                            xhi[:, kt, sl].bitcast(F32), ALU.mult, ALU.subtract,
                        ).then_inc(xlo_done, 1)
                if tok:
                    steps.restart()
                    root_mean_square(v * 2 + 2)
                    dve.tensor_scalar(rs_half, rs, 0.5, None, ALU.mult)
                    dve.tensor_tensor(rs_sq, rs, rs, ALU.mult).then_inc(rstd_done, 1)

            def root_mean_square(count):
                dve.wait_ge(squares_done, count)
                rsqrt(ss, ms, msh, rs, t0, t1, D)

            def ffn(l, occ):
                o = l * 2 + occ
                at = occ * (FFN_UNITS + MIX_UNITS)
                if occ == 0:
                    lift(l, 0, 0)
                    lift(l, 0, 1)
                    split(l, at, 2)

                def swiglu(g, tok, chain):
                    dve.wait_ge(tanh_done, g * 2 + tok + 1)
                    chain(dve.scalar_tensor_tensor(h[:, tok, :], tg[:, tok, :], 1.0, G[tok][:, 0:FCH], ALU.add, ALU.mult))
                    dve.scalar_tensor_tensor(
                        h[:, tok, :], h[:, tok, :], rs_sq[:, tok : tok + 1], G[tok][:, FCH : 2 * FCH], ALU.mult, ALU.mult
                    ).then_inc(h_done, 1)

                def turn_h(n, j=0):
                    dve.wait_ge(ht_hi_done, n)
                    dve.tensor_tensor(
                        hTlo[j].rearrange("p k t -> p (k t)"), T[0][:, :],
                        hThi[j].rearrange("p k t -> p (k t)").bitcast(F32), ALU.subtract,
                    ).then_inc(ht_lo_done, 1)

                def x_update(tok):
                    if tok:
                        dve.wait_ge(unit_used, unit_value(l, at + FFN_UNITS - 1))
                    else:
                        dve.wait_ge(acc_done, o + 1)
                    for half in range(2):
                        sl = slice(half * 512, half * 512 + 512)
                        dve.scalar_tensor_tensor(
                            x[:, tok, sl], ACC[tok][half][:, :], 0.25, x[:, tok, sl], ALU.mult, ALU.add
                        ).then_inc(x_up, 1)

                steps.restart()
                dve.wait_ge(rstd_done, lift_of(l, 2 * occ) + 1)
                swiglu(o * FI, 0, steps.then)
                split(l, at, 3)
                swiglu(o * FI, 1, steps.then)
                split(l, at, 4)
                with dve.Fori(1, FI - 1) as i:
                    steps.restart()
                    g = o * FI + i
                    dve.wait_ge(ht_filled, g)
                    swiglu(g, 0, steps.then)
                    turn_h(g)
                    split_in_loop(l, i, at, 2)
                    swiglu(g, 1, steps.then)
                    split_in_loop(l, i, at, 3)
                    split_in_loop(l, i, at, 4)
                last = FI - 1
                steps.restart()
                dve.wait_ge(ht_filled, o * FI + last)
                swiglu(o * FI + last, 0, steps.then)
                turn_h(o * FI + last)
                split(l, at, 3 * last + 2)
                swiglu(o * FI + last, 1, steps.then)
                split(l, at, 3 * last + 3)
                turn_h(o * FI + FI, 1)
                split(l, at, 3 * last + 4)
                for tok in range(TOKS):
                    x_update(tok)
                    if occ == 0:
                        lift(l, 1, tok)
                if occ == 0:
                    split(l, FFN_UNITS, 2)

            def mixer(l):
                at = FFN_UNITS
                then = steps.then

                def index_scores(qt):
                    n = P * (qt + 1)
                    dve.wait_ge(s_drained, l * (NB + 2) + qt + 1)
                    w = work[:, qt, 0:n]
                    for hh in range(4):
                        r = sm[:, hh * n : (hh + 1) * n]
                        iw = z[:, qt, C_IW + hh : C_IW + hh + 1]
                        if hh == 0:
                            then(dve.tensor_scalar(w, r, iw, None, ALU.mult))
                        else:
                            ins = dve.scalar_tensor_tensor(w, r, iw, w, ALU.mult, ALU.add)
                            if hh == 3:
                                ins.then_inc(index_summed, 1)
                                dve.wait_ge(index_summed, l * 2 + qt + 1)
                            else:
                                then(ins)
                    then(dve.tensor_tensor(w, w, const[:, K_CB + S - n : K_CB + S], ALU.add))

                def topk_round():
                    for qt in range(2):
                        ins = dve.max(top8[:, qt, :], work[:, qt, 0 : P * (qt + 1)])
                    then(ins)
                    for qt in range(2):
                        w = work[:, qt, 0 : P * (qt + 1)]
                        ins = dve.match_replace(w, top8[:, qt, :], w, TAKEN)
                    then(ins)

                def selection_bias():
                    for qt in range(2):
                        w = work[:, qt, 0 : P * (qt + 1)]
                        ins = dve.tensor_scalar(w, w, 0.5 * TAKEN, NEG, ALU.is_ge, ALU.mult)
                    then(ins)
                    for qt in range(2):
                        n = P * (qt + 1)
                        w = work[:, qt, 0:n]
                        ins = dve.tensor_tensor(w, w, const[:, K_CB + S - n : K_CB + S], ALU.min)
                    then(ins)

                def mask_and_max(b):
                    kind, qt, _ = BATCHES[b]
                    n, nh = keys_of(b), heads_of(b)
                    w = 16 if kind == "cmp" else n
                    if kind == "cmp":
                        bias = const[:, K_CMPB + 16 * qt : K_CMPB + 16 * qt + n]
                    elif kind == "dsa":
                        bias = work[:, qt, 0:n]
                    else:
                        bias = const[:, K_CB + S - n : K_CB + S]
                    dve.wait_ge(s_filled, l * (NB + 2) + b + 3)
                    if b:
                        dve.wait_ge(exp_done, l * NB + b)
                    dve.memset(unread, 0.0)
                    for hh in range(nh):
                        ins = dve.tensor_tensor_reduce(
                            sm[:, hh * w : hh * w + n], SC[hh % 2][:, (hh // 2) * n : (hh // 2 + 1) * n], bias,
                            1.0, -3.4e38, ALU.add, ALU.max, rowmax[:, hh : hh + 1],
                        )
                    ins.then_inc(s_drained, 1)
                    dve.wait_ge(s_drained, l * (NB + 2) + b + 3)
                    dve.tensor_scalar(negmax[:, 0:nh], rowmax[:, 0:nh], -0.125, None, ALU.mult).then_inc(negmax_done, 1)

                def drain_o(b):
                    kind, qt, g = BATCHES[b]
                    nh = heads_of(b)
                    f = fac[:, 0:nh]
                    dve.wait_ge(exp_done, l * NB + b + 1)
                    then(dve.reciprocal(f, sums[b % 2][:, 0:nh]))
                    if kind != "dsa":
                        j = ("cmp", "sel", "win").index(kind)
                        gate = sig[:, qt, 8 * j + 4 * g : 8 * j + 4 * g + nh]
                        if kind == "cmp":
                            then(dve.scalar_tensor_tensor(
                                f, f, const[:, K_VALID + qt : K_VALID + qt + 1], gate, ALU.mult, ALU.mult))
                        else:
                            then(dve.tensor_tensor(f, f, gate, ALU.mult))
                    dve.wait_ge(o_filled, l * NB + b + 1)
                    src = O[b % 2][:, 0 : nh * HD].rearrange("p (h d) -> p h d", d=HD)
                    fb = f.unsqueeze(2).to_broadcast([P, nh, HD])
                    branch = 0 if kind == "dsa" else 1
                    dst = y[:, qt, branch, 256 * g : 256 * g + nh * HD].rearrange("p (h d) -> p h d", d=HD)
                    if kind in ("dsa", "sel"):
                        dve.tensor_tensor(dst, src, fb, ALU.mult).then_inc(o_drained, 1)
                    else:
                        tmp = oacc[:, 0 : nh * HD].rearrange("p (h d) -> p h d", d=HD)
                        dve.tensor_tensor(tmp, src, fb, ALU.mult).then_inc(o_drained, 1)
                        dve.wait_ge(o_drained, l * NB + b + 1)
                        ins = dve.tensor_tensor(dst, dst, tmp, ALU.add)
                        if kind == "cmp":
                            ins.then_inc(y_done, 1)
                        else:
                            then(ins)

                def split_y(name, n_hi, dst_hi, dst_lo, ks):
                    tok = int(name[-1]) if name[:2] in ("yc", "ya") else MERGED_ORDER[int(name[-1])][0]
                    dve.wait_ge(t_hi_done, l * 10 + n_hi)
                    sl = slice(tok * P, (tok + 1) * P)
                    mark_drained(dve.tensor_tensor(
                        dst_lo[:, ks : ks + 4, sl], turn_bank(name)[:, :].rearrange("p (k t) -> p k t", k=4),
                        dst_hi[:, ks : ks + 4, sl].bitcast(F32), ALU.subtract), name)

                def gated(b_, branch, half, tok):
                    f = 24 + 4 * b_ + 2 * half + tok
                    wait_g(dve, l, f)
                    if b_ == 0 and half == 0:
                        dve.wait_ge(gz_drained, l * 24 + 24)
                    own = gates[:, tok, branch * D + half * 512 : branch * D + half * 512 + 512]
                    total = gates[:, tok, D + half * 512 : D + half * 512 + 512]
                    dve.scalar_tensor_tensor(own, own, 1.0, G[tok][:, :], ALU.add, ALU.mult).then_inc(gp_drained, 1)
                    dve.wait_ge(gp_drained, l * 12 + f - 24 + 1)
                    if b_:
                        ins = dve.tensor_tensor(total, total, own, ALU.add)
                        if b_ == 2:
                            ins.then_inc(merged_done, 1)
                        else:
                            then(ins)

                split(l, at, 3)
                dve.wait_ge(gate_tanh, l + 1)
                then(dve.tensor_scalar(sig[:, :, :], sig[:, :, :], 0.5, 0.5, ALU.mult, ALU.add))
                dve.wait_ge(kv_squares, l * 2 + 2)
                rsqrt(sskv, kms, kmsh, rkv, kt0, kt1, P)
                split(l, at, 4)
                dve.wait_ge(t_filled, filled(l, "kv"))
                for tok in range(TOKS):
                    ins = dve.tensor_scalar(
                        zkv[:, tok, :], turn_bank("kv")[:, tok * P : (tok + 1) * P], rkv[:, tok : tok + 1], None, ALU.mult
                    )
                mark_drained(ins, "kv")
                split(l, at, 5)
                split(l, at, 6)
                index_scores(0)
                split(l, at, 7)
                index_scores(1)
                split(l, at, 8)
                split(l, at, 9)
                split(l, at, 10)
                dve.wait_ge(t_filled, filled(l, "hid"))
                hid = turn_bank("hid")
                then(dve.tensor_copy(gbias[:, :], hid[:, 64:66]))
                for y_ in range(2):
                    ins = dve.tensor_scalar(
                        gel[:, 0, y_, :], hid[:, 32 * y_ : 32 * y_ + 30], gbias[:, y_ : y_ + 1], None, ALU.add)
                mark_drained(ins, "hid")
                i = TURN_AT["hid"]
                dve.wait_ge(t_drained[i % 2], l * PER_BANK[i % 2] + i // 2 + 1)
                then(dve.tensor_tensor(gel[:, 1, :, :], gel[:, 0, :, :], gel[:, 0, :, :], ALU.mult))
                then(dve.tensor_scalar(gel[:, 1, :, :], gel[:, 1, :, :], 0.044715, 1.0, ALU.mult, ALU.add))
                dve.tensor_tensor(gel[:, 2, :, :], gel[:, 1, :, :], gel[:, 0, :, :], ALU.mult).then_inc(gelu_inner, 1)
                split(l, at, 11)
                dve.wait_ge(gelu_tanh, l + 1)
                dve.scalar_tensor_tensor(
                    gel[:, 4, :, :], gel[:, 3, :, :], 1.0, gel[:, 0, :, :], ALU.add, ALU.mult).then_inc(gelu_done, 1)
                mask_and_max(0)
                split(l, at, 12)
                mask_and_max(1)
                split(l, at, 13)
                for k in range(12):
                    c, tok = Z_CHUNKS + k // 2, k % 2
                    if tok:
                        split(l, at, 2 * c + 2)
                    drain_o(k)
                    if k == 8:
                        selection_bias()
                    if k + LEAD < NB:
                        mask_and_max(k + LEAD)
                    if k < 8:
                        topk_round()
                    if 2 <= k < 4:
                        name = f"yb{k - 2}"
                        dve.wait_ge(t_hi_done, l * 10 + k - 1)
                        for g in range(2):
                            gg = 2 * (k - 2) + g
                            ins = dve.scalar_tensor_tensor(
                                yblo[:, gg, :], turn_bank(name)[:, g * S : (g + 1) * S],
                                small[:, W_PSC + gg : W_PSC + gg + 1], ybhi[:, gg, :].bitcast(F32),
                                ALU.mult, ALU.subtract)
                        mark_drained(ins, name)
                    if tok:
                        split(l, at, 2 * c + 3)
                for j in range(2):
                    split_y(f"yc{j}", 3 + j, xhi, xlo, 0)
                gated(0, 1, 0, 0)
                gated(0, 1, 0, 1)
                split(l, at, 26)
                drain_o(12)
                gated(0, 1, 1, 0)
                gated(0, 1, 1, 1)
                split(l, at, 27)
                drain_o(13)
                for half in range(2):
                    for tok in range(TOKS):
                        gated(1, 2, half, tok)
                    split(l, at, 28 + half)
                for j in range(2):
                    split_y(f"ya{j}", 5 + j, xhi, xlo, 4)
                for half in range(2):
                    for tok in range(TOKS):
                        gated(2, 0, half, tok)
                    split(l, at, 30 + half)
                for j, (tok, half) in enumerate(MERGED_ORDER):
                    split_y(f"mg{j}", 7 + j, xhi, xlo, 4 * half)

                def x_update(half, tok):
                    sl = slice(half * 512, half * 512 + 512)
                    wait_g(dve, l, 36 + 2 * half + tok)
                    dve.scalar_tensor_tensor(
                        x[:, tok, sl], G[tok][:, :], 0.5, x[:, tok, sl], ALU.mult, ALU.add
                    ).then_inc(x_up, 1)

                split(l, at, 32)
                x_update(0, 0)
                x_update(0, 1)
                split(l, at, 33)
                x_update(1, 0)
                lift(l, 2, 0)
                split(l, at, 34)
                x_update(1, 1)
                lift(l, 2, 1)
                split(l, at, 35)

            dve.nop().then_inc(lo_done, CREDIT * PARTS)
            dve.nop().then_inc(merged_done, 1)
            for tok in range(TOKS):
                dve.wait_ge(x_in_sem[tok], 16)
                dve.nop().then_inc(x_up, 2)
                for part in range(PARTS):
                    dve.wait_ge(hi_done, part_value(tok, part))
                    subtract_hi(tok, part)
            dve.wait_ge(const_in_sem, 16)
            with dve.Fori(0, L) as l:
                steps.restart()
                ffn(l, 0)
                mixer(l)
                ffn(l, 1)
            root_mean_square(6 * L + 2)
            dve.wait_ge(final_in_sem, 16)
            for tok in range(TOKS):
                dve.scalar_tensor_tensor(
                    x[:, tok, :], x[:, tok, :], rs[:, tok : tok + 1], z[:, 0, 0:D], ALU.mult, ALU.mult
                ).then_inc(out_ready, 1)

        @block.tensor
        def _(pe):
            def mm3(o, ahi, alo, bhi, blo, first, last):
                pe.matmul(o, ahi, bhi, start=first, stop=False)
                pe.matmul(o, ahi, blo, start=False, stop=False)
                return pe.matmul(o, alo, bhi, start=False, stop=last)

            def wait_part(l, n, part):
                pe.wait_ge(lo_done, part_value(n, part, l * LAYER_UNITS))

            def lift(l, which, tok, half):
                v, j = lift_of(l, which), 2 * tok + half
                pe.wait_ge(x_up, v * 4 + LIFT_NEEDS[which][j])
                if tok:
                    pe.wait_ge(xlo_done, v * 16 + 4 * (j - 1))
                for k in range(4):
                    c = half * 512 + k * P
                    ins = pe.transpose(T[half][:, k * P : (k + 1) * P], x[:, tok, c : c + P], ident)
                ins.then_inc(xt_filled, 1)

            def wait_lifted(l, which, tok, kt):
                pe.wait_ge(xlo_done, lift_of(l, which) * 16 + tok * 8 + kt + 1)

            def gemm_half(o, tok, hi, lo, k0, s, n, first, last, unit=None, before=None):
                for k in range(4):
                    if unit and k % 2 == 0:
                        unit(k // 2)
                    if before:
                        before(k0 + k)
                    sl = slice(tok * P, (tok + 1) * P)
                    ins = mm3(
                        o[:, 0:n], hi[:, k0 + k, sl], lo[:, k0 + k, sl], whi[s][:, k * n : (k + 1) * n],
                        wlo[s][:, k * n : (k + 1) * n], first and k == 0, last and k == 3,
                    )
                return ins

            def ffn(l, occ):
                o = l * 2 + occ
                at = occ * (FFN_UNITS + MIX_UNITS)
                which = 2 * occ
                if occ == 0:
                    lift(l, 0, 0, 0)
                    lift(l, 0, 0, 1)

                def gate_up(i, tok, peeled=False):
                    slot = at if peeled else at - 1
                    base = l * LAYER_UNITS + (0 if peeled else i * RING)
                    if not peeled:
                        pe.wait_ge(h_done, (o * FI + i) * 2 + tok - 1)
                    for a in range(2):
                        if peeled and tok == 0 and a:
                            lift(l, which, 1, 0)
                            lift(l, which, 1, 1)

                        def unit(part):
                            pe.wait_ge(lo_done, part_value(slot + a, part, base))

                        def lifted(kt):
                            wait_lifted(l, which, tok, kt)

                        ins = gemm_half(
                            G[tok], tok, xhi, xlo, 4 * a, (slot + a) % RING, 512, a == 0, a == 1,
                            unit=None if tok else unit, before=lifted if peeled else None)
                        if tok and a == 0:
                            ins.then_inc(unit_used, 1)
                    ins.then_inc(unit_used if tok else gu_filled, 1)

                def turn_h(n):
                    pe.wait_ge(h_done, n * 2)
                    for k in range(2):
                        for tok in range(TOKS):
                            ins = pe.transpose(
                                T[0][:, k * S + tok * P : k * S + (tok + 1) * P], h[:, tok, k * P : (k + 1) * P], ident)
                    ins.then_inc(ht_filled, 1)

                def down(n, base, u, first=False, between=None, turn=None):
                    s, j = u % RING, 1 if between else 0
                    pe.wait_ge(ht_lo_done, n)
                    for tok in range(TOKS):
                        sl = slice(tok * P, (tok + 1) * P)
                        for half in range(2):
                            if between:
                                between(tok, half)
                            if turn is not None and tok and half == 0:
                                turn_h(turn)
                            for k in range(2):
                                if tok == 0 and half == 0:
                                    pe.wait_ge(lo_done, part_value(u, k, base))
                                c = k * D + half * 512
                                ins = mm3(
                                    ACC[tok][half][:, :], hThi[j][:, k, sl], hTlo[j][:, k, sl], whi[s][:, c : c + 512],
                                    wlo[s][:, c : c + 512], first and k == 0, between is not None and k == 1,
                                )
                        if tok:
                            ins.then_inc(unit_used, 1)
                        elif between:
                            ins.then_inc(acc_done, 1)

                def lift_between(tok, half):
                    if occ == 0 and tok and half:
                        lift(l, 1, 0, 0)
                        lift(l, 1, 0, 1)

                gate_up(0, 0, peeled=True)
                gate_up(0, 1, peeled=True)
                gate_up(1, 0)
                turn_h(o * FI + 1)
                gate_up(1, 1)
                down(o * FI + 1, l * LAYER_UNITS, at + 4, first=True)
                with pe.Fori(2, FI - 1) as i:
                    gate_up(i, 0)
                    turn_h(o * FI + i)
                    gate_up(i, 1)
                    down(o * FI + i, l * LAYER_UNITS + i * RING, at + 1)
                last = FI - 1
                gate_up(last, 0)
                turn_h(o * FI + last)
                gate_up(last, 1)
                down(o * FI + last, l * LAYER_UNITS, at + 3 * last + 1, turn=o * FI + FI)
                down(o * FI + FI, l * LAYER_UNITS, at + 3 * last + 2, between=lift_between)

            def mixer(l):
                at = FFN_UNITS

                def chunk(c, tok):
                    f = 2 * c + tok
                    if f >= 2:
                        pe.wait_ge(gz_drained, l * 24 + f - 1)
                    if c == 0:
                        if tok == 0:
                            wait_part(l, at, PARTS - 1)
                        s, n = at % RING, C_S
                        for kt in range(KT):
                            wait_lifted(l, 1, tok, kt)
                            sl = slice(tok * P, (tok + 1) * P)
                            w = slice(kt * n, (kt + 1) * n)
                            ins = mm3(
                                G[tok][:, 0:n], xhi[:, kt, sl], xlo[:, kt, sl], whi[s][:, w], wlo[s][:, w],
                                kt == 0, kt == KT - 1)
                    else:
                        for a in range(2):
                            u = 2 * c - 1 + a
                            ins = unit_gemm(u, xhi, xlo, 4 * a, tok, a == 0, a == 1)
                            if tok and a == 0:
                                ins.then_inc(unit_used, 1)
                    ins.then_inc(unit_used if tok else g_filled, 1)

                def unit_gemm(u, hi, lo, k0, tok, first, last):
                    def unit(part):
                        wait_part(l, at + u, part)

                    return gemm_half(
                        G[tok], tok, hi, lo, k0, (at + u) % RING, 512, first, last, unit=None if tok else unit)

                def open_turn(name, *needs):
                    wait_drained(pe, l, *needs, opening=name)
                    return turn_bank(name)

                def turn(name, tiles, rows=P):
                    t = open_turn(name)
                    for n, src in enumerate(tiles):
                        ins = pe.transpose(t[0:rows, n * P : (n + 1) * P], src, ident)
                    ins.then_inc(t_filled, 1)

                def scores(si, qT, kT_, pairs, qt, n):
                    if si:
                        pe.wait_ge(s_drained, l * (NB + 2) + si)
                    for j, pr in enumerate(pairs):
                        for half in range(2):
                            rows = slice(half * HD, (half + 1) * HD)
                            ins = pe.matmul(
                                SC[half][:, j * n : (j + 1) * n], qT[rows, pr, qt * P : (qt + 1) * P], kT_[rows, 0:n],
                                start=True, stop=True)
                    ins.then_inc(s_filled, 1)

                def batch_scores(b):
                    kind, qt, g = BATCHES[b]
                    if b == 0:
                        wait_drained(pe, l, "qn0", "qn1", "ksw")
                    if kind == "cmp" and qt == 0:
                        wait_drained(pe, l, "cmpo")
                    if kind == "dsa" and qt == 0 and g == 0:
                        wait_drained(pe, l, "qd0", "qd1", "kd")
                    qT = qdT if kind == "dsa" else qnT
                    keys = {"sel": kswT[:, 0, :], "win": kswT[:, 1, :], "cmp": kcT, "dsa": kdT}[kind]
                    pairs = range(4) if kind == "cmp" else range(2 * g, 2 * g + 2)
                    scores(b + 2, qT, keys, pairs, qt, keys_of(b))

                def batch_turn(b):
                    n = keys_of(b)
                    w = 16 if n == N_CMP else n
                    bw = min(n, P)
                    pe.wait_ge(exp_done, l * NB + b + 1)
                    for j, name in enumerate(turn_names(b)):
                        turn(
                            name, [probs[:, hh * w + kb * P : hh * w + kb * P + bw] for hh, kb in turns_of(b)[j]],
                            rows=bw)

                def batch_values(b):
                    kind, qt, g = BATCHES[b]
                    if b >= 2:
                        pe.wait_ge(o_drained, l * NB + b - 1)
                    wait_drained(pe, l, *turn_names(b))
                    for j, name in enumerate(turn_names(b)):
                        for n, (hh, kb) in enumerate(turns_of(b)[j]):
                            grp = hh % 2
                            if kind == "cmp":
                                lhs, rhs, last = pT[0:N_CMP, 4 * j + n, :], vc[0:N_CMP, grp, :], True
                            else:
                                v = {
                                    "sel": z[:, kb, C_KVS + 128 + HD * grp : C_KVS + 128 + HD * (grp + 1)],
                                    "win": z[:, kb, C_KVW + 128 + HD * grp : C_KVW + 128 + HD * (grp + 1)],
                                    "dsa": zkv[:, kb, HD:P],
                                }[kind]
                                lhs, rhs, last = pT[:, 4 * j + n, :], v, kb == qt
                            ins = pe.matmul(O[b % 2][:, hh * HD : (hh + 1) * HD], lhs, rhs, start=kb == 0, stop=last)
                    ins.then_inc(o_filled, 1)

                def wait_roped(n):
                    pe.wait_ge(roped, l * 8 + n)

                def pairs_of(col, n):
                    return [z[:, tok, col + P * pr : col + P * (pr + 1)] for pr in n for tok in range(TOKS)]

                chunk(0, 0)
                lift(l, 1, 1, 0)
                lift(l, 1, 1, 1)
                chunk(0, 1)
                chunk(1, 0)
                pe.wait_ge(gz_drained, l * 24 + 2)
                turn("ckv", [z[:, tok, C_CKV : C_CKV + P] for tok in range(TOKS)])
                chunk(1, 1)
                t = open_turn("kv", "ckv")
                for tok in range(TOKS):
                    ins = pe.matmul(
                        t[:, tok * P : (tok + 1) * P], ckvT[:, tok * P : (tok + 1) * P], small[:, W_UKV : W_UKV + P],
                        start=True, stop=True)
                ins.then_inc(t_filled, 1)
                chunk(2, 0)
                wait_roped(2)
                turn("ik", [ikd[:, tok, :, :].rearrange("p a d -> p (a d)") for tok in range(TOKS)])
                turn("iq", pairs_of(C_IQ, range(2)))
                chunk(2, 1)
                wait_roped(4)
                turn("kd", [kd[:, tok, :, :].rearrange("p a d -> p (a d)") for tok in range(TOKS)])
                wait_drained(pe, l, "ik", "iq")
                scores(0, iqT, ikT, range(2), 0, P)
                chunk(3, 0)
                wait_roped(3)
                turn("kvc", pairs_of(C_KVC, range(2)))
                scores(1, iqT, ikT, range(2), 1, S)
                chunk(3, 1)
                wait_roped(6)
                turn("ksw", pairs_of(C_KVS, [0]) + pairs_of(C_KVW, [0]))
                chunk(4, 0)
                wait_roped(7)
                turn("qn0", pairs_of(C_QN, [0, 1]))
                turn("qn1", pairs_of(C_QN, [2, 3]))
                chunk(4, 1)
                t = open_turn("hid")
                pe.wait_ge(shifted, l * 16 + 16)
                pe.wait_ge(w1_in_sem, l * 16 + 16)
                for y_ in range(2):
                    for k in range(16):
                        pe.matmul(
                            t[:, 64 + y_ : 65 + y_], w1[:, y_, k, :], small[:, W_POS + 16 * y_ + k : W_POS + 16 * y_ + k + 1],
                            start=k == 0, stop=k == 15)
                    for k in range(16):
                        ins = pe.matmul(
                            t[:, 32 * y_ : 32 * y_ + 30].rearrange("p (g n) -> p g n", g=2), w1[:, y_, k, :],
                            kvcT[:, 2 * y_ : 2 * y_ + 2, 2 * k : 2 * k + 16 * (N_CMP - 1) + 1 : 16],
                            start=k == 0, stop=k == 15)
                ins.then_inc(t_filled, 1)
                chunk(5, 0)
                wait_roped(8)
                turn("qd0", pairs_of(C_QD, [0, 1]))
                turn("qd1", pairs_of(C_QD, [2, 3]))
                batch_scores(0)
                chunk(5, 1)
                t = open_turn("cmpo")
                pe.wait_ge(gelu_done, l + 1)
                for g in range(2):
                    pe.matmul(
                        t[g * HD : (g + 1) * HD, 0:N_CMP], small[:, W_W2 : W_W2 + HD],
                        gel[:, 4, 0, g * N_CMP : (g + 1) * N_CMP], start=True, stop=True)
                for g in range(2):
                    ins = pe.matmul(
                        t[0:N_CMP, 64 + g * HD : 64 + (g + 1) * HD], gel[:, 4, 1, g * N_CMP : (g + 1) * N_CMP],
                        small[:, W_W2 + HD : W_W2 + 2 * HD], start=True, stop=True)
                ins.then_inc(t_filled, 1)
                batch_turn(0)
                batch_scores(1)
                for k in range(12):
                    c, tok = Z_CHUNKS + k // 2, k % 2
                    chunk(c, tok)
                    batch_values(k)
                    batch_turn(k + 1)
                    if k + LEAD < NB:
                        batch_scores(k + LEAD)
                    if k < 2:
                        pe.wait_ge(gz_drained, l * 24 + 12)
                        t = open_turn(f"band{k}")
                        for g in range(2):
                            gg = 2 * k + g
                            u = [z[:, tk, C_U + gg * P : C_U + (gg + 1) * P] for tk in range(TOKS)]
                            band = const[:, K_BAND + gg * 384 : K_BAND + (gg + 1) * 384]
                            pe.matmul(t[:, g * S : (g + 1) * S], u[0], band[:, 0:S], start=g == 0, stop=False,
                                      skip_group_check=True)
                            ins = pe.matmul(t[:, g * S + P : (g + 1) * S], u[1], band[:, S : S + P], start=False,
                                            stop=True, skip_group_check=True)
                        ins.then_inc(t_filled, 1)
                    elif k < 4:
                        t = open_turn(f"yb{k - 2}", f"band{k - 2}")
                        for g in range(2):
                            gg = 2 * (k - 2) + g
                            ins = pe.matmul(
                                t[:, g * S : (g + 1) * S], small[:, W_POOL + gg * P : W_POOL + (gg + 1) * P],
                                pooledT[:, gg, :], start=True, stop=True)
                        ins.then_inc(t_filled, 1)

                def y_tiles(branch, tok):
                    return [y[:, tok, branch, k * P : (k + 1) * P] for k in range(4)]

                def project(b_, half, hi, lo, k0):
                    for tok in range(TOKS):
                        f = 24 + 4 * b_ + 2 * half + tok
                        if f < 26:
                            pe.wait_ge(gz_drained, l * 24 + f - 1)
                        else:
                            pe.wait_ge(gp_drained, l * 12 + f - 25)
                        ins = unit_gemm(23 + 2 * b_ + half, hi, lo, k0, tok, True, True)
                        ins.then_inc(unit_used if tok else g_filled, 1)

                pe.wait_ge(y_done, l * 2 + 2)
                turn("yc0", y_tiles(1, 0))
                turn("yc1", y_tiles(1, 1))
                wait_drained(pe, l, "yb0", "yb1")
                project(0, 0, ybhi, yblo, 0)
                batch_values(12)
                batch_turn(13)
                project(0, 1, ybhi, yblo, 0)
                batch_values(13)
                wait_drained(pe, l, "yc0", "yc1")
                project(1, 0, xhi, xlo, 0)
                project(1, 1, xhi, xlo, 0)
                pe.wait_ge(o_drained, l * NB + NB)
                turn("ya0", y_tiles(0, 0))
                turn("ya1", y_tiles(0, 1))
                wait_drained(pe, l, "ya0", "ya1")
                project(2, 0, xhi, xlo, 4)
                project(2, 1, xhi, xlo, 4)
                for j, (tok, half) in enumerate(MERGED_ORDER):
                    pe.wait_ge(merged_done, l * 4 + j + 2)
                    turn(f"mg{j}", [gates[:, tok, D + half * 512 + k * P : D + half * 512 + (k + 1) * P] for k in range(4)])
                for n in range(2):
                    for tok in range(TOKS):
                        f = 36 + 2 * n + tok
                        if n == 0:
                            pe.wait_ge(gp_drained, l * 12 + f - 25)
                        else:
                            pe.wait_ge(x_up, lift_of(l, 2) * 4 + f - 37)
                        for a in range(2):
                            u = 29 + 2 * n + a
                            wait_drained(pe, l, f"mg{MERGED_ORDER.index((tok, a))}")
                            if n and tok:
                                lift(l, 2, 0, a)
                            ins = unit_gemm(u, xhi, xlo, 4 * a, tok, a == 0, a == 1)
                            if tok and a == 0:
                                ins.then_inc(unit_used, 1)
                        ins.then_inc(unit_used if tok else g_filled, 1)

            pe.nop().then_inc(unit_used, CREDIT)
            pe.wait_ge(first_const_in_sem, 16)
            with pe.Fori(0, L) as l:
                ffn(l, 0)
                mixer(l)
                ffn(l, 1)


IN_SPLITS = (512, 128, 256, 64, 4, 512, 512, 256, 256, 256, 24, 3072)
PAIRED = [0, 4, 1, 5, 2, 6, 3, 7]


def _tiles(w):
    k, n = w.shape
    return w.reshape(k // P, P, n).transpose(1, 0, 2).reshape(P, -1)


def _ffn_units(gate, up, down):
    units = []

    def gu(i):
        c = slice(i * FCH, (i + 1) * FCH)
        w = np.concatenate([gate[:, c], up[:, c]], axis=1)
        units.extend([_tiles(w[:512]), _tiles(w[512:])])

    def dn(i):
        units.append(_tiles(down[i * FCH : (i + 1) * FCH]))

    gu(0)
    for i in range(1, FI):
        gu(i)
        dn(i - 1)
    dn(FI - 1)
    return units


def _mix_units(w_in, pa, pb, pc, w_out):
    offs = np.cumsum((0,) + IN_SPLITS)
    q, ckv, iq, ik, iw, u, cq, kvc, kvs, kvw, gate, merge = (
        w_in[:, offs[i] : offs[i + 1]] for i in range(len(IN_SPLITS)))
    cq = cq.reshape(D, 8, HD)[:, PAIRED].reshape(D, 512)
    gate = gate.reshape(D, 8, 3)[:, PAIRED].transpose(0, 2, 1).reshape(D, 24)
    pc = pc.reshape(8, HD, D)[PAIRED].reshape(512, D)
    cols = np.concatenate([ckv, ik, iw, gate, iq, kvc, kvs, kvw, cq, q, u, merge], axis=1)
    first = np.zeros((P, UNIT), np.float32)
    first[:, : KT * C_S] = _tiles(cols[:, :C_S])
    units = [first]
    for c in range(CHUNKS - 1):
        w = cols[:, C_S + c * 512 : C_S + (c + 1) * 512]
        units += [_tiles(w[:512]), _tiles(w[512:])]
    for w in (pb, pc, pa):
        units += [_tiles(w[:, :512]), _tiles(w[:, 512:])]
    for n in range(2):
        w = w_out[:, n * 512 : (n + 1) * 512]
        units += [_tiles(w[:512]), _tiles(w[512:])]
    return units


def _constants():
    c = np.zeros((P, KC), np.float32)
    r = np.arange(P)
    c[:, K_ID : K_ID + P] = np.eye(P)
    c[:, K_CB + P : K_CB + 2 * P] = np.where(r[None, :] <= r[:, None], 0.0, NEG)
    ends = np.arange(N_CMP) * 16 + 31
    for qt in range(2):
        t = qt * P + r
        ok = ends[None, :] <= t[:, None]
        c[:, K_CMPB + 16 * qt : K_CMPB + 16 * qt + N_CMP] = np.where(ok, 0.0, NEG)
        c[:, K_VALID + qt] = ok.any(axis=1)
    for g, w in enumerate(WINDOWS):
        s, t = np.arange(S)[:, None], np.arange(S)[None, :]
        band = ((s <= t) & (s > t - w)) / np.minimum(t + 1, w) - (s == t)
        c[:, K_BAND + g * 384 : K_BAND + g * 384 + S] = band[:P]
        c[:, K_BAND + g * 384 + S : K_BAND + (g + 1) * 384] = band[P:, P:]
    exps = -np.arange(0, 2 * HALF_ROT, 2, dtype=np.float32) / np.float32(2 * HALF_ROT)
    c[:, K_FREQ : K_FREQ + HALF_ROT] = np.float64(THETA) ** exps.astype(np.float64)
    return c


def kernel(x, positions, ffn1_norm, ffn1_gate, ffn1_up, ffn1_down, mix_norm, w_in,
           dsa_kv_norm, dsa_w_ukv, pool_w, pool_scale, nsa_cmp_pos, nsa_cmp_w1, nsa_cmp_w2,
           proj_a, proj_b, proj_c, w_out, ffn2_norm, ffn2_gate, ffn2_up, ffn2_down, final_norm):
    import concourse.bacc as _bacc
    from concourse.bass_utils import run_bass_kernel_spmd as _run

    a = [np.asarray(v) for v in (
        x, positions, ffn1_norm, ffn1_gate, ffn1_up, ffn1_down, mix_norm, w_in, dsa_kv_norm, dsa_w_ukv, pool_w,
        pool_scale, nsa_cmp_pos, nsa_cmp_w1, nsa_cmp_w2, proj_a, proj_b, proj_c, w_out, ffn2_norm, ffn2_gate,
        ffn2_up, ffn2_down, final_norm)]
    (x, positions, ffn1_norm, ffn1_gate, ffn1_up, ffn1_down, mix_norm, w_in, dsa_kv_norm, dsa_w_ukv, pool_w,
     pool_scale, nsa_cmp_pos, nsa_cmp_w1, nsa_cmp_w2, proj_a, proj_b, proj_c, w_out, ffn2_norm, ffn2_gate,
     ffn2_up, ffn2_down, final_norm) = a
    units = []
    small = np.zeros((L + 1, P, W_SMALL), np.float32)
    w1 = np.zeros((L, P, W1C), np.float32)
    for l in range(L):
        units += _ffn_units(ffn1_gate[l], ffn1_up[l], ffn1_down[l])
        units += _mix_units(w_in[l], proj_a[l], proj_b[l], proj_c[l], w_out[l])
        units += _ffn_units(ffn2_gate[l], ffn2_up[l], ffn2_down[l])
        s = small[l]
        s[:, W_G1 : W_G1 + 8] = ffn1_norm[l].reshape(8, P).T
        s[:, W_GM : W_GM + 8] = mix_norm[l].reshape(8, P).T
        s[:, W_G2 : W_G2 + 8] = ffn2_norm[l].reshape(8, P).T
        s[:, W_KVG] = dsa_kv_norm[l]
        s[:, W_PSC : W_PSC + 4] = pool_scale[l].reshape(4, P).T
        s[:, W_POS : W_POS + 32] = nsa_cmp_pos[l].reshape(2, 16, P).transpose(2, 0, 1).reshape(P, 32)
        s[:, W_UKV : W_UKV + P] = dsa_w_ukv[l]
        s[:, W_POOL : W_POOL + 512] = pool_w[l].transpose(1, 0, 2).reshape(P, 512)
        s[:, W_W2 : W_W2 + P] = nsa_cmp_w2[l].transpose(1, 0, 2).reshape(P, P)
        w1[l] = nsa_cmp_w1[l].reshape(2, 16, P, P).transpose(2, 0, 1, 3).reshape(P, W1C)
    units += [np.zeros((P, UNIT), np.float32)] * PAD_UNITS
    arrays = {
        "x_in": x.reshape(S, D), "pos_in": positions.reshape(TOKS, P).T, "stream": np.stack(units), "small_in": small,
        "w1_in": w1, "const_in": _constants(), "final_in": final_norm,
    }
    nc = _bacc.Bacc("TRN2", target_bir_lowering=False, num_devices=1)
    args = []
    for name, v in arrays.items():
        arrays[name] = v = np.ascontiguousarray(v)
        args.append(nc.dram_tensor(name, v.shape, mybir.dt.from_np(v.dtype), kind="ExternalInput").ap())
    args.append(nc.dram_tensor("out", (S, D), F32, kind="ExternalOutput").ap())
    trunk(nc, *args)
    r = _run(nc, [arrays], core_ids=[0])
    return r.results[0]["out"].reshape(1, S, D)
```

```python
import math
from contextlib import ExitStack

import numpy as np

import concourse.bass as bass
from concourse import mybir

F32 = mybir.dt.float32
F32R = mybir.dt.float32r
I32 = mybir.dt.int32
ALU = mybir.AluOpType
ACT = mybir.ActivationFunctionType
AX = mybir.AxisListType

P = 128
L, S, D, F = 2, 256, 1024, 2816
TOKS = S // P
KT = D // P
HD, HALF_ROT = 64, 8
EPS = 1e-6
NEG = -1e30
TAKEN = -3e38
THETA = 500000.0
TOPK = min(256, S // 4)
N_CMP = (S - 32) // 16 + 1
WINDOWS = (2, 4, 8, 16)

UNIT = 2048
RING = 3
CREDIT = RING
PARTS = 2
PART = UNIT // PARTS
FCH = 256
FI = F // FCH
FFN_UNITS = 3 * FI
MIX_UNITS = 33
LAYER_UNITS = 2 * FFN_UNITS + MIX_UNITS
assert FFN_UNITS % RING == 0 and MIX_UNITS % RING == 0
PAD_UNITS = RING

C_CKV, C_IK, C_IW, C_GATE = 0, 128, 192, 196
C_S = 220
C_IQ, C_KVC, C_KVS, C_KVW, C_QN, C_QD, C_U = 220, 476, 732, 988, 1244, 1756, 2268
ZC = 2780
Z_CHUNKS = 6
CHUNKS = 12

W_G1, W_GM, W_G2, W_KVG, W_PSC, W_POS = 0, 8, 16, 24, 25, 29
W_UKV, W_POOL, W_W2 = 61, 189, 701
W_SMALL = 829
W1C = 2 * 16 * P

K_ID, K_FREQ = 0, 128
KC_FIRST = K_FREQ + HALF_ROT
K_CB, K_CMPB, K_VALID, K_BAND = (KC_FIRST + o for o in (0, 256, 288, 290))
BAND0 = P + max(WINDOWS)
BANDC = BAND0 + P
KC = K_BAND + len(WINDOWS) * BANDC

BATCHES = (
    [("sel", qt, g) for qt in range(2) for g in range(2)]
    + [("win", qt, g) for qt in range(2) for g in range(2)]
    + [("cmp", qt, 0) for qt in range(2)]
    + [("dsa", qt, g) for qt in range(2) for g in range(2)]
)
NB = len(BATCHES)
LEAD = 2
WARM_UP = 16


def keys_of(b):
    kind, qt, _ = BATCHES[b]
    return N_CMP if kind == "cmp" else P * (qt + 1)


def heads_of(b):
    return 8 if BATCHES[b][0] == "cmp" else 4


def turns_of(b):
    kind, qt, _ = BATCHES[b]
    if kind == "cmp":
        return [[(h, 0) for h in range(4)], [(h, 0) for h in range(4, 8)]]
    blocks = [(h, kb) for h in range(4) for kb in range(qt + 1)]
    return [blocks[i : i + 4] for i in range(0, len(blocks), 4)]


def turn_names(b):
    return [f"p{b}_{j}" for j in range(len(turns_of(b)))]


def turn_order():
    names = ["ckv", "kv", "ik", "iq", "kd", "kvc", "ksw", "qn0", "qn1", "hid", "qd0", "qd1", "gelt", "cmpo"]
    names += turn_names(0)
    extra = {0: ["band0"], 1: ["band1"], 2: ["yb0"], 3: ["yb1"]}
    for k in range(12):
        names += turn_names(k + 1) + extra.get(k, [])
    names += ["yc0", "yc1"] + turn_names(13) + ["ya0", "ya1", "mg0", "mg1", "mg2", "mg3"]
    return names


TURNS = turn_order()
TURN_AT = {n: i for i, n in enumerate(TURNS)}
PER_BANK = [len(TURNS[0::2]), len(TURNS[1::2])]


def trunk(nc, x_in, pos_in, stream, small_in, w1_in, const_in, final_in, out):
    ctx = ExitStack()
    with ctx:
        def sb(name, shape, dt=F32):
            return ctx.enter_context(nc.sbuf_tensor(name, shape, dt))

        def sem(name):
            return ctx.enter_context(nc.semaphore(name))

        raw = [sb(f"raw{i}", [P, UNIT]) for i in range(RING)]
        whi = [sb(f"whi{i}", [P, UNIT], F32R) for i in range(RING)]
        wlo = [sb(f"wlo{i}", [P, UNIT], F32R) for i in range(RING)]
        x = sb("x", [P, TOKS, D])
        xhi = sb("xhi", [P, KT, S], F32R)
        xlo = sb("xlo", [P, KT, S], F32R)
        z = sb("z", [P, TOKS, ZC])
        gates = sb("gates", [P, TOKS, 3 * D])
        gain = z[:, 0, 0:D]
        w1 = gates[:, :, :].rearrange("p t c -> p (t c)")[:, 0:W1C].rearrange("p (y k h) -> p y k h", y=2, k=16)
        ybhi = sb("ybhi", [P, 4, S], F32R)
        yblo = sb("yblo", [P, 4, S], F32R)
        small = sb("small", [P, W_SMALL])
        const = sb("const", [P, KC])
        ident = const[:, K_ID : K_ID + P]
        shared_q = sb("shared_q", [P, 2048])
        qnT = shared_q[:, 0:1024].rearrange("p (a t) -> p a t", a=4)
        qdT = shared_q[:, 1024:2048].rearrange("p (a t) -> p a t", a=4)
        h = shared_q[:, 0:512].rearrange("p (t c) -> p t c", t=TOKS)
        tg = shared_q[:, 512:1024].rearrange("p (t c) -> p t c", t=TOKS)
        hThi = [ybhi[:, 0:2, :], ybhi[:, 2:4, :]]
        hTlo = [yblo[:, 0:2, :], yblo[:, 2:4, :]]
        ikd = sb("ikd", [P, TOKS, 2, HD])
        kd = sb("kd", [P, TOKS, 2, HD])
        iqT = sb("iqT", [P, 2, S])
        oacc = iqT[:, :, :].rearrange("p a t -> p (a t)")
        ikT = sb("ikT", [P, S])
        kdT = sb("kdT", [P, S])
        kswT = sb("kswT", [P, 2, S])
        zkv = sb("zkv", [P, TOKS, P])
        ckvT = sb("ckvT", [P, S])
        kvcT = sb("kvcT", [P, 4, S])
        pooledT = kvcT
        sm = sb("sm", [P, 1024])
        probs = sb("probs", [P, 1024])
        pT = sb("pT", [P, 8, P])
        y = sb("y", [P, TOKS, 2, 512])
        work = sb("work", [P, TOKS, S])
        top8 = sb("top8", [P, TOKS, 8])
        trig = sb("trig", [P, 2, TOKS, 16])
        cos16, sin16 = trig[:, 0], trig[:, 1]
        rot = sb("rot", [P, 2, TOKS, 8, 16])
        stat = sb("stat", [P, 64])
        ss, ms, msh, rs, t0, t1, rs_half, rs_sq = (stat[:, 2 * i : 2 * i + 2] for i in range(8))
        sskv, kms, kmsh, rkv, kt0, kt1 = (stat[:, 16 + 2 * i : 18 + 2 * i] for i in range(6))
        unread = stat[:, 28:29]
        posf = stat[:, 30:32]
        negmax = stat[:, 32:40]
        rowmax = stat[:, 40:48]
        sums = [stat[:, 48 + 8 * i : 56 + 8 * i] for i in range(2)]
        sig = sb("sig", [P, TOKS, 24])
        fac = sb("fac", [P, 8])
        windows = sm[:, 0 : 2 * 16 * 2 * N_CMP].rearrange("p (y k g n) -> p y k g n", y=2, k=16, g=2)
        ROWS = 2 * N_CMP
        hid_v, hid_t = oacc[0:ROWS, 0:256], oacc[0:ROWS, 256:512]
        gelT = oacc[:, 0 : 2 * ROWS].rearrange("p (y n) -> p y n", y=2)
        kcT = sb("kcT", [P, 16])
        vc = ikd[:, 0, :, :]
        posi = sb("posi", [P, TOKS], I32)
        ang = rot[:, 0, :, :, :].rearrange("p t h d -> p (t h d)")[:, 0 : 5 * 16].rearrange("p (s t f) -> p s t f", s=5, t=TOKS)

        def bank(name):
            return ctx.enter_context(nc.psum_tensor(name, [P, 512], F32))

        G = [bank("G0"), bank("G1")]
        T = [bank("T0"), bank("T1")]
        SC = [bank("SC0"), bank("SC1")]
        O = [bank("O0"), bank("O1")]
        ACC = [[SC[0], SC[1]], [O[0], O[1]]]

        raw_in = [sem(f"raw_in{i}") for i in range(RING)]
        hi_done = sem("hi_done")
        lo_done = sem("lo_done")
        unit_used = sem("unit_used")
        x_in_sem = [sem(f"x_in_sem{i}") for i in range(TOKS)]
        first_const_in_sem = sem("first_const_in_sem")
        const_in_sem = sem("const_in_sem")
        pos_in_sem = sem("pos_in_sem")
        small_in_sem = sem("small_in_sem")
        w1_in_sem = sem("w1_in_sem")
        final_in_sem = sem("final_in_sem")
        x_up = sem("x_up")
        xt_filled = sem("xt_filled")
        xhi_done = sem("xhi_done")
        xlo_done = sem("xlo_done")
        squares_done = sem("squares_done")
        rstd_done = sem("rstd_done")
        gu_filled = sem("gu_filled")
        tanh_done = sem("tanh_done")
        h_done = sem("h_done")
        ht_filled = sem("ht_filled")
        ht_hi_done = sem("ht_hi_done")
        ht_lo_done = sem("ht_lo_done")
        acc_done = sem("acc_done")
        g_filled = sem("g_filled")
        gz_drained = sem("gz_drained")
        gp_drained = sem("gp_drained")
        t_filled = sem("t_filled")
        t_drained = [sem("t_drained0"), sem("t_drained1")]
        t_hi_done = sem("t_hi_done")
        s_filled = sem("s_filled")
        s_drained = sem("s_drained")
        index_summed = sem("index_summed")
        o_filled = sem("o_filled")
        o_drained = sem("o_drained")
        negmax_done = sem("negmax_done")
        exp_done = sem("exp_done")
        roped = sem("roped")
        kv_squares = sem("kv_squares")
        gate_tanh = sem("gate_tanh")
        shifted = sem("shifted")
        windows_done = sem("windows_done")
        gelu_inner = sem("gelu_inner")
        gelu_tanh = sem("gelu_tanh")
        gelu_done = sem("gelu_done")
        y_done = sem("y_done")
        merged_done = sem("merged_done")
        out_ready = sem("out_ready")
        out_sent = sem("out_sent")
        dve_step = sem("dve_step")
        pool_step = sem("pool_step")

        block = ctx.enter_context(nc.Block())

        class Steps:

            def __init__(self, eng, s):
                self.eng, self.s, self.n = eng, s, 0

            def restart(self):
                self.eng.sem_clear(self.s)
                self.n = 0

            def then(self, ins, between=None):
                ins.then_inc(self.s, 1)
                self.n += 1
                if between:
                    between()
                self.eng.wait_ge(self.s, self.n)

        def filled(l, name):
            return l * len(TURNS) + TURN_AT[name] + 1

        def wait_drained(eng, l, *names, opening=None):
            last = [0, 0]
            for i in map(TURN_AT.get, names):
                last[i % 2] = max(last[i % 2], i // 2 + 1)
            if opening is not None:
                i = TURN_AT[opening]
                last[i % 2] = max(last[i % 2], i // 2)
            for b in range(2):
                if last[b]:
                    eng.wait_ge(t_drained[b], l * PER_BANK[b] + last[b])

        def turn_bank(name):
            return T[TURN_AT[name] % 2]

        def mark_drained(ins, name):
            ins.then_inc(t_drained[TURN_AT[name] % 2], 1)

        def ffn_base(l, occ):
            return l * LAYER_UNITS + occ * (FFN_UNITS + MIX_UNITS)

        def mix_base(l):
            return l * LAYER_UNITS + FFN_UNITS

        def unit_value(l, n):
            return l * LAYER_UNITS + n + 1 + CREDIT

        def part_value(n, part, base=0):
            return base * PARTS + (n * PARTS + part + 1 + CREDIT * PARTS)

        OPENING = [(0, 0), (1, 0), (0, 1), (1, 1)]

        def wait_g(eng, l, f):
            if f == 1 or f % 2 == 0 and f != 2:
                eng.wait_ge(g_filled, l * 20 + (f + 1) // 2 + 1)
            else:
                n = 0 if f == 2 else f - 1 if f < 24 else 23 + (f - 25) // 2 if f < 36 else 30 + (f - 37)
                eng.wait_ge(unit_used, unit_value(l, FFN_UNITS + n))

        BY_HALF = [(0, 0), (1, 0), (0, 1), (1, 1)]


        def lift_of(l, which):
            return l * 3 + which

        LIFT_GAIN = [W_G1, W_GM, W_G2]
        LIFT_LEAD = [3, 11, 3]
        LIFT_NEEDS = [[1, 2, 3, 4], [1, 2, 3, 4], [1, 3, 3, 4]]
        MERGED_ORDER = BY_HALF

        @block.sync
        def _(sp):
            def load_unit(j, n):
                sp.dma_start(raw[j][:, :], stream[n, :, :].rearrange("u p n -> p (u n)")).then_inc(raw_in[j], 16)

            x_v = x_in.rearrange("(t p) d -> p t d", p=P)
            sp.dma_start(x[:, 0, :], x_v[:, 0, :]).then_inc(x_in_sem[0], 16)
            sp.dma_start(const[:, 0:KC_FIRST], const_in[:, 0:KC_FIRST]).then_inc(first_const_in_sem, 16)
            load_unit(0, slice(0, 1))
            sp.dma_start(small[:, :], small_in[0, :, :]).then_inc(small_in_sem, 16)
            load_unit(1, slice(1, 2))
            sp.dma_start(x[:, 1, :], x_v[:, 1, :]).then_inc(x_in_sem[1], 16)
            load_unit(2, slice(2, 3))
            sp.dma_start(const[:, KC_FIRST:KC], const_in[:, KC_FIRST:KC]).then_inc(const_in_sem, 16)
            n_units = L * LAYER_UNITS + PAD_UNITS
            with sp.Fori(1, n_units // RING) as r:
                for j in range(RING):
                    sp.wait_ge(hi_done, r * RING * PARTS + (j + 1) * PARTS)
                    sp.wait_ge(lo_done, r * RING * PARTS + (j + 1) * PARTS)
                    load_unit(j, bass.ds(r * RING + j, 1))
            for j in range(1, RING):
                sp.wait_ge(raw_in[j], n_units // RING * 16)
            sp.wait_ge(x_up, 4 * (3 * L))
            sp.dma_start(gain, final_in.partition_broadcast(P)).then_inc(final_in_sem, 16)
            out_v = out.rearrange("(t p) d -> p t d", p=P)
            for tok in range(TOKS):
                for half in range(2):
                    sl = slice(half * 512, half * 512 + 512)
                    sp.wait_ge(out_ready, 2 * tok + half + 1)
                    sp.dma_start(out_v[:, tok, sl], x[:, tok, sl]).then_inc(out_sent, 16)
            sp.wait_ge(out_sent, 16 * 2 * TOKS)

        @block.gpsimd
        def _(pool):
            pool.dma_start(posi[:, :], pos_in).then_inc(pos_in_sem, 16)
            for tok in range(TOKS):
                pool.wait_ge(x_in_sem[tok], 16)
                pool.nop().then_inc(x_up, 2)
            steps = Steps(pool, pool_step)

            def series_term(n):
                return (-1.0) ** (n // 2) / float(math.factorial(n))

            def rope(cols, heads, last):
                v = cols.rearrange("p t (h d) -> p t h d", d=HD)
                c = cos16[:, :, :].unsqueeze(2).to_broadcast([P, TOKS, heads, 16])
                s = sin16[:, :, :].unsqueeze(2).to_broadcast([P, TOKS, heads, 16])
                a, b = rot[:, 0, :, 0:heads, :], rot[:, 1, :, 0:heads, :]
                pool.tensor_tensor(a, v[:, :, :, 0:16], c, ALU.mult)
                pool.tensor_tensor(b[:, :, :, 0:8], v[:, :, :, 8:16], s[:, :, :, 0:8], ALU.mult)
                steps.then(pool.tensor_tensor(b[:, :, :, 8:16], v[:, :, :, 0:8], s[:, :, :, 8:16], ALU.mult))
                o = pool.tensor_tensor(v[:, :, :, 0:16], a, b, ALU.add)
                if last:
                    o.then_inc(roped, 1)
                else:
                    steps.then(o)

            pool.wait_ge(pos_in_sem, 16)
            pool.wait_ge(first_const_in_sem, 16)
            then = steps.then
            a0, a1, a2, a3, sq = (ang[:, i, :, :] for i in range(5))
            then(pool.tensor_copy(posf, posi[:, :]))
            freq = const[:, K_FREQ : K_FREQ + HALF_ROT].unsqueeze(1).to_broadcast([P, TOKS, HALF_ROT])
            then(pool.tensor_tensor(a0, posf.unsqueeze(2).to_broadcast([P, TOKS, HALF_ROT]), freq, ALU.mult))
            magic = 1.5 * 2.0**23
            turns = a1
            then(pool.tensor_scalar(turns, a0, float(np.float32(1 / (2 * np.pi))), magic, ALU.mult, ALU.add))
            then(pool.tensor_scalar(turns, turns, -magic, None, ALU.add))
            then(pool.tensor_scalar(a2, turns, 1.0 / 4096, magic, ALU.mult, ALU.add))
            then(pool.tensor_scalar(a2, a2, -magic, 4096.0, ALU.add, ALU.mult))
            then(pool.tensor_tensor(a3, turns, a2, ALU.subtract))
            rest = 2 * np.pi
            for bits in (9, 21, 33, 45):
                part = np.floor(rest * 2.0**bits) / 2.0**bits
                rest -= part
                for src in (a2, a3):
                    then(pool.tensor_scalar(sq, src, -float(part), None, ALU.mult))
                    then(pool.tensor_tensor(a0, a0, sq, ALU.add))
            then(pool.tensor_scalar(a0, a0, 0.5, None, ALU.mult))
            then(pool.tensor_tensor(sq, a0, a0, ALU.mult))
            for series, start in ((a1, 1), (a2, 0)):
                n = start + 14
                then(pool.tensor_scalar(series, sq, series_term(n), series_term(n - 2), ALU.mult, ALU.add))
                for k in range(n - 4, start - 1, -2):
                    then(pool.tensor_tensor(series, series, sq, ALU.mult))
                    then(pool.tensor_scalar(series, series, series_term(k), None, ALU.add))
            then(pool.tensor_tensor(a1, a1, a0, ALU.mult))
            then(pool.tensor_tensor(a2, a2, a1, ALU.mult))
            then(pool.tensor_tensor(a3, a1, a1, ALU.mult))
            for i in range(2):
                pool.tensor_scalar(cos16[:, :, 8 * i : 8 * i + 8], a3, -2.0, 1.0, ALU.mult, ALU.add)
            pool.tensor_scalar(sin16[:, :, 0:8], a2, -2.0, None, ALU.mult)
            then(pool.tensor_scalar(sin16[:, :, 8:16], a2, 2.0, None, ALU.mult))
            with pool.Fori(0, L) as l:
                steps.restart()
                pool.wait_ge(gz_drained, l * 24 + 3)
                rope(z[:, :, C_IK : C_IK + HD], 1, False)
                src = z[:, :, C_IK : C_IK + HD].unsqueeze(2).to_broadcast([P, TOKS, 2, HD])
                pool.tensor_copy(ikd[:, :, :, :], src).then_inc(roped, 1)
                pool.wait_ge(gz_drained, l * 24 + 4)
                rope(z[:, :, C_IQ : C_IQ + 256], 4, True)
                pool.wait_ge(roped, l * 8 + 2)
                rope(z[:, :, C_KVC : C_KVC + 128], 2, True)
                wait_drained(pool, l, "kv")
                pool.wait_ge(roped, l * 8 + 3)
                rope(zkv[:, :, 0:HD], 1, False)
                src = zkv[:, :, 0:HD].unsqueeze(2).to_broadcast([P, TOKS, 2, HD])
                pool.tensor_copy(kd[:, :, :, :], src).then_inc(roped, 1)
                pool.wait_ge(gz_drained, l * 24 + 6)
                rope(z[:, :, C_KVS : C_KVS + 128], 2, True)
                pool.wait_ge(roped, l * 8 + 5)
                rope(z[:, :, C_KVW : C_KVW + 128], 2, True)
                pool.wait_ge(gz_drained, l * 24 + 8)
                pool.wait_ge(roped, l * 8 + 6)
                rope(z[:, :, C_QN : C_QN + 512], 8, True)
                pool.wait_ge(index_summed, l * 2 + 2)
                pool.wait_ge(shifted, l * 16 + 16)
                for gg in range(4):
                    y_, g = gg // 2, gg % 2
                    for ko in range(2):
                        k = slice(8 * ko, 8 * ko + 8)
                        tokens = kvcT[:, gg, 16 * ko : 16 * ko + 16 * N_CMP].rearrange(
                            "p (n k two) -> p k n two", k=8, two=2)[:, :, :, 0]
                        posn = small[:, W_POS + 16 * y_ + 8 * ko : W_POS + 16 * y_ + 8 * ko + 8]
                        ins = pool.tensor_tensor(
                            windows[:, y_, k, g, :], tokens, posn.unsqueeze(2).to_broadcast([P, 8, N_CMP]), ALU.add)
                ins.then_inc(windows_done, 1)
                pool.wait_ge(gz_drained, l * 24 + 10)
                pool.wait_ge(roped, l * 8 + 7)
                rope(z[:, :, C_QD : C_QD + 512], 8, True)
                pool.wait_ge(roped, l * 8 + 8)

        @block.scalar
        def _(act):
            def round_unit(s):
                for c in range(0, UNIT, PART):
                    act.activation(whi[s][:, c : c + PART], raw[s][:, c : c + PART], ACT.Copy).then_inc(hi_done, 1)

            def split(l, at, u):
                n = at + u
                s = n % RING
                act.wait_ge(raw_in[s], (l * (LAYER_UNITS // RING) + n // RING + 1) * 16)
                act.wait_ge(unit_used, l * LAYER_UNITS + (n + 1))
                round_unit(s)

            def split_in_loop(l, i, at, u):
                n = at + u
                s = n % RING
                act.wait_ge(raw_in[s], (l * (LAYER_UNITS // RING) + i + n // RING + 1) * 16)
                act.wait_ge(unit_used, l * LAYER_UNITS + i * RING + (n + 1))
                round_unit(s)

            def lift(l, which, tok):
                v = lift_of(l, which)
                if which == 0 and tok == 0:
                    act.wait_ge(small_in_sem, (l + 1) * 16)
                for half in range(2):
                    act.wait_ge(xt_filled, v * 4 + 2 * tok + half + 1)
                    for k in range(4):
                        g = LIFT_GAIN[which] + half * 4 + k
                        act.activation(
                            xhi[:, half * 4 + k, tok * P : (tok + 1) * P], T[half][:, k * P : (k + 1) * P],
                            ACT.Copy, scale=small[:, g : g + 1],
                        ).then_inc(xhi_done, 1)

            def square(v, tok):
                if tok:
                    act.wait_ge(x_up, (v + 1) * 4)
                    act.wait_ge(squares_done, v * 2 + 1)
                act.activation(
                    probs[:, :], x[:, tok, :], ACT.Square, accum_out=ss[:, tok : tok + 1]
                ).then_inc(squares_done, 1)

            def ffn(l, occ):
                o = l * 2 + occ
                at = occ * (FFN_UNITS + MIX_UNITS)
                if occ == 0:
                    lift(l, 0, 0)
                    square(lift_of(l, 0), 0)
                    split(l, at, 1)
                    square(lift_of(l, 0), 1)
                    lift(l, 0, 1)
                    split(l, at, 2)

                def swish(g, tok, last_unit):
                    if tok:
                        act.wait_ge(unit_used, last_unit + 1 + CREDIT)
                    else:
                        act.wait_ge(gu_filled, g + 1)
                    act.activation(tg[:, tok, :], G[tok][:, 0:FCH], ACT.Tanh, scale=rs_half[:, tok : tok + 1]).then_inc(
                        tanh_done, 1
                    )

                def turn_h(n, j=0):
                    act.wait_ge(ht_filled, n)
                    act.activation(hThi[j].rearrange("p k t -> p (k t)"), T[0][:, :], ACT.Copy).then_inc(ht_hi_done, 1)

                act.wait_ge(rstd_done, lift_of(l, 2 * occ) + 1)
                if occ == 0:
                    act.wait_ge(merged_done, l * 4 + 1)
                    act.dma_start(
                        gates[:, :, :].rearrange("p t c -> p (t c)")[:, 0:W1C],
                        w1_in[bass.ds(l, 1), :, :].rearrange("l p n -> p (l n)"),
                    ).then_inc(w1_in_sem, 16)
                else:
                    act.wait_ge(xlo_done, (lift_of(l, 2) + 1) * 16)
                    act.dma_start(
                        small[:, :], small_in[bass.ds(l + 1, 1), :, :].rearrange("l p n -> p (l n)")
                    ).then_inc(small_in_sem, 16)
                swish(o * FI, 0, None)
                split(l, at, 3)
                swish(o * FI, 1, l * LAYER_UNITS + (at + 1))
                split(l, at, 4)
                with act.Fori(1, FI - 1) as i:
                    g = o * FI + i
                    swish(g, 0, None)
                    turn_h(g)
                    split_in_loop(l, i, at, 2)
                    swish(g, 1, l * LAYER_UNITS + i * RING + at)
                    split_in_loop(l, i, at, 3)
                    split_in_loop(l, i, at, 4)
                last = FI - 1
                swish(o * FI + last, 0, None)
                turn_h(o * FI + last)
                split(l, at, 3 * last + 2)
                swish(o * FI + last, 1, l * LAYER_UNITS + last * RING + at)
                split(l, at, 3 * last + 3)
                turn_h(o * FI + FI, 1)
                if occ == 0:
                    split(l, FFN_UNITS, 1)
                    lift(l, 1, 0)
                    square(lift_of(l, 1), 0)
                    split(l, FFN_UNITS, 2)
                    square(lift_of(l, 1), 1)
                    lift(l, 1, 1)

            def mixer(l):
                at = FFN_UNITS
                act.wait_ge(rstd_done, lift_of(l, 1) + 1)

                def drain_z(f):
                    c, tok = OPENING[f] if f < 4 else (f // 2, f % 2)
                    wait_g(act, l, f)
                    lo, hi = (0, C_S) if c == 0 else (C_S + (c - 1) * 512, C_S + c * 512)
                    act.activation(
                        z[:, tok, lo:hi], G[f % 2][:, 0 : hi - lo], ACT.Copy, scale=rs[:, tok : tok + 1]
                    ).then_inc(gz_drained, 1)

                def drain_gate(c, tok):
                    wait_g(act, l, 2 * c + tok)
                    o = (c - Z_CHUNKS) * 512
                    act.activation(
                        gates[:, tok, o : o + 512], G[tok][:, :], ACT.Tanh, scale=rs_half[:, tok : tok + 1]
                    ).then_inc(gz_drained, 1)

                def drain(name, dst, src, **kw):
                    act.wait_ge(t_filled, filled(l, name))
                    mark_drained(act.activation(dst, src, kw.pop("func", ACT.Copy), **kw), name)

                def relu(qt):
                    n = P * (qt + 1)
                    act.wait_ge(s_filled, l * (NB + 2) + qt + 1)
                    if qt:
                        act.wait_ge(index_summed, l * 2 + 1)
                    rl = sm[:, 0 : 4 * n].rearrange("p (a b n) -> p a b n", a=2, b=2)
                    for half in range(2):
                        ins = act.activation(
                            rl[:, :, half, :], SC[half][:, 0 : 2 * n].rearrange("p (a n) -> p a n", a=2),
                            ACT.Relu, scale=1.0 / 16,
                        )
                    ins.then_inc(s_drained, 1)

                def exps(b):
                    n, nh = keys_of(b), heads_of(b)
                    w = 16 if n == N_CMP else n
                    act.wait_ge(negmax_done, l * NB + b + 1)
                    if b:
                        act.wait_ge(t_filled, filled(l, turn_names(b - 1)[-1]))
                    for hh in range(nh):
                        ins = act.activation(
                            probs[:, hh * w : hh * w + n], sm[:, hh * w : hh * w + n], ACT.Exp,
                            scale=0.125, bias=negmax[:, hh : hh + 1], accum_out=sums[b % 2][:, hh : hh + 1],
                        )
                    ins.then_inc(exp_done, 1)

                def drain_probs(b):
                    if b:
                        act.wait_ge(o_filled, l * NB + b)
                    rows = N_CMP if BATCHES[b][0] == "cmp" else P
                    for j, name in enumerate(turn_names(b)):
                        n = len(turns_of(b)[j])
                        drain(
                            name, pT[0:rows, 4 * j : 4 * j + n, :].rearrange("p b q -> p (b q)"),
                            turn_bank(name)[0:rows, 0 : n * P],
                        )

                def split_y(name, dst, ks):
                    tok = int(name[-1]) if name[:2] in ("yc", "ya") else MERGED_ORDER[int(name[-1])][0]
                    act.wait_ge(t_filled, filled(l, name))
                    act.activation(
                        dst[:, ks : ks + 4, tok * P : (tok + 1) * P],
                        turn_bank(name)[:, :].rearrange("p (k t) -> p k t", k=4), ACT.Copy,
                    ).then_inc(t_hi_done, 1)

                def split_mg(j):
                    split_y(f"mg{j}", xhi, 4 * MERGED_ORDER[j][1])

                for f in range(3):
                    drain_z(f)
                act.wait_ge(gz_drained, l * 24 + 3)
                for tok in range(TOKS):
                    if tok:
                        act.wait_ge(kv_squares, l * 2 + 1)
                    act.activation(
                        probs[:, 0:P], z[:, tok, C_CKV : C_CKV + P], ACT.Square, accum_out=sskv[:, tok : tok + 1]
                    ).then_inc(kv_squares, 1)
                act.activation(sig[:, :, :], z[:, :, C_GATE : C_GATE + 24], ACT.Tanh, scale=0.5).then_inc(gate_tanh, 1)
                split(l, at, 3)
                split(l, at, 4)
                drain_z(3)
                drain("ckv", ckvT[:, :], turn_bank("ckv")[:, 0:S], scale=small[:, W_KVG : W_KVG + 1])
                split(l, at, 5)
                drain_z(4)
                drain("ik", ikT[:, :], turn_bank("ik")[:, 0:S])
                split(l, at, 6)
                drain_z(5)
                drain("iq", iqT[:, :, :].rearrange("p a t -> p (a t)"), turn_bank("iq")[:, :])
                split(l, at, 7)
                drain_z(6)
                drain("kd", kdT[:, :], turn_bank("kd")[:, 0:S])
                kvc = turn_bank("kvc")[:, :].rearrange("p (y t) -> p y t", y=2)
                act.wait_ge(t_filled, filled(l, "kvc"))
                act.activation(kvcT[0:HD, 0:4:2, :], kvc[0:HD], ACT.Copy)
                drain("kvc", kvcT[0:HD, 1:4:2, :], kvc[HD:P])
                wait_drained(act, l, "kvc")
                act.dma_start(kvcT[HD:P, :, 0 : S - 1], kvcT[0:HD, :, 1:S]).then_inc(shifted, 16)
                relu(0)
                split(l, at, 8)
                drain_z(7)
                drain("ksw", kswT[:, :, :].rearrange("p a t -> p (a t)"), turn_bank("ksw")[:, :])
                relu(1)
                split(l, at, 9)
                drain_z(8)
                for j in range(2):
                    drain(
                        f"qn{j}", qnT[:, 2 * j : 2 * j + 2, :].rearrange("p a t -> p (a t)"),
                        turn_bank(f"qn{j}")[:, :],
                    )
                split(l, at, 10)
                drain_z(9)
                act.wait_ge(gelu_inner, l + 1)
                act.activation(hid_t, hid_t, ACT.Tanh, scale=0.7978845608028654).then_inc(gelu_tanh, 1)
                split(l, at, 11)
                drain_z(10)
                for j in range(2):
                    drain(
                        f"qd{j}", qdT[:, 2 * j : 2 * j + 2, :].rearrange("p a t -> p (a t)"),
                        turn_bank(f"qd{j}")[:, :],
                    )
                drain("gelt", gelT.rearrange("p y n -> p (y n)"), turn_bank("gelt")[:, 0 : 2 * ROWS])
                exps(0)
                split(l, at, 12)
                drain_z(11)
                act.wait_ge(t_filled, filled(l, "cmpo"))
                act.activation(kcT[:, 0:N_CMP], turn_bank("cmpo")[:, 0:N_CMP], ACT.Copy, scale=0.5)
                drain(
                    "cmpo", vc[0:N_CMP, :, :].rearrange("p g d -> p (g d)"), turn_bank("cmpo")[0:N_CMP, 64:192],
                    scale=0.5,
                )
                drain_probs(0)
                exps(1)
                split(l, at, 13)
                for k in range(12):
                    c, tok = Z_CHUNKS + k // 2, k % 2
                    if tok:
                        split(l, at, 2 * c + 2)
                    drain_gate(c, tok)
                    drain_probs(k + 1)
                    if k + LEAD < NB:
                        exps(k + LEAD)
                    if k < 2:
                        drain(
                            f"band{k}", pooledT[:, 2 * k : 2 * k + 2, :].rearrange("p g t -> p (g t)"),
                            turn_bank(f"band{k}")[:, :],
                        )
                    elif k < 4:
                        name = f"yb{k - 2}"
                        act.wait_ge(t_filled, filled(l, name))
                        for g in range(2):
                            gg = 2 * (k - 2) + g
                            ins = act.activation(
                                ybhi[:, gg, :], turn_bank(name)[:, g * S : (g + 1) * S], ACT.Copy,
                                scale=small[:, W_PSC + gg : W_PSC + gg + 1],
                            )
                        ins.then_inc(t_hi_done, 1)
                    if tok:
                        split(l, at, 2 * c + 3)
                for j in range(2):
                    split_y(f"yc{j}", xhi, 0)
                split(l, at, 26)
                drain_probs(13)
                split(l, at, 27)
                split(l, at, 28)
                for j in range(2):
                    split_y(f"ya{j}", xhi, 4)
                split(l, at, 29)
                split(l, at, 30)
                split_mg(0)
                split_mg(1)
                split_mg(2)
                split(l, at, 31)
                split_mg(3)
                for u in range(32, 34):
                    split(l, at, u)
                lift(l, 2, 0)
                split(l, at, 34)
                square(lift_of(l, 2), 0)
                square(lift_of(l, 2), 1)
                lift(l, 2, 1)
                split(l, at, 35)

            act.nop().then_inc(hi_done, CREDIT * PARTS)
            act.wait_ge(raw_in[0], 16)
            act.wait_ge(unit_used, 1)
            round_unit(0)
            with act.Fori(0, L) as l:
                ffn(l, 0)
                mixer(l)
                ffn(l, 1)
            for tok in range(TOKS):
                act.wait_ge(x_up, 12 * L + 2 * tok + 2)
                square(3 * L, tok)
            act.wait_ge(small_in_sem, (L + 1) * 16)

        @block.vector
        def _(dve):
            steps = Steps(dve, dve_step)

            def split(l, at, u):
                n = at + u
                for part in range(PARTS):
                    dve.wait_ge(hi_done, part_value(n, part, l * LAYER_UNITS))
                    subtract_hi(n % RING, part)

            def split_in_loop(l, i, at, u):
                n = at + u
                for part in range(PARTS):
                    dve.wait_ge(hi_done, part_value(n, part, l * LAYER_UNITS + i * RING))
                    subtract_hi(n % RING, part)

            def subtract_hi(s, part):
                c = slice(part * PART, (part + 1) * PART)
                dve.tensor_tensor(
                    wlo[s][:, c], raw[s][:, c], whi[s][:, c].bitcast(F32), ALU.subtract
                ).then_inc(lo_done, 1)

            def rsqrt(sumsq, m, mh, r, a, b, n, between=None):
                def then(ins):
                    steps.then(ins, between)

                then(dve.tensor_scalar(m, sumsq, 1.0 / n, EPS, ALU.mult, ALU.add))
                dve.tensor_scalar(r.bitcast(I32), m.bitcast(I32), -0.5, float(0x5F3759DF), ALU.mult, ALU.add)
                then(dve.tensor_scalar(mh, m, -0.5, None, ALU.mult))
                for _ in range(3):
                    then(dve.tensor_tensor(a, r, r, ALU.mult))
                    then(dve.tensor_tensor(b, a, mh, ALU.mult))
                    then(dve.scalar_tensor_tensor(r, b, 1.5, r, ALU.add, ALU.mult))

            def lift_tile(l, which, tok, kt):
                if kt % 4 == 0:
                    dve.wait_ge(xhi_done, lift_of(l, which) * 16 + tok * 8 + kt + 4)
                sl = slice(tok * P, (tok + 1) * P)
                g = LIFT_GAIN[which] + kt
                dve.scalar_tensor_tensor(
                    xlo[:, kt, sl], T[kt // 4][:, kt % 4 * P : (kt % 4 + 1) * P], small[:, g : g + 1],
                    xhi[:, kt, sl].bitcast(F32), ALU.mult, ALU.subtract,
                ).then_inc(xlo_done, 1)

            def lift_first(l, which):
                if which == 0:
                    dve.wait_ge(small_in_sem, (l + 1) * 16)
                for kt in range(KT):
                    lift_tile(l, which, 0, kt)

            def lift_second(l, which):
                steps.restart()
                dve.wait_ge(squares_done, lift_of(l, which) * 2 + 2)
                order = iter([None] * LIFT_LEAD[which] + list(range(KT)))

                def between():
                    kt = next(order, None)
                    if kt is not None:
                        lift_tile(l, which, 1, kt)

                rsqrt(ss, ms, msh, rs, t0, t1, D, between)
                dve.tensor_scalar(rs_half, rs, 0.5, None, ALU.mult)
                dve.tensor_tensor(rs_sq, rs, rs, ALU.mult).then_inc(rstd_done, 1)
                for kt in order:
                    if kt is not None:
                        lift_tile(l, which, 1, kt)

            def ffn(l, occ):
                o = l * 2 + occ
                at = occ * (FFN_UNITS + MIX_UNITS)
                if occ == 0:
                    lift_first(l, 0)
                    split(l, at, 1)
                    lift_second(l, 0)
                    split(l, at, 2)

                def swiglu(g, tok, chain):
                    dve.wait_ge(tanh_done, g * 2 + tok + 1)
                    chain(dve.scalar_tensor_tensor(h[:, tok, :], tg[:, tok, :], 1.0, G[tok][:, 0:FCH], ALU.add, ALU.mult))
                    dve.scalar_tensor_tensor(
                        h[:, tok, :], h[:, tok, :], rs_sq[:, tok : tok + 1], G[tok][:, FCH : 2 * FCH], ALU.mult, ALU.mult
                    ).then_inc(h_done, 1)

                def turn_h(n, j=0):
                    dve.wait_ge(ht_hi_done, n)
                    dve.tensor_tensor(
                        hTlo[j].rearrange("p k t -> p (k t)"), T[0][:, :],
                        hThi[j].rearrange("p k t -> p (k t)").bitcast(F32), ALU.subtract,
                    ).then_inc(ht_lo_done, 1)

                def x_update(tok):
                    if tok:
                        dve.wait_ge(unit_used, unit_value(l, at + FFN_UNITS - 1))
                    else:
                        dve.wait_ge(acc_done, o + 1)
                    for half in range(2):
                        sl = slice(half * 512, half * 512 + 512)
                        dve.scalar_tensor_tensor(
                            x[:, tok, sl], ACC[tok][half][:, :], 0.25, x[:, tok, sl], ALU.mult, ALU.add
                        ).then_inc(x_up, 1)

                steps.restart()
                dve.wait_ge(rstd_done, lift_of(l, 2 * occ) + 1)
                swiglu(o * FI, 0, steps.then)
                split(l, at, 3)
                swiglu(o * FI, 1, steps.then)
                split(l, at, 4)
                with dve.Fori(1, FI - 1) as i:
                    steps.restart()
                    g = o * FI + i
                    dve.wait_ge(ht_filled, g)
                    swiglu(g, 0, steps.then)
                    turn_h(g)
                    split_in_loop(l, i, at, 2)
                    swiglu(g, 1, steps.then)
                    split_in_loop(l, i, at, 3)
                    split_in_loop(l, i, at, 4)
                last = FI - 1
                steps.restart()
                dve.wait_ge(ht_filled, o * FI + last)
                swiglu(o * FI + last, 0, steps.then)
                turn_h(o * FI + last)
                split(l, at, 3 * last + 2)
                swiglu(o * FI + last, 1, steps.then)
                split(l, at, 3 * last + 3)
                turn_h(o * FI + FI, 1)
                if occ == 0:
                    split(l, FFN_UNITS, 1)
                    x_update(0)
                    lift_first(l, 1)
                    x_update(1)
                    split(l, FFN_UNITS, 2)
                    lift_second(l, 1)
                else:
                    x_update(0)
                    x_update(1)

            def mixer(l):
                at = FFN_UNITS
                then = steps.then

                def index_scores(qt):
                    n = P * (qt + 1)
                    dve.wait_ge(s_drained, l * (NB + 2) + qt + 1)
                    w = work[:, qt, 0:n]
                    for hh in range(4):
                        r = sm[:, hh * n : (hh + 1) * n]
                        iw = z[:, qt, C_IW + hh : C_IW + hh + 1]
                        if hh == 0:
                            then(dve.tensor_scalar(w, r, iw, None, ALU.mult))
                        else:
                            ins = dve.scalar_tensor_tensor(w, r, iw, w, ALU.mult, ALU.add)
                            if hh == 3:
                                ins.then_inc(index_summed, 1)
                                dve.wait_ge(index_summed, l * 2 + qt + 1)
                            else:
                                then(ins)
                    then(dve.tensor_tensor(w, w, const[:, K_CB + S - n : K_CB + S], ALU.add))

                def topk_round():
                    for qt in range(2):
                        ins = dve.max(top8[:, qt, :], work[:, qt, 0 : P * (qt + 1)])
                    then(ins)
                    for qt in range(2):
                        w = work[:, qt, 0 : P * (qt + 1)]
                        ins = dve.match_replace(w, top8[:, qt, :], w, TAKEN)
                    then(ins)

                def selection_bias():
                    for qt in range(2):
                        w = work[:, qt, 0 : P * (qt + 1)]
                        ins = dve.tensor_scalar(w, w, 0.5 * TAKEN, NEG, ALU.is_ge, ALU.mult)
                    then(ins)
                    for qt in range(2):
                        n = P * (qt + 1)
                        w = work[:, qt, 0:n]
                        ins = dve.tensor_tensor(w, w, const[:, K_CB + S - n : K_CB + S], ALU.min)
                    then(ins)

                def mask_and_max(b):
                    kind, qt, _ = BATCHES[b]
                    n, nh = keys_of(b), heads_of(b)
                    w = 16 if kind == "cmp" else n
                    if kind == "cmp":
                        bias = const[:, K_CMPB + 16 * qt : K_CMPB + 16 * qt + n]
                    elif kind == "dsa":
                        bias = work[:, qt, 0:n]
                    else:
                        bias = const[:, K_CB + S - n : K_CB + S]
                    dve.wait_ge(s_filled, l * (NB + 2) + b + 3)
                    if b:
                        dve.wait_ge(exp_done, l * NB + b)
                    dve.memset(unread, 0.0)
                    for hh in range(nh):
                        ins = dve.tensor_tensor_reduce(
                            sm[:, hh * w : hh * w + n], SC[hh % 2][:, (hh // 2) * n : (hh // 2 + 1) * n], bias,
                            1.0, -3.4e38, ALU.add, ALU.max, rowmax[:, hh : hh + 1],
                        )
                    ins.then_inc(s_drained, 1)
                    dve.wait_ge(s_drained, l * (NB + 2) + b + 3)
                    dve.tensor_scalar(negmax[:, 0:nh], rowmax[:, 0:nh], -0.125, None, ALU.mult).then_inc(negmax_done, 1)

                def drain_o(b):
                    kind, qt, g = BATCHES[b]
                    nh = heads_of(b)
                    f = fac[:, 0:nh]
                    dve.wait_ge(exp_done, l * NB + b + 1)
                    then(dve.reciprocal(f, sums[b % 2][:, 0:nh]))
                    if kind != "dsa":
                        j = ("cmp", "sel", "win").index(kind)
                        gate = sig[:, qt, 8 * j + 4 * g : 8 * j + 4 * g + nh]
                        if kind == "cmp":
                            then(dve.scalar_tensor_tensor(
                                f, f, const[:, K_VALID + qt : K_VALID + qt + 1], gate, ALU.mult, ALU.mult))
                        else:
                            then(dve.tensor_tensor(f, f, gate, ALU.mult))
                    dve.wait_ge(o_filled, l * NB + b + 1)
                    src = O[b % 2][:, 0 : nh * HD].rearrange("p (h d) -> p h d", d=HD)
                    fb = f.unsqueeze(2).to_broadcast([P, nh, HD])
                    branch = 0 if kind == "dsa" else 1
                    dst = y[:, qt, branch, 256 * g : 256 * g + nh * HD].rearrange("p (h d) -> p h d", d=HD)
                    if kind in ("dsa", "sel"):
                        dve.tensor_tensor(dst, src, fb, ALU.mult).then_inc(o_drained, 1)
                    else:
                        tmp = oacc[:, 0 : nh * HD].rearrange("p (h d) -> p h d", d=HD)
                        dve.tensor_tensor(tmp, src, fb, ALU.mult).then_inc(o_drained, 1)
                        dve.wait_ge(o_drained, l * NB + b + 1)
                        ins = dve.tensor_tensor(dst, dst, tmp, ALU.add)
                        if kind == "cmp":
                            ins.then_inc(y_done, 1)
                        else:
                            then(ins)

                def split_y(name, n_hi, dst_hi, dst_lo, ks):
                    tok = int(name[-1]) if name[:2] in ("yc", "ya") else MERGED_ORDER[int(name[-1])][0]
                    dve.wait_ge(t_hi_done, l * 10 + n_hi)
                    sl = slice(tok * P, (tok + 1) * P)
                    mark_drained(dve.tensor_tensor(
                        dst_lo[:, ks : ks + 4, sl], turn_bank(name)[:, :].rearrange("p (k t) -> p k t", k=4),
                        dst_hi[:, ks : ks + 4, sl].bitcast(F32), ALU.subtract), name)

                def gated(b_, branch, half, tok):
                    f = 24 + 4 * b_ + 2 * half + tok
                    wait_g(dve, l, f)
                    if b_ == 0 and half == 0:
                        dve.wait_ge(gz_drained, l * 24 + 24)
                    own = gates[:, tok, branch * D + half * 512 : branch * D + half * 512 + 512]
                    total = gates[:, tok, D + half * 512 : D + half * 512 + 512]
                    dve.scalar_tensor_tensor(own, own, 1.0, G[tok][:, :], ALU.add, ALU.mult).then_inc(gp_drained, 1)
                    dve.wait_ge(gp_drained, l * 12 + f - 24 + 1)
                    if b_:
                        ins = dve.tensor_tensor(total, total, own, ALU.add)
                        if b_ == 2:
                            ins.then_inc(merged_done, 1)
                        else:
                            then(ins)

                dve.wait_ge(gate_tanh, l + 1)
                then(dve.tensor_scalar(sig[:, :, :], sig[:, :, :], 0.5, 0.5, ALU.mult, ALU.add))
                dve.wait_ge(kv_squares, l * 2 + 2)
                rsqrt(sskv, kms, kmsh, rkv, kt0, kt1, P)
                split(l, at, 3)
                split(l, at, 4)
                split(l, at, 5)
                dve.wait_ge(t_filled, filled(l, "kv"))
                for tok in range(TOKS):
                    ins = dve.tensor_scalar(
                        zkv[:, tok, :], turn_bank("kv")[:, tok * P : (tok + 1) * P], rkv[:, tok : tok + 1], None, ALU.mult
                    )
                mark_drained(ins, "kv")
                split(l, at, 6)
                split(l, at, 7)
                dve.wait_ge(const_in_sem, 16)
                index_scores(0)
                split(l, at, 8)
                index_scores(1)
                split(l, at, 9)
                split(l, at, 10)
                dve.wait_ge(t_filled, filled(l, "hid"))
                mark_drained(dve.tensor_copy(hid_v, turn_bank("hid")[0:ROWS, 0:256]), "hid")
                wait_drained(dve, l, "hid")
                then(dve.tensor_tensor(hid_t, hid_v, hid_v, ALU.mult))
                then(dve.tensor_scalar(hid_t, hid_t, 0.044715, 1.0, ALU.mult, ALU.add))
                dve.tensor_tensor(hid_t, hid_t, hid_v, ALU.mult).then_inc(gelu_inner, 1)
                split(l, at, 11)
                dve.wait_ge(gelu_tanh, l + 1)
                dve.scalar_tensor_tensor(hid_t, hid_t, 1.0, hid_v, ALU.add, ALU.mult).then_inc(gelu_done, 1)
                mask_and_max(0)
                split(l, at, 12)
                mask_and_max(1)
                split(l, at, 13)
                for k in range(12):
                    c, tok = Z_CHUNKS + k // 2, k % 2
                    if tok:
                        split(l, at, 2 * c + 2)
                    drain_o(k)
                    if k == 8:
                        selection_bias()
                    if k + LEAD < NB:
                        mask_and_max(k + LEAD)
                    if k < 8:
                        topk_round()
                    if 2 <= k < 4:
                        name = f"yb{k - 2}"
                        dve.wait_ge(t_hi_done, l * 10 + k - 1)
                        for g in range(2):
                            gg = 2 * (k - 2) + g
                            ins = dve.scalar_tensor_tensor(
                                yblo[:, gg, :], turn_bank(name)[:, g * S : (g + 1) * S],
                                small[:, W_PSC + gg : W_PSC + gg + 1], ybhi[:, gg, :].bitcast(F32),
                                ALU.mult, ALU.subtract)
                        mark_drained(ins, name)
                    if tok:
                        split(l, at, 2 * c + 3)
                for j in range(2):
                    split_y(f"yc{j}", 3 + j, xhi, xlo, 0)
                gated(0, 1, 0, 0)
                gated(0, 1, 0, 1)
                split(l, at, 26)
                drain_o(12)
                gated(0, 1, 1, 0)
                gated(0, 1, 1, 1)
                split(l, at, 27)
                drain_o(13)
                gated(1, 2, 0, 0)
                gated(1, 2, 0, 1)
                split(l, at, 28)
                for j in range(2):
                    split_y(f"ya{j}", 5 + j, xhi, xlo, 4)
                gated(1, 2, 1, 0)
                gated(1, 2, 1, 1)
                split(l, at, 29)

                def split_mg(j):
                    split_y(f"mg{j}", 7 + j, xhi, xlo, 4 * MERGED_ORDER[j][1])

                gated(2, 0, 0, 0)
                gated(2, 0, 0, 1)
                split(l, at, 30)
                gated(2, 0, 1, 0)
                split_mg(0)
                split_mg(1)
                gated(2, 0, 1, 1)
                split_mg(2)
                split(l, at, 31)
                split_mg(3)

                def x_update(half, tok):
                    sl = slice(half * 512, half * 512 + 512)
                    wait_g(dve, l, 36 + 2 * half + tok)
                    dve.scalar_tensor_tensor(
                        x[:, tok, sl], G[tok][:, :], 0.5, x[:, tok, sl], ALU.mult, ALU.add
                    ).then_inc(x_up, 1)

                x_update(0, 0)
                split(l, at, 32)
                x_update(0, 1)
                split(l, at, 33)
                x_update(1, 0)
                lift_first(l, 2)
                split(l, at, 34)
                x_update(1, 1)
                lift_second(l, 2)
                split(l, at, 35)

            dve.nop().then_inc(lo_done, CREDIT * PARTS)
            dve.nop().then_inc(merged_done, 1)
            for part in range(PARTS):
                dve.wait_ge(hi_done, part_value(0, part))
                subtract_hi(0, part)
            with dve.Fori(0, L) as l:
                steps.restart()
                ffn(l, 0)
                mixer(l)
                ffn(l, 1)
            dve.wait_ge(squares_done, 6 * L + 2)
            rsqrt(ss, ms, msh, rs, t0, t1, D)
            dve.wait_ge(final_in_sem, 16)
            for tok in range(TOKS):
                for half in range(2):
                    sl = slice(half * 512, half * 512 + 512)
                    dve.scalar_tensor_tensor(
                        x[:, tok, sl], x[:, tok, sl], rs[:, tok : tok + 1], gain[:, sl], ALU.mult, ALU.mult
                    ).then_inc(out_ready, 1)

        @block.tensor
        def _(pe):
            def mm3(o, ahi, alo, bhi, blo, first, last):
                pe.matmul(o, ahi, bhi, start=first, stop=False)
                pe.matmul(o, ahi, blo, start=False, stop=False)
                return pe.matmul(o, alo, bhi, start=False, stop=last)

            def wait_part(l, n, part):
                pe.wait_ge(lo_done, part_value(n, part, l * LAYER_UNITS))

            def lift(l, which, tok, half):
                v, j = lift_of(l, which), 2 * tok + half
                pe.wait_ge(x_up, v * 4 + LIFT_NEEDS[which][j])
                if tok:
                    pe.wait_ge(xlo_done, v * 16 + 4 * (j - 1))
                for k in range(4):
                    c = half * 512 + k * P
                    ins = pe.transpose(T[half][:, k * P : (k + 1) * P], x[:, tok, c : c + P], ident)
                ins.then_inc(xt_filled, 1)

            def wait_lifted(l, which, tok, kt):
                pe.wait_ge(xlo_done, lift_of(l, which) * 16 + tok * 8 + kt + 1)

            def gemm_half(o, tok, hi, lo, k0, s, n, first, last, unit=None, before=None):
                for k in range(4):
                    if unit and k % 2 == 0:
                        unit(k // 2)
                    if before:
                        before(k0 + k)
                    sl = slice(tok * P, (tok + 1) * P)
                    ins = mm3(
                        o[:, 0:n], hi[:, k0 + k, sl], lo[:, k0 + k, sl], whi[s][:, k * n : (k + 1) * n],
                        wlo[s][:, k * n : (k + 1) * n], first and k == 0, last and k == 3,
                    )
                return ins

            def ffn(l, occ):
                o = l * 2 + occ
                at = occ * (FFN_UNITS + MIX_UNITS)
                which = 2 * occ
                if occ == 0:
                    lift(l, 0, 0, 0)
                    lift(l, 0, 0, 1)

                def gate_up(i, tok, peeled=False):
                    slot = at if peeled else at - 1
                    base = l * LAYER_UNITS + (0 if peeled else i * RING)
                    if not peeled:
                        pe.wait_ge(h_done, (o * FI + i) * 2 + tok - 1)
                    for a in range(2):
                        if peeled and tok == 0 and a:
                            lift(l, which, 1, 0)
                            lift(l, which, 1, 1)

                        def unit(part):
                            pe.wait_ge(lo_done, part_value(slot + a, part, base))

                        def lifted(kt):
                            wait_lifted(l, which, tok, kt)

                        ins = gemm_half(
                            G[tok], tok, xhi, xlo, 4 * a, (slot + a) % RING, 512, a == 0, a == 1,
                            unit=None if tok else unit, before=lifted if peeled else None)
                        if tok and a == 0:
                            ins.then_inc(unit_used, 1)
                    ins.then_inc(unit_used if tok else gu_filled, 1)

                def turn_h(n):
                    pe.wait_ge(h_done, n * 2)
                    for k in range(2):
                        for tok in range(TOKS):
                            ins = pe.transpose(
                                T[0][:, k * S + tok * P : k * S + (tok + 1) * P], h[:, tok, k * P : (k + 1) * P], ident)
                    ins.then_inc(ht_filled, 1)

                def down(n, base, u, first=False, between=None, turn=None):
                    s, j = u % RING, 1 if between else 0
                    pe.wait_ge(ht_lo_done, n)
                    for tok in range(TOKS):
                        sl = slice(tok * P, (tok + 1) * P)
                        for half in range(2):
                            if between:
                                between(tok, half)
                            if turn is not None and tok and half == 0:
                                turn_h(turn)
                            for k in range(2):
                                if tok == 0 and half == 0:
                                    pe.wait_ge(lo_done, part_value(u, k, base))
                                c = k * D + half * 512
                                ins = mm3(
                                    ACC[tok][half][:, :], hThi[j][:, k, sl], hTlo[j][:, k, sl], whi[s][:, c : c + 512],
                                    wlo[s][:, c : c + 512], first and k == 0, between is not None and k == 1,
                                )
                        if tok:
                            ins.then_inc(unit_used, 1)
                        elif between:
                            ins.then_inc(acc_done, 1)

                def lift_between(tok, half):
                    if occ == 0 and tok and half:
                        lift(l, 1, 0, 0)
                        lift(l, 1, 0, 1)

                gate_up(0, 0, peeled=True)
                gate_up(0, 1, peeled=True)
                gate_up(1, 0)
                turn_h(o * FI + 1)
                gate_up(1, 1)
                down(o * FI + 1, l * LAYER_UNITS, at + 4, first=True)
                with pe.Fori(2, FI - 1) as i:
                    gate_up(i, 0)
                    turn_h(o * FI + i)
                    gate_up(i, 1)
                    down(o * FI + i, l * LAYER_UNITS + i * RING, at + 1)
                last = FI - 1
                gate_up(last, 0)
                turn_h(o * FI + last)
                gate_up(last, 1)
                down(o * FI + last, l * LAYER_UNITS, at + 3 * last + 1, turn=o * FI + FI)
                down(o * FI + FI, l * LAYER_UNITS, at + 3 * last + 2, between=lift_between)

            def mixer(l):
                at = FFN_UNITS

                def chunk(c, tok):
                    f = OPENING.index((c, tok)) if c < 2 else 2 * c + tok
                    if f >= 2:
                        pe.wait_ge(gz_drained, l * 24 + f - 1)
                    if c == 0:
                        if tok == 0:
                            wait_part(l, at, PARTS - 1)
                        s, n = at % RING, C_S
                        for kt in range(KT):
                            wait_lifted(l, 1, tok, kt)
                            sl = slice(tok * P, (tok + 1) * P)
                            w = slice(kt * n, (kt + 1) * n)
                            ins = mm3(
                                G[f % 2][:, 0:n], xhi[:, kt, sl], xlo[:, kt, sl], whi[s][:, w], wlo[s][:, w],
                                kt == 0, kt == KT - 1)
                    else:
                        for a in range(2):
                            u = 2 * c - 1 + a
                            ins = unit_gemm(f % 2, u, xhi, xlo, 4 * a, tok, a == 0, a == 1)
                            if tok and a == 0:
                                ins.then_inc(unit_used, 1)
                    ins.then_inc(unit_used if tok else g_filled, 1)

                def unit_gemm(g, u, hi, lo, k0, tok, first, last):
                    def unit(part):
                        wait_part(l, at + u, part)

                    return gemm_half(
                        G[g], tok, hi, lo, k0, (at + u) % RING, 512, first, last, unit=None if tok else unit)

                def open_turn(name, *needs):
                    wait_drained(pe, l, *needs, opening=name)
                    return turn_bank(name)

                def turn(name, tiles, rows=P):
                    t = open_turn(name)
                    for n, src in enumerate(tiles):
                        ins = pe.transpose(t[0:rows, n * P : (n + 1) * P], src, ident)
                    ins.then_inc(t_filled, 1)

                def scores(si, qT, kT_, pairs, qt, n):
                    if si:
                        pe.wait_ge(s_drained, l * (NB + 2) + si)
                    for j, pr in enumerate(pairs):
                        for half in range(2):
                            rows = slice(half * HD, (half + 1) * HD)
                            ins = pe.matmul(
                                SC[half][:, j * n : (j + 1) * n], qT[rows, pr, qt * P : (qt + 1) * P], kT_[rows, 0:n],
                                start=True, stop=True)
                    ins.then_inc(s_filled, 1)

                def batch_scores(b):
                    kind, qt, g = BATCHES[b]
                    if b == 0:
                        wait_drained(pe, l, "qn0", "qn1", "ksw")
                    if kind == "cmp" and qt == 0:
                        wait_drained(pe, l, "cmpo")
                    if kind == "dsa" and qt == 0 and g == 0:
                        wait_drained(pe, l, "qd0", "qd1", "kd")
                    qT = qdT if kind == "dsa" else qnT
                    keys = {"sel": kswT[:, 0, :], "win": kswT[:, 1, :], "cmp": kcT, "dsa": kdT}[kind]
                    pairs = range(4) if kind == "cmp" else range(2 * g, 2 * g + 2)
                    scores(b + 2, qT, keys, pairs, qt, keys_of(b))

                def batch_turn(b):
                    n = keys_of(b)
                    w = 16 if n == N_CMP else n
                    bw = min(n, P)
                    pe.wait_ge(exp_done, l * NB + b + 1)
                    for j, name in enumerate(turn_names(b)):
                        turn(
                            name, [probs[:, hh * w + kb * P : hh * w + kb * P + bw] for hh, kb in turns_of(b)[j]],
                            rows=bw)

                def batch_values(b):
                    kind, qt, g = BATCHES[b]
                    if b >= 2:
                        pe.wait_ge(o_drained, l * NB + b - 1)
                    wait_drained(pe, l, *turn_names(b))
                    for j, name in enumerate(turn_names(b)):
                        for n, (hh, kb) in enumerate(turns_of(b)[j]):
                            grp = hh % 2
                            if kind == "cmp":
                                lhs, rhs, last = pT[0:N_CMP, 4 * j + n, :], vc[0:N_CMP, grp, :], True
                            else:
                                v = {
                                    "sel": z[:, kb, C_KVS + 128 + HD * grp : C_KVS + 128 + HD * (grp + 1)],
                                    "win": z[:, kb, C_KVW + 128 + HD * grp : C_KVW + 128 + HD * (grp + 1)],
                                    "dsa": zkv[:, kb, HD:P],
                                }[kind]
                                lhs, rhs, last = pT[:, 4 * j + n, :], v, kb == qt
                            ins = pe.matmul(O[b % 2][:, hh * HD : (hh + 1) * HD], lhs, rhs, start=kb == 0, stop=last)
                    ins.then_inc(o_filled, 1)

                def wait_roped(n):
                    pe.wait_ge(roped, l * 8 + n)

                def pairs_of(col, n):
                    return [z[:, tok, col + P * pr : col + P * (pr + 1)] for pr in n for tok in range(TOKS)]

                chunk(0, 0)
                lift(l, 1, 1, 0)
                lift(l, 1, 1, 1)
                chunk(1, 0)
                chunk(0, 1)
                chunk(1, 1)
                pe.wait_ge(gz_drained, l * 24 + 3)
                turn("ckv", [z[:, tok, C_CKV : C_CKV + P] for tok in range(TOKS)])
                chunk(2, 0)
                t = open_turn("kv", "ckv")
                for tok in range(TOKS):
                    ins = pe.matmul(
                        t[:, tok * P : (tok + 1) * P], ckvT[:, tok * P : (tok + 1) * P], small[:, W_UKV : W_UKV + P],
                        start=True, stop=True)
                ins.then_inc(t_filled, 1)
                wait_roped(2)
                turn("ik", [ikd[:, tok, :, :].rearrange("p a d -> p (a d)") for tok in range(TOKS)])
                chunk(2, 1)
                turn("iq", pairs_of(C_IQ, range(2)))
                chunk(3, 0)
                wait_roped(4)
                turn("kd", [kd[:, tok, :, :].rearrange("p a d -> p (a d)") for tok in range(TOKS)])
                turn("kvc", pairs_of(C_KVC, range(2)))
                wait_drained(pe, l, "ik", "iq")
                scores(0, iqT, ikT, range(2), 0, P)
                chunk(3, 1)
                wait_roped(6)
                turn("ksw", pairs_of(C_KVS, [0]) + pairs_of(C_KVW, [0]))
                scores(1, iqT, ikT, range(2), 1, S)
                chunk(4, 0)
                wait_roped(7)
                turn("qn0", pairs_of(C_QN, [0, 1]))
                turn("qn1", pairs_of(C_QN, [2, 3]))
                chunk(4, 1)
                t = open_turn("hid")
                pe.wait_ge(windows_done, l + 1)
                pe.wait_ge(w1_in_sem, l * 16 + 16)
                for y_ in range(2):
                    for k in range(16):
                        ins = pe.matmul(
                            t[0:ROWS, P * y_ : P * (y_ + 1)], windows[:, y_, k, :, :].rearrange("p g n -> p (g n)"),
                            w1[:, y_, k, :], start=k == 0, stop=k == 15)
                ins.then_inc(t_filled, 1)
                chunk(5, 0)
                wait_roped(8)
                turn("qd0", pairs_of(C_QD, [0, 1]))
                turn("qd1", pairs_of(C_QD, [2, 3]))
                batch_scores(0)
                t = open_turn("gelt")
                pe.wait_ge(gelu_done, l + 1)
                for y_ in range(2):
                    ins = pe.matmul(
                        t[:, ROWS * y_ : ROWS * (y_ + 1)], hid_t[:, P * y_ : P * (y_ + 1)], ident[0:ROWS, 0:ROWS],
                        start=True, stop=True)
                ins.then_inc(t_filled, 1)
                chunk(5, 1)
                t = open_turn("cmpo", "gelt")
                for g in range(2):
                    pe.matmul(
                        t[g * HD : (g + 1) * HD, 0:N_CMP], small[:, W_W2 : W_W2 + HD],
                        gelT[:, 0, g * N_CMP : (g + 1) * N_CMP], start=True, stop=True)
                for g in range(2):
                    ins = pe.matmul(
                        t[0:N_CMP, 64 + g * HD : 64 + (g + 1) * HD], gelT[:, 1, g * N_CMP : (g + 1) * N_CMP],
                        small[:, W_W2 + HD : W_W2 + 2 * HD], start=True, stop=True)
                ins.then_inc(t_filled, 1)
                batch_turn(0)
                batch_scores(1)
                for k in range(12):
                    c, tok = Z_CHUNKS + k // 2, k % 2
                    chunk(c, tok)
                    batch_values(k)
                    batch_turn(k + 1)
                    if k + LEAD < NB:
                        batch_scores(k + LEAD)
                    if k < 2:
                        pe.wait_ge(const_in_sem, 16)
                        pe.wait_ge(gz_drained, l * 24 + 12)
                        t = open_turn(f"band{k}")
                        for g in range(2):
                            gg = 2 * k + g
                            u = [z[:, tk, C_U + gg * P : C_U + (gg + 1) * P] for tk in range(TOKS)]
                            band = const[:, K_BAND + gg * BANDC : K_BAND + (gg + 1) * BANDC]
                            pe.matmul(t[:, g * S : g * S + BAND0], u[0], band[:, 0:BAND0], start=g == 0, stop=False,
                                      skip_group_check=True)
                            ins = pe.matmul(t[:, g * S + P : (g + 1) * S], u[1], band[:, BAND0:BANDC], start=False,
                                            stop=True, skip_group_check=True)
                        ins.then_inc(t_filled, 1)
                    elif k < 4:
                        t = open_turn(f"yb{k - 2}", f"band{k - 2}")
                        for g in range(2):
                            gg = 2 * (k - 2) + g
                            ins = pe.matmul(
                                t[:, g * S : (g + 1) * S], small[:, W_POOL + gg * P : W_POOL + (gg + 1) * P],
                                pooledT[:, gg, :], start=True, stop=True)
                        ins.then_inc(t_filled, 1)

                def y_tiles(branch, tok):
                    return [y[:, tok, branch, k * P : (k + 1) * P] for k in range(4)]

                def project(b_, half, hi, lo, k0, toks=range(TOKS)):
                    for tok in toks:
                        f = 24 + 4 * b_ + 2 * half + tok
                        if f < 26:
                            pe.wait_ge(gz_drained, l * 24 + f - 1)
                        else:
                            pe.wait_ge(gp_drained, l * 12 + f - 25)
                        ins = unit_gemm(tok, 23 + 2 * b_ + half, hi, lo, k0, tok, True, True)
                        ins.then_inc(unit_used if tok else g_filled, 1)

                pe.wait_ge(y_done, l * 2 + 2)
                turn("yc0", y_tiles(1, 0))
                turn("yc1", y_tiles(1, 1))
                wait_drained(pe, l, "yb0", "yb1")
                project(0, 0, ybhi, yblo, 0)
                batch_values(12)
                batch_turn(13)
                project(0, 1, ybhi, yblo, 0)
                batch_values(13)
                wait_drained(pe, l, "yc0", "yc1")
                project(1, 0, xhi, xlo, 0)
                pe.wait_ge(o_drained, l * NB + NB)
                turn("ya0", y_tiles(0, 0))
                turn("ya1", y_tiles(0, 1))
                project(1, 1, xhi, xlo, 0)
                wait_drained(pe, l, "ya0", "ya1")
                project(2, 0, xhi, xlo, 4)

                def turn_mg(j):
                    tok, half = MERGED_ORDER[j]
                    pe.wait_ge(merged_done, l * 4 + j + 2)
                    turn(f"mg{j}", [gates[:, tok, D + half * 512 + k * P : D + half * 512 + (k + 1) * P] for k in range(4)])

                project(2, 1, xhi, xlo, 4, toks=[0])
                turn_mg(0)
                turn_mg(1)
                project(2, 1, xhi, xlo, 4, toks=[1])
                turn_mg(2)
                for n in range(2):
                    for tok in range(TOKS):
                        f = 36 + 2 * n + tok
                        if n == 0:
                            pe.wait_ge(gp_drained, l * 12 + f - 25)
                        else:
                            pe.wait_ge(x_up, lift_of(l, 2) * 4 + f - 37)
                        for a in range(2):
                            u = 29 + 2 * n + a
                            if n and tok:
                                lift(l, 2, 0, a)
                            wait_drained(pe, l, f"mg{MERGED_ORDER.index((tok, a))}")
                            ins = unit_gemm(tok, u, xhi, xlo, 4 * a, tok, a == 0, a == 1)
                            if tok and a == 0:
                                ins.then_inc(unit_used, 1)
                            if n == 0 and tok == 0 and a == 0:
                                turn_mg(3)
                        ins.then_inc(unit_used if tok else g_filled, 1)

            pe.nop().then_inc(unit_used, CREDIT)
            pe.wait_ge(first_const_in_sem, 16)
            for _ in range(WARM_UP):
                pe.transpose(SC[0][:, 0:P], ident, ident)
            with pe.Fori(0, L) as l:
                ffn(l, 0)
                mixer(l)
                ffn(l, 1)


IN_SPLITS = (512, 128, 256, 64, 4, 512, 512, 256, 256, 256, 24, 3072)
PAIRED = [0, 4, 1, 5, 2, 6, 3, 7]


def _tiles(w):
    k, n = w.shape
    return w.reshape(k // P, P, n).transpose(1, 0, 2).reshape(P, -1)


def _ffn_units(gate, up, down):
    units = []

    def gu(i):
        c = slice(i * FCH, (i + 1) * FCH)
        w = np.concatenate([gate[:, c], up[:, c]], axis=1)
        units.extend([_tiles(w[:512]), _tiles(w[512:])])

    def dn(i):
        units.append(_tiles(down[i * FCH : (i + 1) * FCH]))

    gu(0)
    for i in range(1, FI):
        gu(i)
        dn(i - 1)
    dn(FI - 1)
    return units


def _mix_units(w_in, pa, pb, pc, w_out):
    offs = np.cumsum((0,) + IN_SPLITS)
    q, ckv, iq, ik, iw, u, cq, kvc, kvs, kvw, gate, merge = (
        w_in[:, offs[i] : offs[i + 1]] for i in range(len(IN_SPLITS)))
    cq = cq.reshape(D, 8, HD)[:, PAIRED].reshape(D, 512)
    gate = gate.reshape(D, 8, 3)[:, PAIRED].transpose(0, 2, 1).reshape(D, 24)
    pc = pc.reshape(8, HD, D)[PAIRED].reshape(512, D)
    cols = np.concatenate([ckv, ik, iw, gate, iq, kvc, kvs, kvw, cq, q, u, merge], axis=1)
    first = np.zeros((P, UNIT), np.float32)
    first[:, : KT * C_S] = _tiles(cols[:, :C_S])
    units = [first]
    for c in range(CHUNKS - 1):
        w = cols[:, C_S + c * 512 : C_S + (c + 1) * 512]
        units += [_tiles(w[:512]), _tiles(w[512:])]
    for w in (pb, pc, pa):
        units += [_tiles(w[:, :512]), _tiles(w[:, 512:])]
    for n in range(2):
        w = w_out[:, n * 512 : (n + 1) * 512]
        units += [_tiles(w[:512]), _tiles(w[512:])]
    return units


def _constants():
    c = np.zeros((P, KC), np.float32)
    r = np.arange(P)
    c[:, K_ID : K_ID + P] = np.eye(P)
    c[:, K_CB + P : K_CB + 2 * P] = np.where(r[None, :] <= r[:, None], 0.0, NEG)
    ends = np.arange(N_CMP) * 16 + 31
    for qt in range(2):
        t = qt * P + r
        ok = ends[None, :] <= t[:, None]
        c[:, K_CMPB + 16 * qt : K_CMPB + 16 * qt + N_CMP] = np.where(ok, 0.0, NEG)
        c[:, K_VALID + qt] = ok.any(axis=1)
    for g, w in enumerate(WINDOWS):
        s, t = np.arange(S)[:, None], np.arange(S)[None, :]
        band = ((s <= t) & (s > t - w)) / np.minimum(t + 1, w) - (s == t)
        o = K_BAND + g * BANDC
        c[:, o : o + BAND0] = band[:P, :BAND0]
        c[:, o + BAND0 : o + BANDC] = band[P:, P:]
    exps = -np.arange(0, 2 * HALF_ROT, 2, dtype=np.float32) / np.float32(2 * HALF_ROT)
    c[:, K_FREQ : K_FREQ + HALF_ROT] = np.float64(THETA) ** exps.astype(np.float64)
    return c


def kernel(x, positions, ffn1_norm, ffn1_gate, ffn1_up, ffn1_down, mix_norm, w_in,
           dsa_kv_norm, dsa_w_ukv, pool_w, pool_scale, nsa_cmp_pos, nsa_cmp_w1, nsa_cmp_w2,
           proj_a, proj_b, proj_c, w_out, ffn2_norm, ffn2_gate, ffn2_up, ffn2_down, final_norm):
    import concourse.bacc as _bacc
    from concourse.bass_utils import run_bass_kernel_spmd as _run

    a = [np.asarray(v) for v in (
        x, positions, ffn1_norm, ffn1_gate, ffn1_up, ffn1_down, mix_norm, w_in, dsa_kv_norm, dsa_w_ukv, pool_w,
        pool_scale, nsa_cmp_pos, nsa_cmp_w1, nsa_cmp_w2, proj_a, proj_b, proj_c, w_out, ffn2_norm, ffn2_gate,
        ffn2_up, ffn2_down, final_norm)]
    (x, positions, ffn1_norm, ffn1_gate, ffn1_up, ffn1_down, mix_norm, w_in, dsa_kv_norm, dsa_w_ukv, pool_w,
     pool_scale, nsa_cmp_pos, nsa_cmp_w1, nsa_cmp_w2, proj_a, proj_b, proj_c, w_out, ffn2_norm, ffn2_gate,
     ffn2_up, ffn2_down, final_norm) = a
    units = []
    small = np.zeros((L + 1, P, W_SMALL), np.float32)
    w1 = np.zeros((L, P, W1C), np.float32)
    for l in range(L):
        units += _ffn_units(ffn1_gate[l], ffn1_up[l], ffn1_down[l])
        units += _mix_units(w_in[l], proj_a[l], proj_b[l], proj_c[l], w_out[l])
        units += _ffn_units(ffn2_gate[l], ffn2_up[l], ffn2_down[l])
        s = small[l]
        s[:, W_G1 : W_G1 + 8] = ffn1_norm[l].reshape(8, P).T
        s[:, W_GM : W_GM + 8] = mix_norm[l].reshape(8, P).T
        s[:, W_G2 : W_G2 + 8] = ffn2_norm[l].reshape(8, P).T
        s[:, W_KVG] = dsa_kv_norm[l]
        s[:, W_PSC : W_PSC + 4] = pool_scale[l].reshape(4, P).T
        s[:, W_POS : W_POS + 32] = nsa_cmp_pos[l].reshape(2, 16, P).transpose(2, 0, 1).reshape(P, 32)
        s[:, W_UKV : W_UKV + P] = dsa_w_ukv[l]
        s[:, W_POOL : W_POOL + 512] = pool_w[l].transpose(1, 0, 2).reshape(P, 512)
        s[:, W_W2 : W_W2 + P] = nsa_cmp_w2[l].transpose(1, 0, 2).reshape(P, P)
        w1[l] = nsa_cmp_w1[l].reshape(2, 16, P, P).transpose(2, 0, 1, 3).reshape(P, W1C)
    units += [np.zeros((P, UNIT), np.float32)] * PAD_UNITS
    arrays = {
        "x_in": x.reshape(S, D), "pos_in": positions.reshape(TOKS, P).T, "stream": np.stack(units), "small_in": small,
        "w1_in": w1, "const_in": _constants(), "final_in": final_norm,
    }
    nc = _bacc.Bacc("TRN2", target_bir_lowering=False, num_devices=1)
    args = []
    for name, v in arrays.items():
        arrays[name] = v = np.ascontiguousarray(v)
        args.append(nc.dram_tensor(name, v.shape, mybir.dt.from_np(v.dtype), kind="ExternalInput").ap())
    args.append(nc.dram_tensor("out", (S, D), F32, kind="ExternalOutput").ap())
    trunk(nc, *args)
    r = _run(nc, [arrays], core_ids=[0])
    return r.results[0]["out"].reshape(1, S, D)
```
